# Optimizing a Trainium2 kernel written in Bass

```python
import jax, jax.numpy as jnp
from jax import lax
import numpy as np
import math

D_MODEL = 1024
BATCH = 1
SEQ = 1024
DEPTH = 1

D_MIX = D_MODEL
D_POOL = D_MIX // 2
D_LRU = D_MIX - D_POOL
POOL_WINDOWS = (2, 4, 8, 16)
N_POOL_GROUPS = len(POOL_WINDOWS)
POOL_GROUP_WIDTH = D_POOL // N_POOL_GROUPS
LRU_HEADS = 8
LRU_BLOCK = D_LRU // LRU_HEADS
CONV_WIDTH = 4
LRU_C = 8.0
D_FF = 4 * D_MODEL
PLE_DIM = 256
RMS_EPS = 1e-6
D_IN_PROJ = D_POOL + D_LRU + D_LRU


def rms_norm(x, g):
    xf = x.astype(jnp.float32)
    y = xf * lax.rsqrt(jnp.mean(xf * xf, axis=-1, keepdims=True) + RMS_EPS)
    return (y * g.astype(jnp.float32)).astype(x.dtype)

def multiscale_pool_mixer(u, pool_w, pool_b, pool_scale):
    B, S, _ = u.shape
    ug = u.reshape(B, S, N_POOL_GROUPS, POOL_GROUP_WIDTH).astype(jnp.float32)
    csum = jnp.cumsum(ug, axis=1)
    t = jnp.arange(S)
    outs = []
    for g, w in enumerate(POOL_WINDOWS):
        c = csum[:, :, g]
        c_lag = jnp.pad(c, ((0, 0), (w, 0), (0, 0)))[:, :S]
        count = jnp.minimum(t + 1, w).astype(jnp.float32)
        outs.append((c - c_lag) / count[None, :, None] - ug[:, :, g])
    d = jnp.stack(outs, axis=2).astype(u.dtype)
    y = jnp.einsum('bsgc,gcd->bsgd', d, pool_w) + pool_b
    return y.reshape(B, S, D_POOL) * pool_scale

def causal_depthwise_conv(u, w, b):
    S = u.shape[1]
    upad = jnp.pad(u, ((0, 0), (CONV_WIDTH - 1, 0), (0, 0)))
    y = b
    for k in range(CONV_WIDTH):
        y = y + upad[:, k:k + S] * w[k]
    return y

def _linear_recurrence_combine(c1, c2):
    a1, b1 = c1
    a2, b2 = c2
    return a1 * a2, a2 * b1 + b2

def rg_lru(u, gate_a_w, gate_a_b, gate_x_w, gate_x_b, lru_L):
    B, S, W = u.shape
    uh = u.reshape(B, S, LRU_HEADS, LRU_BLOCK)
    r = jax.nn.sigmoid(jnp.einsum('bshi,hij->bshj', uh, gate_a_w) + gate_a_b).reshape(B, S, W)
    i = jax.nn.sigmoid(jnp.einsum('bshi,hij->bshj', uh, gate_x_w) + gate_x_b).reshape(B, S, W)
    log_a = LRU_C * r.astype(jnp.float32) * jax.nn.log_sigmoid(lru_L.astype(jnp.float32))
    a = jnp.exp(log_a)
    mult = jnp.sqrt(-jnp.expm1(2.0 * log_a))
    is_first = (jnp.arange(S) == 0)[None, :, None]
    mult = jnp.where(is_first, 1.0, mult)
    b = mult * (i * u).astype(jnp.float32)
    _, h = lax.associative_scan(_linear_recurrence_combine, (a, b), axis=1)
    return h.astype(u.dtype)

def first_inputs(seed: int = 0) -> dict:
    key = jax.random.key(seed)
    ks = jax.random.split(key, 24)
    f32 = jnp.float32
    nrm = lambda k, shape, scale: jax.random.normal(k, shape, f32) * scale
    gain = lambda k, shape: 1.0 + 0.05 * jax.random.normal(k, shape, f32)
    L = DEPTH
    rad = jnp.sqrt(jax.random.uniform(ks[12], (L, D_LRU), f32, 0.9 ** 2, 0.999 ** 2))
    lru_L = jnp.log(rad) - jnp.log1p(-rad)
    return {
        "x": jax.random.normal(ks[0], (BATCH, SEQ, D_MODEL), f32),
        "p": jax.random.normal(ks[1], (DEPTH, BATCH, SEQ, PLE_DIM), f32),
        "norm_mix_g": gain(ks[2], (L, D_MODEL)),
        "w_in": nrm(ks[3], (L, D_MODEL, D_IN_PROJ), D_MODEL ** -0.5),
        "pool_w": nrm(ks[4], (L, N_POOL_GROUPS, POOL_GROUP_WIDTH, POOL_GROUP_WIDTH), POOL_GROUP_WIDTH ** -0.5),
        "pool_b": nrm(ks[5], (L, N_POOL_GROUPS, POOL_GROUP_WIDTH), 0.01),
        "pool_scale": gain(ks[6], (L, D_POOL)),
        "conv_w": nrm(ks[7], (L, CONV_WIDTH, D_LRU), CONV_WIDTH ** -0.5),
        "conv_b": nrm(ks[8], (L, D_LRU), 0.01),
        "gate_a_w": nrm(ks[9], (L, LRU_HEADS, LRU_BLOCK, LRU_BLOCK), LRU_BLOCK ** -0.5),
        "gate_a_b": nrm(ks[10], (L, LRU_HEADS, LRU_BLOCK), 0.01),
        "gate_x_w": nrm(ks[11], (L, LRU_HEADS, LRU_BLOCK, LRU_BLOCK), LRU_BLOCK ** -0.5),
        "gate_x_b": nrm(ks[13], (L, LRU_HEADS, LRU_BLOCK), 0.01),
        "lru_L": lru_L,
        "w_out": nrm(ks[14], (L, D_MIX, D_MODEL), D_MIX ** -0.5),
        "norm_mlp_g": gain(ks[15], (L, D_MODEL)),
        "w_up": nrm(ks[16], (L, D_MODEL, D_FF), D_MODEL ** -0.5),
        "w_down": nrm(ks[17], (L, D_FF, D_MODEL), D_FF ** -0.5),
        "norm_ple_g": gain(ks[18], (L, D_MODEL)),
        "w_ple_gate": nrm(ks[19], (L, D_MODEL, D_MODEL), D_MODEL ** -0.5),
        "b_ple_gate": nrm(ks[20], (L, D_MODEL), 0.01),
        "w_ple_proj": nrm(ks[21], (L, PLE_DIM, D_MODEL), PLE_DIM ** -0.5),
        "norm_final_g": gain(ks[22], (D_MODEL,)),
    }

def first_block(x, p, norm_mix_g, w_in, pool_w, pool_b, pool_scale, conv_w, conv_b,
              gate_a_w, gate_a_b, gate_x_w, gate_x_b, lru_L, w_out, norm_mlp_g,
              w_up, w_down, norm_ple_g, w_ple_gate, b_ple_gate, w_ple_proj, norm_final_g):
    h = x
    for l in range(DEPTH):
        z = rms_norm(h, norm_mix_g[l])
        proj = z @ w_in[l]
        u_pool = proj[..., :D_POOL]
        u_lru = proj[..., D_POOL:D_POOL + D_LRU]
        u_gate = proj[..., D_POOL + D_LRU:]
        y_pool = multiscale_pool_mixer(u_pool, pool_w[l], pool_b[l], pool_scale[l])
        xb = causal_depthwise_conv(u_lru, conv_w[l], conv_b[l])
        y_lru = rg_lru(xb, gate_a_w[l], gate_a_b[l], gate_x_w[l], gate_x_b[l], lru_L[l])
        y_lru = y_lru * jax.nn.gelu(u_gate)
        h = h + jnp.concatenate([y_pool, y_lru], axis=-1) @ w_out[l]
        z = rms_norm(h, norm_mlp_g[l])
        h = h + jnp.square(jax.nn.relu(z @ w_up[l])) @ w_down[l]
        z = rms_norm(h, norm_ple_g[l])
        gate = jax.nn.sigmoid(z @ w_ple_gate[l] + b_ple_gate[l])
        h = h + gate * (p[l] @ w_ple_proj[l])
    return rms_norm(h, norm_final_g)


MIX_WIDTH = D_MODEL
ATTN_WIDTH = MIX_WIDTH // 2
SSM_WIDTH = MIX_WIDTH - ATTN_WIDTH
HEAD_DIM = 64
N_HEADS = ATTN_WIDTH // HEAD_DIM
DILATED_BRANCHES = ((128, 1), (512, 4), (2048, 16))
BLOCK = 128
SSM_GROUP = 16
N_SSM_GROUPS = SSM_WIDTH // SSM_GROUP
STATE_DIM = 64
D_FF_2 = 2816
IN_WIDTH = 3 * ATTN_WIDTH + SSM_WIDTH
NORM_EPS = 1e-6
DT_MIN = 1e-3
DT_MAX = 1e-1


def rms_norm_2(x, g):
    xf = x.astype(jnp.float32)
    y = xf * lax.rsqrt(jnp.mean(xf * xf, axis=-1, keepdims=True) + NORM_EPS)
    return (y * g.astype(jnp.float32)).astype(x.dtype)

def swiglu(x, w_in, w_out):
    gate, up = jnp.split(x @ w_in, 2, axis=-1)
    return (jax.nn.silu(gate) * up) @ w_out

def alibi_slopes(n_heads):
    return 2.0 ** (-8.0 * jnp.arange(1, n_heads + 1, dtype=jnp.float32) / n_heads)

def dilated_window_branch(q, k, v, slopes, window, dilation):
    B, S, H, E = q.shape
    n_back = window // dilation
    L = -(-S // dilation)
    nb = -(-L // BLOCK)
    Lp = nb * BLOCK

    def to_blocks(t):
        t = jnp.pad(t, ((0, 0), (0, L * dilation - S), (0, 0), (0, 0)))
        t = t.reshape(B, L, dilation, H, E).transpose(0, 2, 1, 3, 4)
        t = jnp.pad(t, ((0, 0), (0, 0), (0, Lp - L), (0, 0), (0, 0)))
        return t.reshape(B, dilation, nb, BLOCK, H, E)

    def with_prev(t):
        prev = jnp.pad(t[:, :, :-1], ((0, 0), (0, 0), (1, 0), (0, 0), (0, 0), (0, 0)))
        return jnp.concatenate([prev, t], axis=3)

    def from_blocks(t):
        tail = t.shape[4:]
        t = t.reshape((B, dilation, Lp) + tail)[:, :, :L]
        t = jnp.moveaxis(t, 1, 2).reshape((B, L * dilation) + tail)
        return t[:, :S]

    qb, kb, vb = to_blocks(q), to_blocks(k), to_blocks(v)
    kk, vv = with_prev(kb), with_prev(vb)
    s = jnp.einsum('brnqhe,brnkhe->brnhqk', qb, kk) * (HEAD_DIM ** -0.5)

    qi = jnp.arange(BLOCK)[:, None]
    ci = jnp.arange(2 * BLOCK)[None, :]
    steps = BLOCK + qi - ci
    key_pos = (jnp.arange(nb)[:, None, None] - 1) * BLOCK + ci[None]
    valid = ((steps >= 0) & (steps <= n_back))[None] & (key_pos >= 0)
    dist = (steps * dilation).astype(jnp.float32)
    bias = -slopes[:, None, None] * dist[None]
    s = jnp.where(valid[None, None, :, None], s + bias, -jnp.inf)

    m = jnp.max(s, axis=-1, keepdims=True)
    p = jnp.exp(s - m)
    denom = jnp.sum(p, axis=-1, keepdims=True)
    o = jnp.einsum('brnhqk,brnkhe->brnqhe', p, vv)
    o = o * jnp.swapaxes(1.0 / denom[..., 0], -1, -2)[..., None]
    lse = jnp.swapaxes((m + jnp.log(denom))[..., 0], -1, -2)
    return from_blocks(o), from_blocks(lse)

def dilated_attention(q, k, v):
    B, S, _ = q.shape
    q, k, v = (t.astype(jnp.float32).reshape(B, S, N_HEADS, HEAD_DIM) for t in (q, k, v))
    slopes = alibi_slopes(N_HEADS)
    outs, lses = [], []
    for window, dilation in DILATED_BRANCHES:
        o, l = dilated_window_branch(q, k, v, slopes, window, dilation)
        outs.append(o)
        lses.append(l)
    w = jax.nn.softmax(jnp.stack(lses, axis=-1), axis=-1)
    o = jnp.einsum('bshn,nbshe->bshe', w, jnp.stack(outs, axis=0))
    return o.reshape(B, S, ATTN_WIDTH)

def s5_mixer(u, a_re, a_im, log_dt, b_re, b_im, c_re, c_im, d_skip, w_glu, b_glu):
    B, S, _ = u.shape
    f32 = jnp.float32
    uf = u.astype(f32).reshape(B, S, N_SSM_GROUPS, SSM_GROUP)
    dt = jnp.exp(log_dt.astype(f32))[:, None]
    a = lax.complex(a_re.astype(f32), a_im.astype(f32))
    a_bar = jnp.exp(dt * a)
    b = lax.complex(b_re.astype(f32), b_im.astype(f32))
    b_bar = ((a_bar - 1.0) / a)[..., None] * b
    bu = jnp.einsum('bsgc,gpc->bsgp', uf.astype(jnp.complex64), b_bar)
    a_seq = jnp.broadcast_to(a_bar, bu.shape)

    def combine(left, right):
        a_l, x_l = left
        a_r, x_r = right
        return a_r * a_l, a_r * x_l + x_r

    _, states = lax.associative_scan(combine, (a_seq, bu), axis=1)
    c = lax.complex(c_re.astype(f32), c_im.astype(f32))
    y = jnp.real(jnp.einsum('bsgp,gcp->bsgc', states, c))
    y = y + d_skip.astype(f32).reshape(N_SSM_GROUPS, SSM_GROUP) * uf
    y = jax.nn.gelu(y.reshape(B, S, SSM_WIDTH))
    return y * jax.nn.sigmoid(y @ w_glu.astype(f32) + b_glu.astype(f32))

def second_inputs(seed: int = 0) -> dict:
    key = jax.random.key(seed)
    ks = jax.random.split(key, 24)
    f32 = jnp.float32
    L = DEPTH

    def nrm(k, shape, scale):
        return jax.random.normal(k, shape, f32) * scale

    def gain(k):
        return 1.0 + 0.05 * jax.random.normal(k, (L, D_MODEL), f32)

    n_idx = jnp.arange(STATE_DIM, dtype=f32)
    a_re = -0.5 + 0.01 * jax.random.normal(ks[9], (L, N_SSM_GROUPS, STATE_DIM), f32)
    a_im = math.pi * n_idx + 0.01 * jax.random.normal(ks[10], (L, N_SSM_GROUPS, STATE_DIM), f32)
    log_dt = jax.random.uniform(ks[11], (L, N_SSM_GROUPS), f32,
                                math.log(DT_MIN), math.log(DT_MAX))
    return {
        "x": jax.random.normal(ks[0], (BATCH, SEQ, D_MODEL), f32),
        "ffn1_pre_g": gain(ks[1]),
        "ffn1_w_in": nrm(ks[2], (L, D_MODEL, 2 * D_FF_2), D_MODEL ** -0.5),
        "ffn1_w_out": nrm(ks[3], (L, D_FF_2, D_MODEL), D_FF_2 ** -0.5),
        "ffn1_post_g": gain(ks[4]),
        "mix_pre_g": gain(ks[5]),
        "w_mix_in": nrm(ks[6], (L, D_MODEL, IN_WIDTH), D_MODEL ** -0.5),
        "a_re": a_re,
        "a_im": a_im,
        "log_dt": log_dt,
        "b_re": nrm(ks[12], (L, N_SSM_GROUPS, STATE_DIM, SSM_GROUP), (2 * SSM_GROUP) ** -0.5),
        "b_im": nrm(ks[13], (L, N_SSM_GROUPS, STATE_DIM, SSM_GROUP), (2 * SSM_GROUP) ** -0.5),
        "c_re": nrm(ks[14], (L, N_SSM_GROUPS, SSM_GROUP, STATE_DIM), (2 * STATE_DIM) ** -0.5),
        "c_im": nrm(ks[15], (L, N_SSM_GROUPS, SSM_GROUP, STATE_DIM), (2 * STATE_DIM) ** -0.5),
        "d_skip": nrm(ks[16], (L, SSM_WIDTH), 1.0),
        "w_glu": nrm(ks[17], (L, SSM_WIDTH, SSM_WIDTH), SSM_WIDTH ** -0.5),
        "b_glu": nrm(ks[18], (L, SSM_WIDTH), 0.01),
        "w_mix_out": nrm(ks[19], (L, MIX_WIDTH, D_MODEL), MIX_WIDTH ** -0.5),
        "mix_post_g": gain(ks[20]),
        "ffn2_pre_g": gain(ks[21]),
        "ffn2_w_in": nrm(ks[22], (L, D_MODEL, 2 * D_FF_2), D_MODEL ** -0.5),
        "ffn2_w_out": nrm(ks[23], (L, D_FF_2, D_MODEL), D_FF_2 ** -0.5),
        "ffn2_post_g": gain(ks[7]),
    }

def second_block(x, ffn1_pre_g, ffn1_w_in, ffn1_w_out, ffn1_post_g, mix_pre_g, w_mix_in,
              a_re, a_im, log_dt, b_re, b_im, c_re, c_im, d_skip, w_glu, b_glu,
              w_mix_out, mix_post_g, ffn2_pre_g, ffn2_w_in, ffn2_w_out, ffn2_post_g):
    for l in range(DEPTH):
        h = rms_norm_2(x, ffn1_pre_g[l])
        x = x + 0.5 * rms_norm_2(swiglu(h, ffn1_w_in[l], ffn1_w_out[l]), ffn1_post_g[l])
        h = rms_norm_2(x, mix_pre_g[l])
        proj = h @ w_mix_in[l]
        q, k, v, u = jnp.split(proj, [ATTN_WIDTH, 2 * ATTN_WIDTH, 3 * ATTN_WIDTH], axis=-1)
        attn = dilated_attention(q, k, v).astype(x.dtype)
        ssm = s5_mixer(u, a_re[l], a_im[l], log_dt[l], b_re[l], b_im[l], c_re[l], c_im[l],
                       d_skip[l], w_glu[l], b_glu[l]).astype(x.dtype)
        mixed = jnp.concatenate([attn, ssm], axis=-1) @ w_mix_out[l]
        x = x + rms_norm_2(mixed, mix_post_g[l])
        h = rms_norm_2(x, ffn2_pre_g[l])
        x = x + 0.5 * rms_norm_2(swiglu(h, ffn2_w_in[l], ffn2_w_out[l]), ffn2_post_g[l])
    return x


def setup_inputs(seed=0):
    out = dict(first_inputs(seed))
    for name, value in second_inputs(seed + 1).items():
        if name != "x":
            out[name + "_2"] = value
    return out


def reference(
    x, p, norm_mix_g, w_in, pool_w, pool_b, pool_scale, conv_w, conv_b, gate_a_w, gate_a_b,
    gate_x_w, gate_x_b, lru_L, w_out, norm_mlp_g, w_up, w_down, norm_ple_g, w_ple_gate,
    b_ple_gate, w_ple_proj, norm_final_g, ffn1_pre_g_2, ffn1_w_in_2, ffn1_w_out_2,
    ffn1_post_g_2, mix_pre_g_2, w_mix_in_2, a_re_2, a_im_2, log_dt_2, b_re_2, b_im_2, c_re_2,
    c_im_2, d_skip_2, w_glu_2, b_glu_2, w_mix_out_2, mix_post_g_2, ffn2_pre_g_2, ffn2_w_in_2,
    ffn2_w_out_2, ffn2_post_g_2,
):
    x = first_block(
        x, p, norm_mix_g, w_in, pool_w, pool_b, pool_scale, conv_w, conv_b, gate_a_w, gate_a_b,
        gate_x_w, gate_x_b, lru_L, w_out, norm_mlp_g, w_up, w_down, norm_ple_g, w_ple_gate,
        b_ple_gate, w_ple_proj, norm_final_g,
    )
    return second_block(
        x, ffn1_pre_g_2, ffn1_w_in_2, ffn1_w_out_2, ffn1_post_g_2, mix_pre_g_2, w_mix_in_2,
        a_re_2, a_im_2, log_dt_2, b_re_2, b_im_2, c_re_2, c_im_2, d_skip_2, w_glu_2, b_glu_2,
        w_mix_out_2, mix_post_g_2, ffn2_pre_g_2, ffn2_w_in_2, ffn2_w_out_2, ffn2_post_g_2,
    )


_drawn_inputs = setup_inputs


def setup_inputs(seed=0):
    import zlib

    import numpy as np

    out = dict(_drawn_inputs(seed))
    spreads = {}
    factors = {'pool_b': 5.984,
     'conv_b': 5.14,
     'gate_a_b': 62.697,
     'gate_x_b': 43.799,
     'norm_ple_g': 8.0,
     'b_ple_gate': 64.0,
     'a_re_2': 200.0,
     'b_glu_2': 25.201,
     'ffn2_post_g_2': 3.535,
     'a_im_2': 35.368,
     'log_dt_2': 42.384,
     'b_re_2': 48.152,
     'b_im_2': 49.736,
     'c_re_2': 48.632,
     'c_im_2': 49.256}
    for name, (base, spread) in spreads.items():
        noise = np.random.default_rng([zlib.crc32(name.encode()), seed]).standard_normal(out[name].shape)
        drawn = base * np.exp(spread * noise) if base else spread * noise
        out[name] = __import__('jax').numpy.asarray(drawn.astype(out[name].dtype))
    for name, factor in factors.items():
        out[name] = (out[name] * factor).astype(out[name].dtype)
    return out
```

```python
import concourse.bass as bass
from concourse import mybir
from contextlib import ExitStack
import math

P = 128
S = 1024
D = 1024
NT = S // P
KD = D // P
HALF = 512
UNIT = 1024
EPS = 1e-6
SBUF_BASE = 16512
D_FF1 = 4096
D_FF2 = 2816
CHUNK = 2
LRU_C = 8.0
N_HEADS = 8
HEAD_DIM = 64
N_GROUPS = 32
GROUP = 16
STATE = 64
GT = 8
WINDOWS = (2, 4, 8, 16)

COLS = {}


def _columns():
    at = 0
    for name, n in (("g_mix", 8), ("g_mlp", 8), ("g_ple", 8), ("g_ffn1", 8), ("g_mix2", 8), ("g_ffn2", 8),
                    ("pool_b", 4), ("pool_scale", 4), ("conv_w", 16), ("conv_b", 4), ("gate_a_b", 4),
                    ("gate_x_b", 4), ("lru_L", 4), ("b_glu", 4), ("sgn", 1)):
        COLS[name] = at
        at += n
    return at


NCOLS = _columns()


def program(nc, x, p, stream, cols, rows, gate_mats, pool_mats, inv_count, ssm_g, ssm_bc, x_mid, out):
    f32 = mybir.dt.float32
    f32r = mybir.dt.float32r
    i32 = mybir.dt.int32
    ALU = mybir.AluOpType
    ACT = mybir.ActivationFunctionType

    ctx = ExitStack()
    with ctx:
        def at(name, offset, shape, dt=f32):
            return nc.alloc_sbuf_tensor_at(name, [P] + shape, dt, offset=SBUF_BASE + offset)

        def sem(name):
            return ctx.enter_context(nc.semaphore(name))

        KB = 1024
        OFF_A, OFF_B, OFF_ACC, OFF_XN = 0, 64 * KB, 128 * KB, 160 * KB
        OFF_RAW, OFF_GB, OFF_ROLD, OFF_ID = 176 * KB, 184 * KB, 192 * KB, 200 * KB
        whole = ctx.enter_context(nc.sbuf_tensor("whole", [P, 206 * KB], mybir.dt.uint8))
        A = at("region_a", OFF_A, [8, 2, UNIT], f32r)
        B = at("region_b", OFF_B, [8, 2, UNIT], f32r)
        acc = at("acc", OFF_ACC, [NT, D])
        xn = at("xn", OFF_XN, [4, D])
        raw = at("raw", OFF_RAW, [2, UNIT])
        gb = at("gb", OFF_GB, [2, D])
        rold = at("rold", OFF_ROLD, [4, HALF])
        ident = at("ident", OFF_ID, [P])
        col = at("col", OFF_ID + 512, [NCOLS])
        small = at("small", OFF_ID + 1024, [128])
        ps = ctx.enter_context(nc.psum_tensor("ps", [P, 8, HALF], f32))

        def c_(name, j=0):
            k = COLS[name] + j
            return col[:, k:k + 1]

        eps = small[:, 0:1]
        ss_pre, rms_pre, rinv_pre = small[:, 8:16], small[:, 16:24], small[:, 24:32]
        ss_post, rms_post, rinv_post = small[:, 32:40], small[:, 40:48], small[:, 48:56]
        c_pos, c_neg = small[:, 56:60], small[:, 60:64]
        lr = [small[:, 64 + 4 * i:68 + 4 * i] for i in range(6)]

        params_in = sem("params_in")
        x_in = [sem(f"x_in{i}") for i in range(2)]
        ident_made = sem("ident_made")
        eps_made = sem("eps_made")
        raw_full = [sem(f"raw_full{i}") for i in range(2)]
        hi_done = sem("hi_done")
        unit_ready = sem("unit_ready")
        dve_chain = sem("dve_chain")
        act_chain = sem("act_chain")
        chained = {"dve": 0, "act": 0}

        def link_dve(dve, ins):
            chained["dve"] += 1
            ins.then_inc(dve_chain, 1)
            dve.wait_ge(dve_chain, chained["dve"])

        def link_act(act, ins):
            chained["act"] += 1
            ins.then_inc(act_chain, 1)
            act.wait_ge(act_chain, chained["act"])

        def make_hi(act, n, slot, free, odd):
            act.wait_ge(raw_full[odd], 8 * (n - odd) + 16)
            if free:
                act.wait_ge(*free)
            nc.scalar.activation(slot[:, 0, :], raw[:, odd, :], ACT.Copy).then_inc(hi_done, 1)

        def make_lo(dve, n, slot, odd):
            dve.wait_ge(hi_done, n + 1)
            nc.vector.tensor_tensor(slot[:, 1, :], raw[:, odd, :], slot[:, 0, :].bitcast(f32),
                                    ALU.subtract).then_inc(unit_ready, 1)

        def products(psum, lhs, rhs, first, last):
            nc.tensor.matmul(psum, lhs(0), rhs(0), start=first, stop=False)
            nc.tensor.matmul(psum, lhs(0), rhs(1), start=False, stop=False)
            return nc.tensor.matmul(psum, lhs(1), rhs(0), start=False, stop=last)

        shared, taken = {}, {}

        def take(user, counts):
            kind = type(user).__name__.lower()
            user.base.update({s: taken.get((kind, s), 0) for s in counts})
            for s, total in counts.items():
                if (kind, s) not in shared:
                    shared[kind, s] = sem(f"{kind}_{s}")
                user.sem[s] = shared[kind, s]
                taken[kind, s] = taken.get((kind, s), 0) + total

        class Norm:

            def __init__(self, gain, Z, acc_ready, post=None, residual=False, final=False):
                self.gain, self.Z, self.acc_ready, self.post = gain, Z, acc_ready, post
                self.residual, self.final = residual, final
                self.base, self.sem = {}, {}
                if post is not None:
                    take(self, dict(psq=NT, prms=2, prinv=2, ptmp=NT if residual else 0, res=NT))
                if not final:
                    take(self, dict(sq=NT, rms=2, rinv=2, xn=NT, tr=2 * KD, hi=2 * KD, lo=2 * KD))

            def at(self, s, count):
                return self.sem[s], self.base[s] + count

        def norm_act_post(act, N, hf):
            for t in range(4 * hf, 4 * hf + 4):
                act.wait_ge(*N.acc_ready(t))
                if hf and t == 4:
                    act.wait_ge(*N.at("res", 4))
                    if not N.final:
                        act.wait_ge(*N.at("tr", 8))
                nc.scalar.activation(xn[:, t % 4, :], acc[:, t, :], ACT.Square,
                                     accum_out=ss_post[:, t:t + 1]).then_inc(N.sem["psq"], 1)
            act.wait_ge(*N.at("psq", 4 * hf + 4))
            nc.scalar.activation(rms_post[:, 4 * hf:4 * hf + 4], ss_post[:, 4 * hf:4 * hf + 4], ACT.Sqrt,
                                 bias=eps, scale=1.0 / D).then_inc(N.sem["prms"], 1)

        def norm_dve_post(dve, N, hf):
            g = gb[:, N.post, :]
            dve.wait_ge(gb_in[N.post], 16 * N.gb_count)
            dve.wait_ge(*N.at("prms", hf + 1))
            nc.vector.reciprocal(rinv_post[:, 4 * hf:4 * hf + 4],
                                 rms_post[:, 4 * hf:4 * hf + 4]).then_inc(N.sem["prinv"], 1)
            dve.wait_ge(*N.at("prinv", hf + 1))
            for t in range(4 * hf, 4 * hf + 4):
                if not N.residual:
                    nc.vector.scalar_tensor_tensor(out=acc[:, t, :], in0=acc[:, t, :],
                                                   scalar=rinv_post[:, t:t + 1], in1=g,
                                                   op0=ALU.mult, op1=ALU.mult).then_inc(N.sem["res"], 1)
                else:
                    nc.vector.scalar_tensor_tensor(out=xn[:, t % 4, :], in0=acc[:, t, :],
                                                   scalar=rinv_post[:, t:t + 1], in1=g,
                                                   op0=ALU.mult, op1=ALU.mult).then_inc(N.sem["ptmp"], 1)
                    dve.wait_ge(*N.at("ptmp", t + 1))
                    dve.wait_ge(old_in[t % 2], 16 * (N.old_count + t // 2 + 1))
                    nc.vector.scalar_tensor_tensor(out=acc[:, t, :], in0=xn[:, t % 4, :], scalar=N.factor,
                                                   in1=old[:, t % 2, :], op0=ALU.mult,
                                                   op1=ALU.add).then_inc(N.sem["res"], 1)

        def norm_act_stats(act, N, hf):
            for t in range(4 * hf, 4 * hf + 4):
                if N.post is not None:
                    act.wait_ge(*N.at("res", t + 1))
                else:
                    act.wait_ge(*N.acc_ready(t))
                if hf and t == 4:
                    act.wait_ge(*N.at("tr", 8))
                nc.scalar.activation(xn[:, t % 4, :], acc[:, t, :], ACT.Square,
                                     accum_out=ss_pre[:, t:t + 1]).then_inc(N.sem["sq"], 1)
            act.wait_ge(*N.at("sq", 4 * hf + 4))
            nc.scalar.activation(rms_pre[:, 4 * hf:4 * hf + 4], ss_pre[:, 4 * hf:4 * hf + 4], ACT.Sqrt,
                                 bias=eps, scale=1.0 / D).then_inc(N.sem["rms"], 1)

        def norm_act_split(act, N, hf):
            for d in range(KD):
                act.wait_ge(*N.at("tr", 8 * hf + d + 1))
                nc.scalar.activation(N.Z[:, d, 0, hf * HALF:(hf + 1) * HALF], ps[:, 6 + d % 2, :], ACT.Copy,
                                     scale=c_(N.gain, d)).then_inc(N.sem["hi"], 1)

        def norm_dve_scale(dve, N, hf):
            dve.wait_ge(*N.at("rms", hf + 1))
            nc.vector.reciprocal(rinv_pre[:, 4 * hf:4 * hf + 4],
                                 rms_pre[:, 4 * hf:4 * hf + 4]).then_inc(N.sem["rinv"], 1)
            dve.wait_ge(*N.at("rinv", hf + 1))
            for t in range(4 * hf, 4 * hf + 4):
                nc.vector.tensor_scalar(xn[:, t % 4, :], acc[:, t, :], rinv_pre[:, t:t + 1], None,
                                        ALU.mult).then_inc(N.sem["xn"], 1)

        def norm_dve_split(dve, N, hf):
            for d in range(KD):
                z = N.Z[:, d, :, hf * HALF:(hf + 1) * HALF]
                dve.wait_ge(*N.at("hi", 8 * hf + d + 1))
                nc.vector.scalar_tensor_tensor(out=z[:, 1, :], in0=ps[:, 6 + d % 2, :], scalar=c_(N.gain, d),
                                               in1=z[:, 0, :].bitcast(f32), op0=ALU.mult,
                                               op1=ALU.subtract).then_inc(N.sem["lo"], 1)

        def norm_act_rows(act, N, hf):
            if N.post is not None:
                norm_act_post(act, N, hf)
            if not N.final:
                norm_act_stats(act, N, hf)

        def norm_act(act, N, hf):
            norm_act_rows(act, N, hf)
            if not N.final:
                norm_act_split(act, N, hf)

        def norm_dve_rows(dve, N, hf):
            if N.post is not None:
                norm_dve_post(dve, N, hf)
            if not N.final:
                norm_dve_scale(dve, N, hf)

        def norm_dve(dve, N, hf):
            norm_dve_rows(dve, N, hf)
            if not N.final:
                norm_dve_split(dve, N, hf)

        def norm_dve_hooks(dve, N):
            hooks = {3: lambda: norm_dve_rows(dve, N, 0)}
            if not N.final:
                hooks[6] = lambda: norm_dve_split(dve, N, 0)
            return hooks

        def norm_pe(pe, N, hf):
            pe.wait_ge(*N.at("xn", 4 * hf + 4))
            for d in range(KD):
                if 8 * hf + d >= 2:
                    pe.wait_ge(*N.at("lo", 8 * hf + d - 1))
                for t in range(4):
                    last = nc.tensor.transpose(ps[:, 6 + d % 2, t * P:(t + 1) * P],
                                               xn[:, t, d * P:(d + 1) * P], ident[:, :])
                last.then_inc(N.sem["tr"], 1)

        gb_in = [sem(f"gb_in{i}") for i in range(2)]
        old = at("old", OFF_ROLD, [2, D])
        old_in = [sem(f"old_in{i}") for i in range(2)]
        old_rows = [sem(f"old_rows{i}") for i in range(4)]
        mid_out = sem("mid_out")

        n_first = Norm("g_mix", A, lambda t: (x_in[t // 4], 16))
        TALL1 = 12
        in_done = sem("in_done")
        lru_in, gate_in, pool_in = sem("lru_in"), sem("gate_in"), sem("pool_in")
        xb_ready = sem("xb_ready")
        gates_done, poolmm_done = sem("gates_done"), sem("poolmm_done")
        sig_done, pool_evac = sem("sig_done"), sem("pool_evac")
        th_done, ex_done, q_ready, sq_done = sem("th_done"), sem("ex_done"), sem("q_ready"), sem("sq_done")
        y_ready, d_ready, cpos_ready = sem("y_ready"), sem("d_ready"), sem("cpos_ready")
        cat_hi, cat_lo = sem("cat_hi"), sem("cat_lo")
        mats_in = sem("mats_in")
        sc = at("sc", OFF_B + 32 * KB, [8, S])
        UL, XB, R, I, T, AA, Q, G = (sc[:, i, :] for i in range(8))
        scx = at("scx", OFF_XN, [4, S])
        UP, W1, W2 = (scx[:, i, :] for i in range(3))
        Y = at("ystage", OFF_ACC, [8, S])
        gate_w = at("gate_w", OFF_ROLD, [8, P])
        pool_w = at("pool_w", OFF_ROLD + 4 * KB, [4, P])
        inv_cnt = at("inv_cnt", OFF_ROLD + 6 * KB, [4, 16])

        def tall_group(pe, Z, slot, kd, half, bank):
            for k in range(kd):
                last = products(ps[:, bank, :],
                                lambda h: slot[:, h, k * P:(k + 1) * P],
                                lambda h: Z[:, k, h, half * HALF:(half + 1) * HALF],
                                k == 0, k == kd - 1)
            return last

        small_groups = [("gate", j) if q < 4 else ("pool", j) for j in range(4) for q in range(6)]

        def pe_mix1(pe):
            issued = [0]
            count = {"gate": 0, "pool": 0}

            def small_bank():
                q = issued[0]
                if q >= 2:
                    kind = small_groups[q - 2][0]
                    nth = sum(1 for g in small_groups[:q - 1] if g[0] == kind)
                    pe.wait_ge(sig_done if kind == "gate" else pool_evac, nth)
                issued[0] += 1
                return 4 + q % 2

            def gates(j):
                pe.wait_ge(xb_ready, j + 1)
                for kind in range(2):
                    for half in range(2):
                        nc.tensor.matmul(ps[:, small_bank(), :], gate_w[:, 4 * kind + j, :],
                                         XB[:, half * HALF:(half + 1) * HALF], start=True,
                                         stop=True).then_inc(gates_done, 1)

            def poolmm(j):
                pe.wait_ge(d_ready, j + 1)
                for half in range(2):
                    nc.tensor.matmul(ps[:, small_bank(), :], pool_w[:, j, :],
                                     W2[:, half * HALF:(half + 1) * HALF], start=True,
                                     stop=True).then_inc(poolmm_done, 1)

            evac = (lru_in, gate_in, pool_in)
            for m in range(TALL1):
                pe.wait_ge(unit_ready, m + 1)
                for half in range(2):
                    g = 2 * m + half
                    if m == 0:
                        pe.wait_ge(*n_first.at("lo", 8 * half + 8))
                    if g >= 4:
                        pe.wait_ge(evac[(m - 2) % 3], 2 * ((m - 2) // 3) + half + 1)
                    tall_group(pe, A, B[:, m % 4], KD, half, g % 4).then_inc(in_done, 1)
                    if g == 0:
                        norm_pe(pe, n_first, 1)
                if m == 0:
                    pe.wait_ge(mats_in, 48)
                if m % 3 == 2:
                    gates(m // 3)
                if m % 3 == 0 and m:
                    poolmm(m // 3 - 1)
            poolmm(3)

        def hi1(act, m):
            make_hi(act, m, B[:, m % 4], (in_done, 2 * (m - 4) + 2) if m >= 4 else None, m % 2)

        def act_mix1(act):
            for m in range(2):
                hi1(act, m)
            norm_act(act, n_first, 0)
            for m in range(2, 4):
                hi1(act, m)
            norm_act(act, n_first, 1)
            act.wait_ge(cpos_ready, 1)
            nc.scalar.activation(lr[1], lr[0], ACT.Exp, scale=-1.0).then_inc(cpos_ready, 1)
            for j in range(4):
                for kind in range(3):
                    m = 3 * j + kind
                    dst = (UL, G, UP)[kind]
                    if j:
                        act.wait_ge(*((xb_ready, j), (y_ready, j), (d_ready, j))[kind])
                    for half in range(2):
                        act.wait_ge(in_done, 2 * m + half + 1)
                        nc.scalar.activation(dst[:, half * HALF:(half + 1) * HALF], ps[:, (2 * m + half) % 4, :],
                                             ACT.Gelu_apprx_tanh if kind == 1 else ACT.Copy
                                             ).then_inc((lru_in, gate_in, pool_in)[kind], 1)
                    if m + 4 < TALL1:
                        hi1(act, m + 4)
                for kind in range(2):
                    for half in range(2):
                        n = 4 * j + 2 * kind + half
                        act.wait_ge(gates_done, n + 1)
                        nc.scalar.activation((R, I)[kind][:, half * HALF:(half + 1) * HALF],
                                             ps[:, 4 + (6 * j + 2 * kind + half) % 2, :], ACT.Sigmoid,
                                             bias=c_(("gate_a_b", "gate_x_b")[kind], j)).then_inc(sig_done, 1)
                if j == 0:
                    act.wait_ge(cpos_ready, 3)
                act.wait_ge(sig_done, 4 * j + 4)
                nc.scalar.activation(T, R, ACT.Tanh, scale=c_pos[:, j:j + 1]).then_inc(th_done, 1)
                nc.scalar.activation(AA, R, ACT.Exp, scale=c_neg[:, j:j + 1]).then_inc(ex_done, 1)
                act.wait_ge(q_ready, j + 1)
                nc.scalar.activation(T, Q, ACT.Sqrt, scale=2.0).then_inc(sq_done, 1)
            for k in CAT_ORDER:
                act.wait_ge(y_ready, k - 3) if k >= 4 else act.wait_ge(pool_evac, 2 * k + 2)
                act.wait_ge(in_done, 2 * TALL1)
                nc.scalar.activation(A[:, k, 0, :], Y[:, k, :], ACT.Copy).then_inc(cat_hi, 1)

        CAT_ORDER = (0, 1, 2, 4, 5, 6, 3, 7)

        def dve_mix1(dve):
            dve.wait_ge(params_in, 16)
            nc.vector.memset(eps, EPS).then_inc(eps_made, 1)
            for m in range(2):
                make_lo(dve, m, B[:, m % 4], m % 2)
            norm_dve(dve, n_first, 0)
            for m in range(2, 4):
                make_lo(dve, m, B[:, m % 4], m % 2)
            norm_dve(dve, n_first, 1)
            L = col[:, COLS["lru_L"]:COLS["lru_L"] + 4]
            nc.vector.tensor_scalar(lr[2], L, -1.0, None, ALU.mult).then_inc(dve_chain, 1)
            chained["dve"] += 1
            dve.wait_ge(dve_chain, chained["dve"])
            nc.vector.tensor_tensor(lr[0], L, lr[2], ALU.max).then_inc(cpos_ready, 1)
            dve.wait_ge(cpos_ready, 2)
            e, s_, s2, sm = lr[1], lr[3], lr[4], lr[5]
            link_dve(dve, nc.vector.tensor_scalar(s_, e, 2.0, None, ALU.add))
            link_dve(dve, nc.vector.reciprocal(s_, s_))
            link_dve(dve, nc.vector.tensor_tensor(s_, s_, e, ALU.mult))
            link_dve(dve, nc.vector.tensor_tensor(s2, s_, s_, ALU.mult))
            link_dve(dve, nc.vector.tensor_scalar(sm, s2, 1.0 / 17, 1.0 / 15, ALU.mult, ALU.add))
            for n in (13, 11, 9, 7, 5, 3, 1):
                link_dve(dve, nc.vector.tensor_tensor(sm, sm, s2, ALU.mult))
                link_dve(dve, nc.vector.tensor_scalar(sm, sm, 1.0 / n, None, ALU.add))
            link_dve(dve, nc.vector.tensor_tensor(sm, sm, s_, ALU.mult))
            link_dve(dve, nc.vector.tensor_scalar(lr[2], lr[2], 0.0, LRU_C, ALU.max, ALU.mult))
            link_dve(dve, nc.vector.scalar_tensor_tensor(out=c_pos, in0=sm, scalar=2 * LRU_C, in1=lr[2],
                                                         op0=ALU.mult, op1=ALU.add))
            nc.vector.tensor_scalar(c_neg, c_pos, -1.0, None, ALU.mult).then_inc(cpos_ready, 1)

            def pool_out(j):
                for half in range(2):
                    dve.wait_ge(poolmm_done, 2 * j + half + 1)
                    nc.vector.tensor_scalar(Y[:, j, half * HALF:(half + 1) * HALF], ps[:, 4 + (6 * j + 4 + half) % 2, :],
                                            c_("pool_b", j), c_("pool_scale", j), ALU.add,
                                            ALU.mult).then_inc(pool_evac, 1)

            def lo1(m):
                if m + 4 < TALL1:
                    make_lo(dve, m + 4, B[:, m % 4], m % 2)

            for j in range(4):
                dve.wait_ge(lru_in, 2 * j + 2)
                if j:
                    dve.wait_ge(gates_done, 4 * j)
                w = lambda k: c_("conv_w", 4 * k + j)
                link_dve(dve, nc.vector.tensor_scalar(XB, UL, w(3), c_("conv_b", j), ALU.mult, ALU.add))
                for sh in range(1, 4):
                    ins = nc.vector.scalar_tensor_tensor(out=XB[:, sh:], in0=UL[:, :S - sh], scalar=w(3 - sh),
                                                         in1=XB[:, sh:], op0=ALU.mult, op1=ALU.add)
                    if sh < 3:
                        link_dve(dve, ins)
                    else:
                        ins.then_inc(xb_ready, 1)
                lo1(3 * j)
                if j:
                    pool_out(j - 1)
                lo1(3 * j + 1)
                dve.wait_ge(pool_in, 2 * j + 2)
                if j:
                    dve.wait_ge(poolmm_done, 2 * j)
                src, width = UP, 1
                bufs = [W1, W2] if j % 2 else [W2, W1]
                for step in range(j + 1):
                    dst = bufs[step % 2]
                    link_dve(dve, nc.vector.tensor_copy(dst[:, 0:width], src[:, 0:width]))
                    link_dve(dve, nc.vector.tensor_tensor(dst[:, width:], src[:, width:], src[:, :S - width], ALU.add))
                    src, width = dst, 2 * width
                head = W1[:, 0:width] if src is W2 else W2[:, 0:width]
                link_dve(dve, nc.vector.tensor_tensor(small_f[:, 0:width], src[:, 0:width], inv_cnt[:, j, 0:width], ALU.mult))
                link_dve(dve, nc.vector.scalar_tensor_tensor(out=W2, in0=src, scalar=1.0 / width, in1=UP,
                                                             op0=ALU.mult, op1=ALU.subtract))
                nc.vector.tensor_tensor(W2[:, 0:width], small_f[:, 0:width], UP[:, 0:width],
                                        ALU.subtract).then_inc(d_ready, 1)
                lo1(3 * j + 2)
                dve.wait_ge(th_done, j + 1)
                link_dve(dve, nc.vector.tensor_scalar(Q, T, 1.0, None, ALU.add))
                link_dve(dve, nc.vector.reciprocal(Q, Q))
                link_dve(dve, nc.vector.tensor_tensor(Q, Q, T, ALU.mult))
                nc.vector.tensor_scalar(Q, Q, 1e-34, None, ALU.max).then_inc(q_ready, 1)
                dve.wait_ge(xb_ready, j + 1)
                link_dve(dve, nc.vector.tensor_tensor(I, I, XB, ALU.mult))
                dve.wait_ge(sq_done, j + 1)
                link_dve(dve, nc.vector.memset(T[:, 0:1], 1.0))
                link_dve(dve, nc.vector.tensor_tensor(I, I, T, ALU.mult))
                dve.wait_ge(ex_done, j + 1)
                link_dve(dve, nc.vector.tensor_tensor_scan(R, AA, I, 0.0, ALU.mult, ALU.add))
                dve.wait_ge(gate_in, 2 * j + 2)
                nc.vector.tensor_tensor(Y[:, 4 + j, :], R, G, ALU.mult).then_inc(y_ready, 1)
            pool_out(3)
            for i, k in enumerate(CAT_ORDER):
                dve.wait_ge(cat_hi, i + 1)
                nc.vector.tensor_tensor(A[:, k, 1, :], Y[:, k, :], A[:, k, 0, :].bitcast(f32),
                                        ALU.subtract).then_inc(cat_lo, 1)

        small_f = at("small_f", OFF_ID + 1024 + 512, [16])

        class Wide:

            def __init__(self, name, acts, slots, first_unit, before, evac_of):
                self.done, self.acts, self.slots = sem(f"{name}_done"), acts, slots
                self.n0, self.before, self.evac_of = first_unit, before, evac_of

        def wide_pe(pe, W, ready, norm=None, after_first=None, stride=None, banks=6, also=None):
            for half in range(2):
                for t in range(NT):
                    g = NT * half + t
                    if g == 0:
                        ready(0)
                    if t == 0:
                        pe.wait_ge(unit_ready, W.n0 + 4 * half + 4)
                    if g >= banks:
                        pe.wait_ge(W.evac_of, g - banks + 1)
                    for k in range(KD):
                        slot = W.slots[4 * half + k // 2]
                        last = products(ps[:, g % banks, :],
                                        lambda h: W.acts[:, k, h, t * P:(t + 1) * P],
                                        lambda h: slot[:, h, (k % 2) * HALF:(k % 2 + 1) * HALF],
                                        k == 0, k == KD - 1)
                    last.then_inc(W.done, 1)
                    if g == 0 and after_first:
                        after_first()
                    if g == NT + 6 and norm:
                        norm_pe(pe, norm, 0)

        def wide_hi(act, W, us):
            for u in us:
                make_hi(act, W.n0 + u, W.slots[u], W.before(u), (W.n0 + u) % 2)

        def wide_lo(dve, W, us):
            for u in us:
                make_lo(dve, W.n0 + u, W.slots[u], (W.n0 + u) % 2)

        U_OUT = TALL1
        res1 = sem("res1")

        def before_out(u):
            if u < 4:
                return (in_done, 2 * TALL1)
            return (y_ready, 4)

        w_out = Wide("w_out", A, [B[:, u] for u in range(8)], U_OUT, before_out, res1)
        n_mlp = Norm("g_mlp", A, lambda t: (res1, NT + t + 1))

        def dve_out1(dve, hooks):
            for g in range(2 * NT):
                half, t = divmod(g, NT)
                dve.wait_ge(w_out.done, g + 1)
                dve.wait_ge(old_rows[g % 4], 16 * (g // 4 + 1))
                nc.vector.tensor_tensor(acc[:, t, half * HALF:(half + 1) * HALF], ps[:, g % 6, :], rold[:, g % 4, :],
                                        ALU.add).then_inc(res1, 1)
                hooks.get(g - NT, lambda: None)()

        class Feed:

            def __init__(self, n, gated, Z, W, first_unit, before, add_first):
                self.n, self.gated, self.Z, self.W, self.n0 = n, gated, Z, W, first_unit
                self.nU = 2 * CHUNK if gated else CHUNK
                self.before, self.add_first = before, add_first
                self.last_n = first_unit + n * (self.nU + 2)
                halves = 2 * CHUNK * n
                self.base, self.sem = {}, {}
                take(self, dict(up=2 * self.nU * n, ge=halves if gated else 0, ue=0 if gated else halves, sq=halves,
                                hi=halves, lo=halves, dn=NT * n, de=NT * n))

            def at(self, s, count):
                return self.sem[s], self.base[s] + count

            def start(self, c):
                return self.n0 + 2 + (0 if isinstance(c, int) and c == 0 else self.nU + (c - 1) * (self.nU + 2))

            def n_up(self, c, j):
                nU = self.nU
                if j < 2 and isinstance(c, int) and c == 0:
                    return self.n0 + j
                if j >= 2:
                    cc, jj = c, j - 2
                else:
                    cc, jj = c - 1, j + nU - 2
                down = 0 if isinstance(cc, int) and cc == 0 else 2
                return self.start(cc) + jj + (down if jj >= nU - 2 else 0)

            def n_down(self, c):
                if isinstance(c, int) and c == self.n - 1:
                    return self.last_n - 2
                return self.start(c + 1) + self.nU - 2

            def down_slot(self, c, f):
                last = isinstance(c, int) and c == self.n - 1
                return self.W[:, f if last else 2 + f]

        def h_slot(F, par, f):
            return F.W[:, 4 + 2 * par + f]

        def feed_up_pe(pe, F, c, par, hooks={}):
            for j in range(F.nU):
                pe.wait_ge(unit_ready, F.n_up(c, j) + 1)
                for half in range(2):
                    g = 2 * j + half
                    f = j // 2 if F.gated else j
                    first = isinstance(c, int) and c == 0 and g < 2
                    if not first:
                        if F.gated:
                            if j % 2:
                                pe.wait_ge(*F.at("ge", 2 * CHUNK * c + 2 * f + half + 1))
                            else:
                                pe.wait_ge(*F.at("sq", 2 * CHUNK * c + 2 * f + half - 1))
                        else:
                            pe.wait_ge(*F.at("ue", 2 * F.nU * c + g - 1))
                    hooks.get(("before", g), lambda: None)()
                    tall_group(pe, F.Z, F.W[:, j % 2], KD, half, g % 2).then_inc(F.sem["up"], 1)
                    hooks.get(("after", g), lambda: None)()

        def feed_down_pe(pe, F, c, par, hooks={}):
            pe.wait_ge(unit_ready, F.n_down(c) + 2)
            pe.wait_ge(*F.at("lo", 2 * CHUNK * c + 2 * CHUNK))
            for t in range(NT):
                if not (isinstance(c, int) and c == 0 and t < 2):
                    pe.wait_ge(*F.at("de", NT * c + t - 1))
                for half in range(2):
                    for f in range(CHUNK):
                        H, slot = h_slot(F, par, f), F.down_slot(c, f)
                        last = products(ps[:, 2 + 2 * (t % 2) + half, :],
                                        lambda h: H[:, h, t * P:(t + 1) * P],
                                        lambda h: slot[:, h, half * HALF:(half + 1) * HALF],
                                        f == 0, f == CHUNK - 1)
                last.then_inc(F.sem["dn"], 1)
                hooks.get(t, lambda: None)()

        rtmp = at("rtmp", OFF_XN, [2, HALF])
        stmp = at("stmp", OFF_XN + 4 * KB, [2, HALF])

        def feed_evac_act(act, F, c, par, j):
            f = j // 2 if F.gated else j
            H = h_slot(F, par, f)
            for half in range(2):
                k = 2 * CHUNK * c + 2 * f + half
                first = isinstance(c, int) and c == 0 and f == 0
                dst = H[:, 0, half * HALF:(half + 1) * HALF]
                act.wait_ge(*F.at("up", 2 * F.nU * c + 2 * j + half + 1))
                if F.gated and j % 2 == 0:
                    if not first:
                        act.wait_ge(*F.at("sq", k - 1))
                    nc.scalar.activation(rtmp[:, half, :], ps[:, half, :], ACT.Silu).then_inc(F.sem["ge"], 1)
                elif F.gated:
                    act.wait_ge(*F.at("sq", k + 1))
                    nc.scalar.activation(dst, stmp[:, half, :], ACT.Copy).then_inc(F.sem["hi"], 1)
                else:
                    if not first:
                        act.wait_ge(*F.at("sq", k - 1))
                    nc.scalar.activation(rtmp[:, half, :], ps[:, half, :], ACT.Relu).then_inc(F.sem["ue"], 1)
                    act.wait_ge(*F.at("ue", k + 1))
                    nc.scalar.activation(dst, rtmp[:, half, :], ACT.Square).then_inc(F.sem["hi"], 1)

        def feed_evac_dve(dve, F, c, par, j):
            f = j // 2 if F.gated else j
            if F.gated and j % 2 == 0:
                return
            H = h_slot(F, par, f)
            for half in range(2):
                k = 2 * CHUNK * c + 2 * f + half
                hi, lo = (H[:, h, half * HALF:(half + 1) * HALF] for h in range(2))
                if F.gated:
                    dve.wait_ge(*F.at("ge", k + 1))
                    dve.wait_ge(*F.at("up", 2 * F.nU * c + 2 * j + half + 1))
                    if not (isinstance(c, int) and c == 0 and f == 0):
                        dve.wait_ge(*F.at("lo", k - 1))
                    nc.vector.tensor_tensor(stmp[:, half, :], rtmp[:, half, :], ps[:, half, :],
                                            ALU.mult).then_inc(F.sem["sq"], 1)
                else:
                    dve.wait_ge(*F.at("ue", k + 1))
                    if not (isinstance(c, int) and c == 0 and f == 0):
                        dve.wait_ge(*F.at("lo", k - 1))
                    nc.vector.tensor_tensor(stmp[:, half, :], rtmp[:, half, :], rtmp[:, half, :],
                                            ALU.mult).then_inc(F.sem["sq"], 1)
                dve.wait_ge(*F.at("sq", k + 1))
                dve.wait_ge(*F.at("hi", k + 1))
                nc.vector.tensor_tensor(lo, stmp[:, half, :], hi.bitcast(f32), ALU.subtract).then_inc(F.sem["lo"], 1)

        def conversions(F, c, j):
            todo = []
            first, last = (isinstance(c, int) and c == k for k in (0, F.n - 1))
            n = F.start(c) + j + (2 if j > F.nU - 2 and not first else 0)
            if j == F.nU - 2 and not first:
                for f in range(2):
                    free = None if isinstance(c, int) and c == 1 else F.at("dn", NT * (c - 1))
                    todo.append((n, F.W[:, 2 + f], free))
                    n = n + 1
            if not (last and j >= F.nU - 2):
                todo.append((n, F.W[:, j % 2], F.at("up", 2 * F.nU * c + 2 * j + 2)))
            elif last and j == F.nU - 1:
                for f in range(2):
                    todo.append((F.last_n - 2 + f, F.W[:, f], F.at("up", 2 * F.nU * F.n)))
            return todo

        def feed_act(act, F, c, par, c_par):
            for j in range(F.nU):
                feed_evac_act(act, F, c, par, j)
                for i, (n, slot, free) in enumerate(conversions(F, c, j)):
                    make_hi(act, n, slot, free, (parity_of(F, c_par, j) + i) % 2)

        def parity_of(F, c, j):
            if c == F.n - 1 and j == F.nU - 1:
                return F.last_n % 2
            return (F.start(c) + j + (2 if j > F.nU - 2 and c != 0 else 0)) % 2

        def feed_dve_up(dve, F, c, par, c_par):
            for j in range(F.nU):
                feed_evac_dve(dve, F, c, par, j)
                for i, (n, slot, free) in enumerate(conversions(F, c, j)):
                    odd = (parity_of(F, c_par, j) + i) % 2
                    make_lo(dve, n, slot, odd)

        def feed_dve_down(dve, F, c, hooks={}):
            for t in range(NT):
                dve.wait_ge(*F.at("dn", NT * c + t + 1))
                src = ps[:, 2 + 2 * (t % 2):4 + 2 * (t % 2), :].rearrange("p a b -> p (a b)")
                if isinstance(c, int) and c == 0 and not F.add_first:
                    dve.wait_ge(mid_out, F.acc_stored)
                    nc.vector.tensor_copy(acc[:, t, :], src).then_inc(F.sem["de"], 1)
                else:
                    if not (isinstance(c, int) and c == 0):
                        dve.wait_ge(*F.at("de", NT * c + t - NT + 1))
                    nc.vector.tensor_tensor(acc[:, t, :], acc[:, t, :], src, ALU.add).then_inc(F.sem["de"], 1)
                hooks.get(t, lambda: None)()

        def feed_steps(eng, F, up, down, first_hooks, last_hooks):
            n = F.n
            up(0, 0, 0, first_hooks)
            up(1, 1, 1, {})
            down(0, 0, {})
            pairs = (n - 3) // 2
            with eng.Fori(1, pairs + 1) as i:
                up(2 * i, 0, 2, {})
                down(2 * i - 1, 1, {})
                up(2 * i + 1, 1, 3, {})
                down(2 * i, 0, {})
            for c in range(2 * pairs + 2, n):
                up(c, c % 2, c, {})
                down(c - 1, (c - 1) % 2, {})
            down(n - 1, (n - 1) % 2, last_hooks)

        def feed_pe(pe, F, first_hooks, last_hooks):
            feed_steps(pe, F, lambda c, par, cp, hk: feed_up_pe(pe, F, c, par, hk),
                       lambda c, par, hk: feed_down_pe(pe, F, c, par, hk), first_hooks, last_hooks)

        def feed_on_act(act, F):
            feed_steps(act, F, lambda c, par, cp, hk: feed_act(act, F, c, par, cp),
                       lambda c, par, hk: None, {}, {})

        def feed_on_dve(dve, F, last_hooks):
            feed_steps(dve, F, lambda c, par, cp, hk: feed_dve_up(dve, F, c, par, cp),
                       lambda c, par, hk: feed_dve_down(dve, F, c, hk), {}, last_hooks)

        def first_hi(act, F):
            for u in range(2):
                make_hi(act, F.n0 + u, F.W[:, u], F.before, (F.n0 + u) % 2)

        def first_lo(dve, F):
            for u in range(2):
                make_lo(dve, F.n0 + u, F.W[:, u], (F.n0 + u) % 2)

        U_MLP = U_OUT + 8
        mlp = Feed(D_FF1 // P // CHUNK, False, A, B, U_MLP, (w_out.done, NT), True)
        U_PLE = mlp.last_n
        n_ple = Norm("g_ple", A, lambda t: mlp.at("de", NT * (mlp.n - 1) + t + 1))

        praw = at("praw", OFF_ROLD, [NT, 256])
        vtmp = at("vtmp", OFF_ROLD, [4, HALF])
        p_in = sem("p_in")
        pt_tr, pt_hi, pt_lo = sem("pt_tr"), sem("pt_hi"), sem("pt_lo")
        ple_done, ple_v, ple_s, ple_m, ple_res = (sem(f"ple_{s}") for s in ("done", "v", "s", "m", "res"))
        PLE_SLOTS = (2, 3, 0, 1)
        mlp_all = NT * mlp.n

        def ple_units():
            units = [(U_PLE + u, B[:, 4 + u], mlp.at("dn", mlp_all - NT)) for u in range(2)]
            for half in range(2):
                for u in range(4):
                    free = (mlp.at("dn", mlp_all - NT) if u < 2 else mlp.at("dn", mlp_all)) if half == 0 else (ple_done, NT)
                    units.append((U_PLE + 2 + 4 * half + u, B[:, PLE_SLOTS[u]], free))
            return units

        def ple_hi(act, a, b):
            for n, slot, free in ple_units()[a:b]:
                make_hi(act, n, slot, free, n % 2)

        def ple_lo(dve, a, b):
            for n, slot, free in ple_units()[a:b]:
                make_lo(dve, n, slot, n % 2)

        def ple_pe(pe, norm_next):
            pe.wait_ge(p_in, 16)
            for q in range(4):
                kp, half = divmod(q, 2)
                if q >= 2:
                    pe.wait_ge(pt_lo, q - 1)
                for t in range(4):
                    last = nc.tensor.transpose(ps[:, q % 2, t * P:(t + 1) * P],
                                               praw[:, 4 * half + t, kp * P:(kp + 1) * P], ident[:, :])
                last.then_inc(pt_tr, 1)
            for g in range(2 * NT):
                half, t = divmod(g, NT)
                if g == 0:
                    pe.wait_ge(pt_lo, 4)
                    pe.wait_ge(*n_ple.at("lo", 8))
                if g == 1:
                    pe.wait_ge(*mlp.at("de", mlp_all))
                if g == 4:
                    pe.wait_ge(*n_ple.at("lo", 16))
                if t == 0:
                    pe.wait_ge(unit_ready, U_PLE + 2 + 4 * (half + 1))
                if g >= 3:
                    pe.wait_ge(ple_res, g - 2)
                b0 = 2 * (g % 3)
                for k in range(KD):
                    slot = B[:, PLE_SLOTS[k // 2]]
                    products(ps[:, b0, :], lambda h: A[:, k, h, t * P:(t + 1) * P],
                             lambda h: slot[:, h, (k % 2) * HALF:(k % 2 + 1) * HALF], k == 0, k == KD - 1)
                for kp in range(2):
                    last = products(ps[:, b0 + 1, :], lambda h: B[:, 6 + kp, h, t * P:(t + 1) * P],
                                    lambda h: B[:, 4 + kp, h, half * HALF:(half + 1) * HALF], kp == 0, kp == 1)
                last.then_inc(ple_done, 1)
                if g == 0:
                    norm_pe(pe, n_ple, 1)
                if g == NT + 6:
                    norm_pe(pe, norm_next, 0)

        def ple_act_p(act):
            for q in range(4):
                kp, half = divmod(q, 2)
                if q == 0:
                    act.wait_ge(*mlp.at("dn", mlp_all))
                act.wait_ge(pt_tr, q + 1)
                nc.scalar.activation(B[:, 6 + kp, 0, half * HALF:(half + 1) * HALF], ps[:, q % 2, :],
                                     ACT.Copy).then_inc(pt_hi, 1)

        def ple_dve_p(dve):
            for q in range(4):
                kp, half = divmod(q, 2)
                dst = B[:, 6 + kp, :, half * HALF:(half + 1) * HALF]
                dve.wait_ge(pt_hi, q + 1)
                nc.vector.tensor_tensor(dst[:, 1, :], ps[:, q % 2, :], dst[:, 0, :].bitcast(f32),
                                        ALU.subtract).then_inc(pt_lo, 1)

        def ple_act(act, g0, g1):
            for g in range(g0, g1):
                act.wait_ge(ple_v, g + 1)
                nc.scalar.activation(vtmp[:, g % 2, :], vtmp[:, g % 2, :], ACT.Sigmoid).then_inc(ple_s, 1)

        def ple_dve(dve, hooks):
            def bias(g):
                half, t = divmod(g, NT)
                dve.wait_ge(ple_done, g + 1)
                if g >= 2:
                    dve.wait_ge(ple_m, g - 1)
                nc.vector.tensor_tensor(vtmp[:, g % 2, :], ps[:, 2 * (g % 3), :],
                                        gb[:, 0, half * HALF:(half + 1) * HALF], ALU.add).then_inc(ple_v, 1)

            late = (NT - 1, NT + 3, NT + 6)
            dve.wait_ge(gb_in[0], 16)
            dve.wait_ge(pt_tr, 4)
            bias(0)
            for g in range(2 * NT):
                half, t = divmod(g, NT)
                if g + 1 < 2 * NT and g not in late:
                    bias(g + 1)
                dve.wait_ge(ple_s, g + 1)
                if g >= 2:
                    dve.wait_ge(ple_res, g - 1)
                nc.vector.tensor_tensor(vtmp[:, 2 + g % 2, :], vtmp[:, g % 2, :], ps[:, 2 * (g % 3) + 1, :],
                                        ALU.mult).then_inc(ple_m, 1)
                dve.wait_ge(ple_m, g + 1)
                nc.vector.tensor_tensor(acc[:, t, half * HALF:(half + 1) * HALF],
                                        acc[:, t, half * HALF:(half + 1) * HALF], vtmp[:, 2 + g % 2, :],
                                        ALU.add).then_inc(ple_res, 1)
                hooks.get(g - NT, lambda: None)()
                if g == NT - 1:
                    ple_lo(dve, 6, 10)
                if g in late:
                    bias(g + 1)

        U_FFN1 = U_PLE + 10
        n_fin = Norm("g_ffn1", A, lambda t: (ple_res, NT + t + 1), post=1)
        n_fin.gb_count = 1
        ffn1 = Feed(D_FF2 // P // CHUNK, True, A, B, U_FFN1, (ple_done, 2 * NT), False)
        n_mix2 = Norm("g_mix2", A, lambda t: ffn1.at("de", NT * (ffn1.n - 1) + t + 1), post=0, residual=True)
        n_mix2.gb_count, n_mix2.old_count, n_mix2.factor, n_mix2.kept = 2, 0, 0.5, x_mid[1]
        U_QK = ffn1.last_n
        mid_stored = [16 * NT * (k + 1) for k in range(3)]

        U_V = U_QK + 8
        U_U = U_V + 4
        U_GLU = U_U + 4
        U_MIXO = U_GLU + 2
        U_FFN2 = U_MIXO + 8
        qk_done, qk_out, v_done, v_out, u_done, u_out = (sem(s) for s in (
            "qk_done", "qk_out", "v_done", "v_out", "u_done", "u_out"))
        QK = at("qk", OFF_ACC, [8, S])
        V = at("v", OFF_XN, [NT, HALF])
        U = at("u", OFF_GB, [GT, HALF])
        SLOTS4 = (2, 3, 0, 1)
        f1_all = NT * ffn1.n

        def qk_unit(m):
            free = (ffn1.at("dn", f1_all - NT) if m < 2 else ffn1.at("dn", f1_all)) if m < 4 \
                else (qk_done, 2 * (m - 4) + 2)
            return U_QK + m, B[:, SLOTS4[m % 4]], free

        def v_unit(u):
            return U_V + u, B[:, 4 + u], ffn1.at("dn", f1_all)

        def u_unit(u):
            return U_U + u, B[:, SLOTS4[u]], (qk_done, 2 * (4 + u) + 2)

        def hi_of(act, unit):
            n, slot, free = unit
            make_hi(act, n, slot, free, n % 2)

        def lo_of(dve, unit):
            make_lo(dve, unit[0], unit[1], unit[0] % 2)

        def proj_pe(pe):
            for m in range(8):
                pe.wait_ge(unit_ready, U_QK + m + 1)
                for half in range(2):
                    g = 2 * m + half
                    if m == 0:
                        pe.wait_ge(*n_mix2.at("lo", 8 * half + 8))
                        if half == 0:
                            pe.wait_ge(*ffn1.at("de", f1_all))
                    if g >= 4:
                        pe.wait_ge(qk_out, g - 3)
                    tall_group(pe, A, B[:, SLOTS4[m % 4]], KD, half, g % 4).then_inc(qk_done, 1)
                    if g == 0:
                        norm_pe(pe, n_mix2, 1)
            pe.wait_ge(unit_ready, U_V + 4)
            for t in range(NT):
                if t >= 2:
                    pe.wait_ge(v_out, t - 1)
                for k in range(KD):
                    slot = B[:, 4 + k // 2]
                    last = products(ps[:, 4 + t % 2, :], lambda h: A[:, k, h, t * P:(t + 1) * P],
                                    lambda h: slot[:, h, (k % 2) * HALF:(k % 2 + 1) * HALF], k == 0, k == KD - 1)
                last.then_inc(v_done, 1)
                if t == 5:
                    pe.wait_ge(g_ready, 1)
                    for q in range(7):
                        last = nc.tensor.transpose(ps[:, 6, q * 32:(q + 1) * 32], QG[:, q, :], ident[0:32, 0:32])
                    last.then_inc(g_tr, 1)
            pe.wait_ge(unit_ready, U_U + 4)
            for t in range(GT):
                pe.wait_ge(*((u_out, t - 1) if t >= 2 else (v_out, NT - 1 + t)))
                for k in range(KD):
                    slot = B[:, SLOTS4[k // 2]]
                    last = products(ps[:, 4 + t % 2, :],
                                    lambda h: A[:, k, h, :].rearrange("p (c t) -> p t c", t=GT)[:, t, :],
                                    lambda h: slot[:, h, (k % 2) * HALF:(k % 2 + 1) * HALF], k == 0, k == KD - 1)
                last.then_inc(u_done, 1)

        def proj_act(act):
            for m in range(8):
                for half in range(2):
                    if m == 0:
                        act.wait_ge(mid_out, mid_stored[1])
                        act.wait_ge(*n_mix2.at("xn", NT))
                    act.wait_ge(qk_done, 2 * m + half + 1)
                    nc.scalar.activation(QK[:, m, half * HALF:(half + 1) * HALF], ps[:, (2 * m + half) % 4, :],
                                         ACT.Copy, scale=HEAD_DIM ** -0.5 if m < 4 else 1.0).then_inc(qk_out, 1)
                hi_of(act, qk_unit(m + 4) if m < 4 else v_unit(m - 4))
            for u in range(4):
                hi_of(act, u_unit(u))

        def proj_dve(dve):
            for m in range(4):
                lo_of(dve, qk_unit(m + 4))
            for u in range(4):
                lo_of(dve, v_unit(u))
            for u in range(4):
                lo_of(dve, u_unit(u))
            ssm_params_dve(dve)
            for t in range(NT):
                dve.wait_ge(v_done, t + 1)
                nc.vector.tensor_copy(V[:, t, :], ps[:, 4 + t % 2, :]).then_inc(v_out, 1)
            ssm_powers_dve(dve)
            for t in range(GT):
                dve.wait_ge(u_done, t + 1)
                nc.vector.tensor_copy(U[:, t, :], ps[:, 4 + t % 2, :]).then_inc(u_out, 1)

        params_g = at("params_g", OFF_GB, [2 * P + 1])
        g_tmp = at("g_tmp", OFF_GB + 2 * KB, [14, P])
        qg = at("qg", OFF_GB + 10 * KB, [7, P])
        G32 = slice(0, N_GROUPS)
        QG = qg[G32]
        st = at("st", OFF_ID + 2048, [26, N_GROUPS])
        (AR, SAI, UR, UI, RHO, FR, SFI, A2R, SA2I, A4R, SA4I) = (st[:, i, :] for i in range(11))
        WR = [st[:, 11 + i, :] for i in range(7)]
        NWI = [st[:, 18 + i, :] for i in range(7)]
        sgn = col[:, COLS["sgn"]:COLS["sgn"] + 1]
        nsgn = small[:, 100:101]
        g_in, g_ready, g_tr = sem("g_in"), sem("g_ready"), sem("g_tr")
        g_d, g_a = sem("g_d"), sem("g_a")
        TWO_PI = 2 * math.pi
        C1 = 6.28125
        C2 = 0.0019340515136718750
        C3 = TWO_PI - C1 - C2
        ROUND = 1.5 * 2 ** 23

        are, aim, ldt = params_g[G32, 0:P], params_g[G32, P:2 * P], params_g[G32, 2 * P:2 * P + 1]
        gt = [g_tmp[G32, i, :] for i in range(14)]
        dt_ = g_tmp[G32, 13, 0:1]
        wr, wi, th, kk_, r_, sn, s2_, cm1, e1, inv, x0, x1 = gt[:12]

        def ssm_params_act(act):
            act.wait_ge(g_in, 16)
            nc.scalar.activation(dt_, ldt, ACT.Exp).then_inc(g_a, 1)
            act.wait_ge(g_d, 1)
            nc.scalar.activation(th, wr, ACT.Tanh, scale=0.5).then_inc(g_a, 1)
            nc.scalar.activation(QG[:, 4, :], wr, ACT.Exp, scale=float(GT)).then_inc(g_a, 1)
            act.wait_ge(g_d, 2)
            nc.scalar.activation(QG[:, 3, :], r_, ACT.Sin).then_inc(g_a, 1)
            nc.scalar.activation(s2_, r_, ACT.Sin, scale=0.5).then_inc(g_a, 1)

        def ssm_params_dve(dve):
            ts, tt, stt = nc.vector.tensor_scalar, nc.vector.tensor_tensor, nc.vector.scalar_tensor_tensor
            link = lambda ins: link_dve(dve, ins)
            dve.wait_ge(g_a, 1)
            link(ts(wi, aim, dt_, None, ALU.mult))
            ts(wr, are, dt_, None, ALU.mult).then_inc(g_d, 1)
            link(ts(kk_, wi, 1.0 / TWO_PI, ROUND, ALU.mult, ALU.add))
            link(ts(kk_, kk_, -ROUND, None, ALU.add))
            link(stt(out=r_, in0=kk_, scalar=-C1, in1=wi, op0=ALU.mult, op1=ALU.add))
            link(stt(out=r_, in0=kk_, scalar=-C2, in1=r_, op0=ALU.mult, op1=ALU.add))
            link(stt(out=r_, in0=kk_, scalar=-C3, in1=r_, op0=ALU.mult, op1=ALU.add))
            ts(r_, r_, 3.1415925, -3.1415925, ALU.min, ALU.max).then_inc(g_d, 1)
            dve.wait_ge(g_a, 3)
            link(ts(x0, th, -1.0, 1.0, ALU.mult, ALU.add))
            link(nc.vector.reciprocal(x0, x0))
            link(stt(out=e1, in0=th, scalar=2.0, in1=x0, op0=ALU.mult, op1=ALU.mult))
            dve.wait_ge(g_a, 5)
            link(stt(out=cm1, in0=s2_, scalar=-2.0, in1=s2_, op0=ALU.mult, op1=ALU.mult))
            link(ts(QG[:, 2, :], cm1, 1.0, None, ALU.add))
            link(ts(x0, e1, 1.0, None, ALU.add))
            link(tt(QG[:, 0, :], x0, QG[:, 2, :], ALU.mult))
            link(tt(QG[:, 1, :], x0, QG[:, 3, :], ALU.mult))
            link(tt(x1, e1, QG[:, 2, :], ALU.mult))
            link(tt(x1, x1, cm1, ALU.add))
            link(tt(x0, are, are, ALU.mult))
            link(tt(inv, aim, aim, ALU.mult))
            link(tt(inv, inv, x0, ALU.add))
            link(nc.vector.reciprocal(inv, inv))
            link(tt(x0, QG[:, 1, :], aim, ALU.mult))
            link(tt(e1, x1, are, ALU.mult))
            link(tt(e1, e1, x0, ALU.add))
            link(tt(QG[:, 5, :], e1, inv, ALU.mult))
            link(tt(x0, QG[:, 1, :], are, ALU.mult))
            link(tt(e1, x1, aim, ALU.mult))
            link(tt(e1, x0, e1, ALU.subtract))
            tt(QG[:, 6, :], e1, inv, ALU.mult).then_inc(g_ready, 1)

        def ssm_powers_dve(dve):
            ts, tt, stt = nc.vector.tensor_scalar, nc.vector.tensor_tensor, nc.vector.scalar_tensor_tensor
            link = lambda ins: link_dve(dve, ins)
            dve.wait_ge(g_tr, 1)
            link(nc.vector.tensor_copy(st[:, 0:7, :].rearrange("p a b -> p (a b)"), ps[:, 6, 0:7 * N_GROUPS]))
            link(ts(nsgn, sgn, -1.0, None, ALU.mult))
            t0, t1 = pw_tmp[:, 0:N_GROUPS], pw_tmp[:, N_GROUPS:2 * N_GROUPS]
            ar_, ai_ = AR, SAI
            for R2, I2 in ((A2R, SA2I), (A4R, SA4I)):
                square(link, R2, I2, ar_, ai_, t0, t1)
                ar_, ai_ = R2, I2
            for x_ in (SAI, SA2I, SA4I, SFI):
                link(ts(x_, x_, sgn, None, ALU.mult))
            ur, ui = UR, UI
            for _ in range(2):
                square(link, ur, ui, ur, ui, t0, t1)
            square(link, WR[0], NWI[0], ur, ui, t0, t1)
            for m in range(1, 7):
                square(link, WR[m], NWI[m], WR[m - 1], NWI[m - 1], t0, t1)
            link(ts(st[:, 18:25, :], st[:, 18:25, :], -1.0, None, ALU.mult))
            nc.vector.tensor_copy(pw_tmp[:, 0:1], pw_tmp[:, 1:2]).then_inc(pw_ready, 1)

        def square(link, R2, I2, R1, I1, t0, t1):
            link(nc.vector.tensor_tensor(t0, R1, R1, ALU.mult))
            link(nc.vector.tensor_tensor(t1, I1, I1, ALU.mult))
            link(nc.vector.scalar_tensor_tensor(out=I2, in0=R1, scalar=2.0, in1=I1, op0=ALU.mult, op1=ALU.mult))
            link(nc.vector.tensor_tensor(R2, t0, t1, ALU.subtract))

        pw_tmp = at("pw_tmp", OFF_ID + 1024 + 256 + 64 + 128, [2 * N_GROUPS])
        pw_ready = sem("pw_ready")

        NB4, GB = 4, N_GROUPS // 4
        bufs_ssm = []
        for par in range(2):
            o = OFF_A + par * 29 * KB
            bufs_ssm.append(dict(
                VV=at(f"vv{par}", o, [GB, 9 * GROUP]), VS=at(f"vs{par}", o + 4608, [GB, 9 * GROUP]),
                Z=at(f"z{par}", o + 9216, [GB, GT * GROUP]), ZS=at(f"zs{par}", o + 13312, [GB, GT * GROUP]),
                T=at(f"toep{par}", o + 17408, [GB, P]), CS=at(f"cs{par}", o + 21504, [GB, P]),
                SN=at(f"sn{par}", o + 25600, [GB, P])))
        ssm_in = at("ssm_in", OFF_B, [4 * N_GROUPS * GROUP + N_GROUPS])
        BA, BB, CA, CB = (ssm_in[:, i * 512:(i + 1) * 512].rearrange("p (g c) -> p g c", g=N_GROUPS) for i in range(4))
        dT = ssm_in[0:GROUP, 2048:2048 + N_GROUPS]
        tmp_v = at("tmp_v", OFF_B + 16 * KB, [4, 512])
        tmp_p = at("tmp_p", OFF_B + 24 * KB, [4, 512])
        o = OFF_B + 32 * KB
        ztb = at("ztb", o, [2, 3, 512])
        kkb = at("kkb", o + 12 * KB, [GB, P])
        nbb = at("nbb", o + 16 * KB, [GB, GROUP])
        kd = at("kd", o + 16 * KB + 512, [GB, GROUP])
        m1b = at("m1b", o + 17 * KB, [512])
        m2b = at("m2b", o + 19 * KB, [512])
        yb = at("yb", o + 21 * KB, [4, P])
        ob = at("ob", o + 23 * KB, [2, 4, P + 1])
        ub = at("ub", OFF_B + 9 * KB, [2, 4, GT * GROUP])
        ub_made = sem("ub_made")
        s_in = sem("s_in")
        zb_ready, tab_ready, v_ready, nb_ready = sem("zb_ready"), sem("tab_ready"), sem("v_ready"), sem("nb_ready")
        t_zero, kk_done, kk_out, kk_d, t_in = (sem(s) for s in ("t_zero", "kk_done", "kk_out", "kk_d", "t_in"))
        s5_tr, s5_cp, s5_s, s5_o, s5_y, s5_g = (sem(s) for s in ("s5_tr", "s5_cp", "s5_s", "s5_o", "s5_y", "s5_g"))
        pool_chain = sem("pool_chain")
        chained["pool"] = 0

        def link_pool(pool, ins):
            chained["pool"] += 1
            ins.then_inc(pool_chain, 1)
            pool.wait_ge(pool_chain, chained["pool"])

        def cmul(eng, link, dst, dsts, src, srcs, pr, spi, tmp, last=None):
            m = src.shape[2]
            t = [tmp[:, i, 0:GB * m].rearrange("p (g m) -> p g m", g=GB) for i in range(4)]
            pr = pr.unsqueeze(2).to_broadcast([P, GB, m])
            spi = spi.unsqueeze(2).to_broadcast([P, GB, m])
            eng.tensor_tensor(t[0], src, pr, ALU.mult)
            eng.tensor_tensor(t[1], srcs, spi, ALU.mult)
            eng.tensor_tensor(t[2], srcs, pr, ALU.mult)
            link(eng.tensor_tensor(t[3], src, spi, ALU.mult))
            eng.tensor_tensor(dst, t[0], t[1], ALU.add)
            ins = eng.tensor_tensor(dsts, t[2], t[3], ALU.subtract)
            if last is None:
                link(ins)
            else:
                ins.then_inc(last, 1)

        def ssm_batch_dve(dve, b):
            bf = bufs_ssm[b % 2]
            gs = slice(GB * b, GB * b + GB)
            link = lambda ins: link_dve(dve, ins)
            if b == 0:
                dve.wait_ge(s_in, 16)
                dve.wait_ge(u_done, GT)
            elif b >= 2:
                dve.wait_ge(s5_y, 2 * (b - 1))
            Z, ZS, CS, SN = (bf[n] for n in ("Z", "ZS", "CS", "SN"))
            cut = lambda X, a, m: X[:, :, a * GROUP:(a + m) * GROUP]
            cmul(nc.vector, link, cut(Z, 7, 1), cut(ZS, 7, 1), BA[:, gs, :], BB[:, gs, :], FR[:, gs], SFI[:, gs], tmp_v)
            if b:
                dve.wait_ge(kk_done, 2 * b)
            nc.vector.tensor_scalar(nbb[:, :, :], cut(Z, 7, 1), nsgn, None, ALU.mult).then_inc(nb_ready, 1)
            cmul(nc.vector, link, cut(Z, 6, 1), cut(ZS, 6, 1), cut(Z, 7, 1), cut(ZS, 7, 1), AR[:, gs], SAI[:, gs], tmp_v)
            cmul(nc.vector, link, cut(Z, 4, 2), cut(ZS, 4, 2), cut(Z, 6, 2), cut(ZS, 6, 2), A2R[:, gs], SA2I[:, gs], tmp_v)
            cmul(nc.vector, link, cut(Z, 0, 4), cut(ZS, 0, 4), cut(Z, 4, 4), cut(ZS, 4, 4), A4R[:, gs], SA4I[:, gs],
                 tmp_v, last=zb_ready)
            nc.vector.memset(CS[:, :, 0:1], 1.0)
            link(nc.vector.memset(SN[:, :, 0:1], 0.0))
            for k in range(7):
                m = 1 << k
                cmul(nc.vector, link, CS[:, :, m:2 * m], SN[:, :, m:2 * m], CS[:, :, 0:m], SN[:, :, 0:m],
                     WR[k][:, gs], NWI[k][:, gs], tmp_v)
            if b == 0:
                dve.wait_ge(ident_made, 2)
            link(nc.vector.tensor_tensor(kd[0:GROUP], ident[0:GROUP, 0:GROUP].unsqueeze(1).to_broadcast([GROUP, GB, GROUP]),
                                         dT[:, gs].unsqueeze(2).to_broadcast([GROUP, GB, GROUP]), ALU.mult))
            dve.wait_ge(kk_out, 2 * b + 2)
            nc.vector.tensor_tensor(kkb[0:GROUP, :, 0:GROUP], kkb[0:GROUP, :, 0:GROUP], kd[0:GROUP],
                                    ALU.add).then_inc(kk_d, 1)

        def ssm_batch_pool(pool, b):
            bf = bufs_ssm[b % 2]
            gs = slice(GB * b, GB * b + GB)
            link = lambda ins: link_pool(pool, ins)
            if b == 0:
                pool.wait_ge(u_done, GT)
                pool.wait_ge(pw_ready, 1)
                pool.dma_start(ssm_in[:, :], ssm_bc).then_inc(s_in, 16)
                pool.wait_ge(s_in, 16)
            elif b >= 2:
                pool.wait_ge(s5_y, 2 * (b - 1))
            VV, VS, T = (bf[n] for n in ("VV", "VS", "T"))
            nc.gpsimd.memset(T[:, :, :], 0.0).then_inc(t_zero, 1)
            cut = lambda X, a, m: X[:, :, a * GROUP:(a + m) * GROUP]
            nc.gpsimd.tensor_copy(cut(VV, 0, 1), CA[:, gs, :])
            link(nc.gpsimd.tensor_copy(cut(VS, 0, 1), CB[:, gs, :]))
            for a, m, src, pr, pi in ((1, 1, 0, AR, SAI), (2, 2, 0, A2R, SA2I), (4, 4, 0, A4R, SA4I), (8, 1, 7, AR, SAI)):
                cmul(nc.gpsimd, link, cut(VV, a, m), cut(VS, a, m), cut(VV, src, m), cut(VS, src, m),
                     pr[:, gs], pi[:, gs], tmp_p, last=v_ready if a == 8 else None)
            pool.wait_ge(kk_d, b + 1)
            pool.wait_ge(t_zero, b + 1)
            for t in range(GT):
                w = (GT - t) * GROUP
                pool.dma_start(T[t * GROUP:(t + 1) * GROUP, :, t * GROUP:P],
                               kkb[0:GROUP, :, 0:w]).then_inc(t_in, 16)

        def ssm_pe(pe):
            def kernels(b):
                bf = bufs_ssm[b % 2]
                pe.wait_ge(nb_ready, b + 1)
                pe.wait_ge(v_ready, b + 1)
                for half in range(2):
                    if b:
                        pe.wait_ge(kk_out, 2 * b - 1 + half)
                    for i in range(4):
                        last = nc.tensor.matmul(ps[0:GROUP, 6 + half, i * P:(i + 1) * P], nbb[:, 4 * half + i, :],
                                                bf["VV"][:, 4 * half + i, 0:P], start=True, stop=True)
                    last.then_inc(kk_done, 1)

            def transposes(q):
                b, half = divmod(q, 2)
                bf = bufs_ssm[b % 2]
                pe.wait_ge(zb_ready, b + 1)
                if q:
                    pe.wait_ge(s5_cp, 3 * q)
                pe.wait_ge(ub_made, q + 1)
                for k, src in enumerate((bf["Z"], bf["ZS"], None)):
                    for i in range(4):
                        g = 4 * half + i
                        x_ = ub[:, q % 2, i, :] if src is None else src[:, g, :]
                        last = nc.tensor.transpose(ps[:, k, i * P:(i + 1) * P], x_, ident[:, :])
                    last.then_inc(s5_tr, 1)

            for b in range(NB4):
                kernels(b)
                for half in range(2):
                    q = 2 * b + half
                    transposes(q)
                    bf = bufs_ssm[b % 2]
                    zt = ztb[:, q % 2]
                    if q:
                        pe.wait_ge(s5_o, q)
                    pe.wait_ge(s5_cp, 3 * q + 3)
                    for k in range(2):
                        for i in range(4):
                            last = nc.tensor.matmul(ps[:, 3 + k, i * P:(i + 1) * P], zt[:, k, i * P:(i + 1) * P],
                                                    zt[:, 2, i * P:(i + 1) * P], start=True, stop=True)
                    last.then_inc(s5_s, 1)
                    pe.wait_ge(t_in, 16 * GT * (b + 1))
                    pe.wait_ge(s5_o, q + 1)
                    if q:
                        pe.wait_ge(s5_g, q)
                    for i in range(4):
                        g = 4 * half + i
                        dst = ps[:, 5, i * P:(i + 1) * P]
                        nc.tensor.matmul(dst, zt[:, 2, i * P:(i + 1) * P], bf["T"][:, g, :], start=True, stop=False)
                        nc.tensor.matmul(dst, ob[:, 0, i, 0:P], bf["VV"][:, g, GROUP:9 * GROUP], start=False, stop=False)
                        last = nc.tensor.matmul(dst, ob[:, 1, i, 0:P], bf["VS"][:, g, GROUP:9 * GROUP], start=False, stop=True)
                    last.then_inc(s5_y, 1)

        def ssm_act(act):
            def kernels(b):
                for half in range(2):
                    act.wait_ge(kk_done, 2 * b + half + 1)
                    if b:
                        act.wait_ge(t_in, 16 * GT * b)
                    nc.scalar.activation(kkb[0:GROUP, 4 * half:4 * half + 4, :].rearrange("p a b -> p (a b)"),
                                         ps[0:GROUP, 6 + half, :], ACT.Copy).then_inc(kk_out, 1)

            def inputs(q):
                if q >= 2:
                    act.wait_ge(s5_tr, 3 * q - 3)
                nc.scalar.activation(ub[:, q % 2, :, :].rearrange("p g (t c) -> p g t c", t=GT), group_columns(q),
                                     ACT.Copy).then_inc(ub_made, 1)

            def group_columns(q):
                return U[:, :, 64 * q:64 * q + 64].rearrange("p t (g c) -> p g t c", g=4)

            act.wait_ge(u_out, GT)
            inputs(0)
            for b in range(NB4):
                kernels(b)
                for half in range(2):
                    q = 2 * b + half
                    if q + 1 < 2 * NB4:
                        inputs(q + 1)
                    for k in range(3):
                        act.wait_ge(s5_tr, 3 * q + k + 1)
                        if q >= 2:
                            act.wait_ge(s5_y, q - 1)
                        nc.scalar.activation(ztb[:, q % 2, k, :], ps[:, k, :], ACT.Copy).then_inc(s5_cp, 1)
                    act.wait_ge(s5_y, q + 1)
                    nc.scalar.activation(group_columns(q),
                                         ps[:, 5, :].rearrange("p (g t c) -> p g t c", g=4, t=GT),
                                         ACT.Gelu_apprx_tanh).then_inc(s5_g, 1)

        def ssm_dve(dve):
            link = lambda ins: link_dve(dve, ins)
            ssm_batch_dve(dve, 0)
            for b in range(NB4):
                bf = bufs_ssm[b % 2]
                for half in range(2):
                    q = 2 * b + half
                    hs = slice(4 * half, 4 * half + 4)
                    cs, sn_ = bf["CS"][:, hs, :], bf["SN"][:, hs, :]
                    v = lambda X: X[:, :].rearrange("p (a b) -> p a b", a=4)
                    pv = lambda k: ps[:, k, :].rearrange("p (a b) -> p a b", a=4)
                    if q == 0:
                        link(nc.vector.memset(ob[:, :, :, 0:1], 0.0))
                    dve.wait_ge(s5_s, q + 1)
                    nc.vector.tensor_tensor(v(m1b), pv(3), cs, ALU.mult)
                    link(nc.vector.scalar_tensor_tensor(out=v(m2b), in0=pv(4), scalar=nsgn, in1=sn_, op0=ALU.mult,
                                                        op1=ALU.mult))
                    link(nc.vector.tensor_tensor(m1b[:, :], m1b[:, :], m2b[:, :], ALU.add))
                    for i in range(4):
                        g = 4 * q + i
                        ins = nc.vector.tensor_tensor_scan(yb[:, i, :], RHO[:, g:g + 1].to_broadcast([P, P]),
                                                           m1b[:, i * P:(i + 1) * P], 0.0, ALU.mult, ALU.add)
                    link(ins)
                    if q:
                        dve.wait_ge(s5_y, q)
                    nc.vector.scalar_tensor_tensor(out=ob[:, 0, :, 1:], in0=yb[:, :, :], scalar=nsgn, in1=cs,
                                                   op0=ALU.mult, op1=ALU.mult)
                    nc.vector.scalar_tensor_tensor(out=ob[:, 1, :, 1:], in0=yb[:, :, :], scalar=-1.0, in1=sn_,
                                                   op0=ALU.mult, op1=ALU.mult).then_inc(s5_o, 1)
                if b + 1 < NB4:
                    ssm_batch_dve(dve, b + 1)

        yf = at("yf", OFF_B, [4, S])
        YH = A[:, 4:8]
        sg = at("sg", OFF_B + 16 * KB, [2, HALF])
        pr_ = at("pr", OFF_B + 20 * KB, [2, HALF])
        yt_tr, yt_f, yt_hi, yt_lo = (sem(s) for s in ("yt_tr", "yt_f", "yt_hi", "yt_lo"))
        gl_done, gl_s, gl_p, gl_hi, gl_lo = (sem(s) for s in ("gl_done", "gl_s", "gl_p", "gl_hi", "gl_lo"))

        def glu_unit(u):
            return U_GLU + u, A[:, 2 + u], (s5_g, 8)

        def eighths(X, half):
            return X.rearrange("p (c t) -> p t c", t=GT)[:, 4 * half:4 * half + 4, :]

        def glu_pe(pe):
            pe.wait_ge(s5_g, 8)
            for q in range(8):
                j, half = divmod(q, 2)
                if q >= 2:
                    pe.wait_ge(yt_f, q - 1)
                for t in range(4):
                    tt_ = 4 * half + t
                    last = nc.tensor.transpose(ps[:, q % 2, t * P:(t + 1) * P],
                                               U[:, tt_, j * P:(j + 1) * P], ident[:, :])
                last.then_inc(yt_tr, 1)
            pe.wait_ge(yt_lo, 8)
            pe.wait_ge(unit_ready, U_GLU + 2)
            for g in range(8):
                j, half = divmod(g, 2)
                if g >= 4:
                    pe.wait_ge(gl_s, g - 3)
                slot = A[:, 2 + j // 2]
                for k in range(4):
                    c0 = (j % 2) * HALF + k * P
                    last = products(ps[:, 2 + g % 4, :], lambda h: slot[:, h, c0:c0 + P],
                                    lambda h: YH[:, k, h, half * HALF:(half + 1) * HALF], k == 0, k == 3)
                last.then_inc(gl_done, 1)

        def glu_act(act):
            for u in range(2):
                hi_of(act, glu_unit(u))
            for q in range(8):
                j, half = divmod(q, 2)
                act.wait_ge(yt_tr, q + 1)
                nc.scalar.activation(eighths(yf[:, j, :], half), ps[:, q % 2, :].rearrange("p (t c) -> p t c", t=4),
                                     ACT.Copy).then_inc(yt_f, 1)
                if half:
                    act.wait_ge(yt_f, q + 1)
                    nc.scalar.activation(YH[:, j, 0, :], yf[:, j, :], ACT.Copy).then_inc(yt_hi, 1)
            for g in range(8):
                j, half = divmod(g, 2)
                act.wait_ge(gl_done, g + 1)
                if g >= 2:
                    act.wait_ge(gl_p, g - 1)
                nc.scalar.activation(sg[:, g % 2, :], ps[:, 2 + g % 4, :], ACT.Sigmoid,
                                     bias=c_("b_glu", j)).then_inc(gl_s, 1)
                act.wait_ge(gl_p, g + 1)
                nc.scalar.activation(B[:, 4 + j, 0, half * HALF:(half + 1) * HALF], pr_[:, g % 2, :],
                                     ACT.Copy).then_inc(gl_hi, 1)

        def glu_dve(dve):
            for u in range(2):
                lo_of(dve, glu_unit(u))
            for j in range(4):
                dve.wait_ge(yt_hi, j + 1)
                nc.vector.tensor_tensor(YH[:, j, 1, :], yf[:, j, :], YH[:, j, 0, :].bitcast(f32),
                                        ALU.subtract).then_inc(yt_lo, 2)
            for g in range(8):
                j, half = divmod(g, 2)
                cut = slice(half * HALF, (half + 1) * HALF)
                dve.wait_ge(gl_s, g + 1)
                if g >= 2:
                    dve.wait_ge(gl_lo, g - 1)
                nc.vector.tensor_tensor(pr_[:, g % 2, :], yf[:, j, cut], sg[:, g % 2, :], ALU.mult).then_inc(gl_p, 1)
                dve.wait_ge(gl_hi, g + 1)
                nc.vector.tensor_tensor(B[:, 4 + j, 1, cut], pr_[:, g % 2, :], B[:, 4 + j, 0, cut].bitcast(f32),
                                        ALU.subtract).then_inc(gl_lo, 1)

        dist = at("dist", OFF_A, [S])
        lmul = at("lmul", OFF_A + 4 * KB, [S])
        ib = at("ib", OFF_A + 8 * KB, [S], i32)
        ibf = at("ibf", OFF_A + 8 * KB, [S])
        xb_i = at("xb_i", OFF_A + 12 * KB, [S], i32)
        xb_f = at("xb_f", OFF_A + 12 * KB, [S])
        bias_h = at("bias_h", OFF_A + 8 * KB, [2, S])
        sco = at("sco", OFF_A + 16 * KB, [2, S])
        prob = at("prob", OFF_A + 24 * KB, [2, S])
        probT = at("probT", OFF_A + 32 * KB, [2, NT, P])
        O = at("att_o", OFF_A + 40 * KB, [NT, HALF])
        stats = at("stats", OFF_ID + 2048, [4, N_HEADS * NT])
        mx_, nm_, den_, rd_ = (stats[:, i, :] for i in range(4))
        io_done = sem("io_done")
        at_s, at_m, at_n, at_e, at_tr, at_pt, at_pv, at_r, at_o = (sem(f"at_{s}") for s in (
            "s", "m", "n", "e", "tr", "pt", "pv", "r", "o"))
        ot_tr, ot_hi, ot_lo = sem("ot_tr"), sem("ot_hi"), sem("ot_lo")
        NA = N_HEADS * NT

        def bias_dve(dve):
            ts, tt, stt = nc.vector.tensor_scalar, nc.vector.tensor_tensor, nc.vector.scalar_tensor_tensor
            link = lambda ins: link_dve(dve, ins)
            dve.wait_ge(io_done, 1)
            d, L = dist[:, :], lmul[:, :]
            link(nc.vector.tensor_copy(d, ib[:, :]))
            link(ts(xb_i[:, :], ib[:, :], 3, None, ALU.bitwise_and))
            link(ts(L, xb_i[:, :], 0.0, None, ALU.is_equal))
            link(stt(out=L, in0=d, scalar=512.0, in1=L, op0=ALU.is_le, op1=ALU.mult))
            link(stt(out=L, in0=d, scalar=128.0, in1=L, op0=ALU.is_le, op1=ALU.add))
            link(ts(xb_i[:, :], ib[:, :], 15, None, ALU.bitwise_and))
            link(stt(out=L, in0=xb_i[:, :], scalar=0.0, in1=L, op0=ALU.is_equal, op1=ALU.add))
            link(stt(out=L, in0=d, scalar=0.0, in1=L, op0=ALU.is_ge, op1=ALU.mult))
            x_, y_ = xb_f[:, :], ibf[:, :]
            link(ts(x_, L, 2.0, math.log(2.0), ALU.is_ge, ALU.mult))
            link(ts(y_, L, 3.0, math.log(1.5), ALU.is_ge, ALU.mult))
            link(tt(x_, x_, y_, ALU.add))
            link(ts(y_, L, 1.0, -1e30, ALU.is_lt, ALU.mult))
            link(tt(L, x_, y_, ALU.add))

        def att_pe(pe):
            def scores(n):
                h, i = divmod(n, NT)
                rows_ = slice(64 * (h % 2), 64 * (h % 2) + 64)
                W = (i + 1) * P
                if n >= 2:
                    pe.wait_ge(at_m, n - 1)
                for c0 in range(0, W, HALF):
                    w = min(HALF, W - c0)
                    last = nc.tensor.matmul(ps[:, 2 * (n % 2) + c0 // HALF, 0:w], QK[rows_, h // 2, i * P:(i + 1) * P],
                                            QK[rows_, 4 + h // 2, c0:c0 + w], start=True, stop=True)
                last.then_inc(at_s, 1)

            def transposes(n):
                i = n % NT
                pe.wait_ge(at_e, n + 1)
                if n:
                    pe.wait_ge(at_pt, n)
                for k in range(i + 1):
                    last = nc.tensor.transpose(ps[:, 4 + k // 4, (k % 4) * P:(k % 4 + 1) * P],
                                               prob[:, n % 2, k * P:(k + 1) * P], ident[:, :])
                last.then_inc(at_tr, 1)

            def values(n):
                h, i = divmod(n, NT)
                pe.wait_ge(at_pt, n + 1)
                if n >= 2:
                    pe.wait_ge(at_o, n - 1)
                for k in range(i + 1):
                    last = nc.tensor.matmul(ps[:, 6 + n % 2, 0:HEAD_DIM], probT[:, n % 2, k, :],
                                            V[:, k, h * HEAD_DIM:(h + 1) * HEAD_DIM], start=k == 0, stop=k == i)
                last.then_inc(at_pv, 1)

            pe.wait_ge(yt_f, 8)
            pe.wait_ge(gl_s, 8)
            scores(0)
            for n in range(NA):
                if n + 1 < NA:
                    scores(n + 1)
                transposes(n)
                if n:
                    values(n - 1)
            values(NA - 1)
            pe.wait_ge(at_o, NA)
            for q in range(8):
                j, half = divmod(q, 2)
                if q >= 2:
                    pe.wait_ge(ot_lo, q - 1)
                for t in range(4):
                    last = nc.tensor.transpose(ps[:, q % 2, t * P:(t + 1) * P],
                                               O[:, 4 * half + t, j * P:(j + 1) * P], ident[:, :])
                last.then_inc(ot_tr, 1)

        def att_act(act):
            def rest(n):
                i = n % NT
                act.wait_ge(at_tr, n + 1)
                if n >= 2:
                    act.wait_ge(at_pv, n - 1)
                w = (i + 1) * P
                nc.scalar.activation(probT[:, n % 2, 0:i + 1, :].rearrange("p a b -> p (a b)"),
                                     ps[:, 4:6, :].rearrange("p a b -> p (a b)")[:, 0:w], ACT.Copy).then_inc(at_pt, 1)

            for n in range(NA):
                w = (n % NT + 1) * P
                act.wait_ge(at_n, n + 1)
                if n >= 2:
                    act.wait_ge(at_tr, n - 1)
                nc.scalar.activation(prob[:, n % 2, 0:w], sco[:, n % 2, 0:w], ACT.Exp, bias=nm_[:, n:n + 1],
                                     accum_out=den_[:, n:n + 1]).then_inc(at_e, 1)
                if n:
                    rest(n - 1)
            rest(NA - 1)
            act.wait_ge(gl_lo, 8)
            for q in range(8):
                j, half = divmod(q, 2)
                act.wait_ge(ot_tr, q + 1)
                nc.scalar.activation(B[:, j, 0, half * HALF:(half + 1) * HALF], ps[:, q % 2, :],
                                     ACT.Copy).then_inc(ot_hi, 1)

        def att_dve(dve):
            link = lambda ins: link_dve(dve, ins)

            def head_bias(h):
                nc.vector.scalar_tensor_tensor(out=bias_h[:, h % 2, :], in0=dist[:, :], scalar=-2.0 ** (-(h + 1.0)),
                                               in1=lmul[:, :], op0=ALU.mult, op1=ALU.add).then_inc(dve_chain, 1)
                chained["dve"] += 1
                return chained["dve"]

            def maximum(n, made):
                h, i = divmod(n, NT)
                w = (i + 1) * P
                if i == 0:
                    dve.wait_ge(dve_chain, made)
                dve.wait_ge(at_s, n + 1)
                if n >= 2:
                    dve.wait_ge(at_e, n - 1)
                b = 2 * (n % 2)
                nc.vector.tensor_tensor_reduce(out=sco[:, n % 2, 0:w],
                                               in0=ps[:, b:b + 2, :].rearrange("p a b -> p (a b)")[:, 0:w],
                                               in1=bias_h[:, h % 2, S - w:S], scale=1.0, scalar=-3e38, op0=ALU.add,
                                               op1=ALU.max, accum_out=mx_[:, n:n + 1]).then_inc(at_m, 1)
                dve.wait_ge(at_m, n + 1)
                nc.vector.tensor_scalar(nm_[:, n:n + 1], mx_[:, n:n + 1], -1.0, None, ALU.mult).then_inc(at_n, 1)

            def finish(n):
                h, i = divmod(n, NT)
                dve.wait_ge(at_e, n + 1)
                nc.vector.reciprocal(rd_[:, n:n + 1], den_[:, n:n + 1]).then_inc(at_r, 1)
                dve.wait_ge(at_r, n + 1)
                dve.wait_ge(at_pv, n + 1)
                nc.vector.tensor_scalar(O[:, i, h * HEAD_DIM:(h + 1) * HEAD_DIM], ps[:, 6 + n % 2, 0:HEAD_DIM],
                                        rd_[:, n:n + 1], None, ALU.mult).then_inc(at_o, 1)

            made = [head_bias(0)]
            made.append(head_bias(1))
            maximum(0, made[0])
            for n in range(NA):
                if n + 1 < NA:
                    maximum(n + 1, made[(n + 1) // NT])
                if n % NT == NT - 1 and n // NT + 2 < N_HEADS:
                    made.append(head_bias(n // NT + 2))
                if n:
                    finish(n - 1)
            finish(NA - 1)
            for q in range(8):
                j, half = divmod(q, 2)
                dst = B[:, j, :, half * HALF:(half + 1) * HALF]
                dve.wait_ge(ot_hi, q + 1)
                nc.vector.tensor_tensor(dst[:, 1, :], ps[:, q % 2, :], dst[:, 0, :].bitcast(f32),
                                        ALU.subtract).then_inc(ot_lo, 1)

        mix_out = sem("mix_out")
        mixo = Wide("mixo", B, [A[:, u] for u in range(8)], U_MIXO,
                    lambda u: (at_pv, NA) if u < 4 else (ot_tr, 8), mix_out)
        n_ffn2 = Norm("g_ffn2", B, lambda t: (mix_out, NT + t + 1), post=1, residual=True)
        n_ffn2.gb_count, n_ffn2.old_count, n_ffn2.factor, n_ffn2.kept = 2, 4, 1.0, x_mid[2]
        ffn2 = Feed(D_FF2 // P // CHUNK, True, B, A, U_FFN2, (mixo.done, NT), False)
        ffn2.acc_stored = mid_stored[2]
        n_last = Norm(None, None, lambda t: ffn2.at("de", NT * (ffn2.n - 1) + t + 1), post=0, residual=True, final=True)
        n_last.gb_count, n_last.old_count, n_last.factor, n_last.kept = 3, 8, 0.5, out
        N_UNITS = ffn2.last_n

        def dve_mixo(dve, hooks):
            for g in range(2 * NT):
                half, t = divmod(g, NT)
                dve.wait_ge(mixo.done, g + 1)
                nc.vector.tensor_copy(acc[:, t, half * HALF:(half + 1) * HALF], ps[:, g % 6, :]).then_inc(mix_out, 1)
                hooks.get(g - NT, lambda: None)()

        block = ctx.enter_context(nc.Block())
        ffn1.acc_stored = mid_stored[0]
        assert N_UNITS % 2 == 0

        @block.sync
        def _(sp):
            for r in range(2):
                sp.dma_start(raw[:, r, :], stream[r, :, :]).then_inc(raw_full[r], 16)
            with sp.Fori(1, N_UNITS // 2) as i:
                for r in range(2):
                    sp.wait_ge(unit_ready, 2 * i + r - 1)
                    sp.dma_start(raw[:, r, :], stream[bass.ds(2 * i + r, 1), :, :].rearrange("a p n -> (a p) n")
                                 ).then_inc(raw_full[r], 16)

        def keep_rows(pool, N, k):
            for t in range(NT):
                pool.wait_ge(*N.at("res", t + 1))
                pool.dma_start(x_mid[k, t * P:(t + 1) * P, :], acc[:, t, :]).then_inc(mid_out, 16)

        def old_rows_again(pool, N, k):
            pool.wait_ge(mid_out, mid_stored[k])
            for t in range(NT):
                if t >= 2:
                    pool.wait_ge(*N.at("res", t - 1))
                pool.dma_start(old[:, t % 2, :], x_mid[k, t * P:(t + 1) * P, :]).then_inc(old_in[t % 2], 16)
                if t >= 1:
                    pool.wait_ge(*N.at("res", t))
                    pool.dma_start(N.kept[(t - 1) * P:t * P, :], acc[:, t - 1, :]).then_inc(mid_out, 16)
            pool.wait_ge(*N.at("res", NT))
            pool.dma_start(N.kept[(NT - 1) * P:NT * P, :], acc[:, NT - 1, :]).then_inc(mid_out, 16)

        @block.gpsimd
        def _(pool):
            pool.dma_start(col[:, :], cols).then_inc(params_in, 16)
            for i in range(2):
                pool.dma_start(acc[:, 4 * i:4 * i + 4, :],
                               x[i * HALF:(i + 1) * HALF, :].rearrange("(t p) d -> p t d", p=P)).then_inc(x_in[i], 16)
            pool.dma_start(gate_w[:, :, :], gate_mats).then_inc(mats_in, 16)
            pool.dma_start(pool_w[:, :, :], pool_mats).then_inc(mats_in, 16)
            pool.dma_start(inv_cnt[:, :, :], inv_count).then_inc(mats_in, 16)
            nc.gpsimd.memset(ident[:, :], 0.0).then_inc(ident_made, 1)
            pool.wait_ge(ident_made, 1)
            nc.gpsimd.affine_select(out=ident[:, :], in_=ident[:, :], compare_op=ALU.not_equal, fill=1.0, base=0,
                                    pattern=[[-1, P]], channel_multiplier=1).then_inc(ident_made, 1)
            pool.wait_ge(gates_done, 16)
            pool.wait_ge(poolmm_done, 8)
            pool.wait_ge(d_ready, 4)
            for g in range(2 * NT):
                half, t = divmod(g, NT)
                if g >= 4:
                    pool.wait_ge(res1, g - 3)
                pool.dma_start(rold[:, g % 4, :], x[t * P:(t + 1) * P, half * HALF:(half + 1) * HALF]
                               ).then_inc(old_rows[g % 4], 16)
            pool.wait_ge(res1, 2 * NT)
            pool.dma_start(praw[:, :, :], p.rearrange("(t p) d -> p t d", p=P)).then_inc(p_in, 16)
            pool.dma_start(gb[:, 0, :], rows[0, :, :]).then_inc(gb_in[0], 16)
            pool.dma_start(gb[:, 1, :], rows[1, :, :]).then_inc(gb_in[1], 16)
            keep_rows(pool, n_fin, 0)
            pool.wait_ge(ple_res, 2 * NT)
            pool.dma_start(gb[:, 0, :], rows[2, :, :]).then_inc(gb_in[0], 16)
            old_rows_again(pool, n_mix2, 0)
            pool.wait_ge(*n_mix2.at("res", NT))
            pool.dma_start(params_g[0:N_GROUPS, :], ssm_g).then_inc(g_in, 16)
            for b in range(NB4):
                ssm_batch_pool(pool, b)
            pool.wait_ge(s5_g, 6)
            nc.gpsimd.iota(ib[:, :], [[-1, S]], base=S - P, channel_multiplier=1).then_inc(io_done, 1)
            pool.wait_ge(yt_tr, 8)
            pool.dma_start(gb[:, 1, :], rows[3, :, :]).then_inc(gb_in[1], 16)
            pool.dma_start(gb[:, 0, :], rows[4, :, :]).then_inc(gb_in[0], 16)
            old_rows_again(pool, n_ffn2, 1)
            old_rows_again(pool, n_last, 2)
            pool.wait_ge(mid_out, 16 * NT * 4)

        @block.scalar
        def _(act):
            act.wait_ge(params_in, 16)
            act.wait_ge(eps_made, 1)
            act_mix1(act)
            wide_hi(act, w_out, range(8))
            norm_act(act, n_mlp, 0)
            first_hi(act, mlp)
            norm_act(act, n_mlp, 1)
            feed_on_act(act, mlp)
            ple_hi(act, 0, 4)
            norm_act(act, n_ple, 0)
            ple_hi(act, 4, 6)
            ple_act_p(act)
            norm_act(act, n_ple, 1)
            ple_act(act, 0, NT)
            ple_hi(act, 6, 10)
            ple_act(act, NT, NT + 4)
            norm_act_rows(act, n_fin, 0)
            ple_act(act, NT + 4, NT + 7)
            norm_act_split(act, n_fin, 0)
            ple_act(act, NT + 7, 2 * NT)
            first_hi(act, ffn1)
            norm_act(act, n_fin, 1)
            feed_on_act(act, ffn1)
            hi_of(act, qk_unit(0))
            hi_of(act, qk_unit(1))
            norm_act(act, n_mix2, 0)
            hi_of(act, qk_unit(2))
            hi_of(act, qk_unit(3))
            norm_act(act, n_mix2, 1)
            proj_act(act)
            ssm_params_act(act)
            ssm_act(act)
            glu_act(act)
            att_act(act)
            wide_hi(act, mixo, range(8))
            norm_act(act, n_ffn2, 0)
            first_hi(act, ffn2)
            norm_act(act, n_ffn2, 1)
            feed_on_act(act, ffn2)
            norm_act(act, n_last, 0)
            norm_act(act, n_last, 1)

        @block.vector
        def _(dve):
            dve.wait_ge(params_in, 16)
            dve.wait_ge(mats_in, 48)
            dve_mix1(dve)
            wide_lo(dve, w_out, range(8))
            dve_out1(dve, {**norm_dve_hooks(dve, n_mlp)})
            first_lo(dve, mlp)
            norm_dve(dve, n_mlp, 1)
            hooks = norm_dve_hooks(dve, n_ple)
            hooks[2] = lambda: ple_lo(dve, 0, 4)
            feed_on_dve(dve, mlp, hooks)
            ple_lo(dve, 4, 6)
            ple_dve_p(dve)
            norm_dve(dve, n_ple, 1)
            ple_dve(dve, norm_dve_hooks(dve, n_fin))
            first_lo(dve, ffn1)
            norm_dve(dve, n_fin, 1)
            hooks = norm_dve_hooks(dve, n_mix2)
            hooks[2] = lambda: [lo_of(dve, qk_unit(m)) for m in range(2)]
            feed_on_dve(dve, ffn1, hooks)
            for m in range(2, 4):
                lo_of(dve, qk_unit(m))
            norm_dve(dve, n_mix2, 1)
            proj_dve(dve)
            ssm_dve(dve)
            glu_dve(dve)
            bias_dve(dve)
            att_dve(dve)
            wide_lo(dve, mixo, range(8))
            dve_mixo(dve, norm_dve_hooks(dve, n_ffn2))
            first_lo(dve, ffn2)
            norm_dve(dve, n_ffn2, 1)
            feed_on_dve(dve, ffn2, norm_dve_hooks(dve, n_last))
            norm_dve(dve, n_last, 1)

        @block.tensor
        def _(pe):
            pe.wait_ge(ident_made, 2)
            norm_pe(pe, n_first, 0)
            pe_mix1(pe)
            wide_pe(pe, w_out, lambda h: pe.wait_ge(cat_lo, 8), norm=n_mlp)
            feed_pe(pe, mlp, {("before", 0): lambda: pe.wait_ge(*n_mlp.at("lo", 8)),
                              ("after", 0): lambda: norm_pe(pe, n_mlp, 1),
                              ("before", 1): lambda: pe.wait_ge(*n_mlp.at("lo", 16))},
                    {6: lambda: norm_pe(pe, n_ple, 0)})
            ple_pe(pe, n_fin)
            feed_pe(pe, ffn1, {("before", 0): lambda: pe.wait_ge(*n_fin.at("lo", 8)),
                               ("after", 0): lambda: norm_pe(pe, n_fin, 1),
                               ("before", 1): lambda: pe.wait_ge(*n_fin.at("lo", 16))},
                    {6: lambda: norm_pe(pe, n_mix2, 0)})
            proj_pe(pe)
            ssm_pe(pe)
            glu_pe(pe)
            att_pe(pe)
            wide_pe(pe, mixo, lambda h: pe.wait_ge(ot_lo, 8), norm=n_ffn2)
            feed_pe(pe, ffn2, {("before", 0): lambda: pe.wait_ge(*n_ffn2.at("lo", 8)),
                               ("after", 0): lambda: norm_pe(pe, n_ffn2, 1),
                               ("before", 1): lambda: pe.wait_ge(*n_ffn2.at("lo", 16))}, {})


def pack(i):
    import numpy as np
    f = lambda n: np.asarray(i[n])

    def tall(w):
        K, N = w.shape
        u = w.reshape(K // P, P, N // P, P).transpose(2, 1, 0, 3)
        return u.reshape(-1, P, UNIT)

    def wide(w):
        u = w.reshape(4, 2, P, w.shape[1] // HALF, HALF).transpose(3, 0, 2, 1, 4)
        return u.reshape(-1, P, UNIT)

    def down(w):
        return w.reshape(-1, P, UNIT)

    def feed(up, dn, nU):
        n = dn.shape[0] // CHUNK
        out = [up[0], up[1]]
        nxt = 2
        for c in range(n):
            for j in range(nU):
                if j == nU - 2 and c:
                    out += [dn[CHUNK * (c - 1)], dn[CHUNK * (c - 1) + 1]]
                if nxt < len(up):
                    out.append(up[nxt])
                    nxt += 1
        out += [dn[-2], dn[-1]]
        return np.stack(out)

    def gated(w):
        u = tall(w)
        n = len(u) // 2
        return np.stack([u[:n], u[n:]], axis=1).reshape(-1, P, UNIT)

    w_mix = f("w_mix_in_2")[0]
    glu = f("w_glu_2")[0].reshape(4, P, 2, 2, P).transpose(2, 1, 3, 0, 4).reshape(2, P, UNIT)
    w_in = tall(f("w_in")[0])
    order = [k for j in range(4) for k in (4 + j, 8 + j, j)]
    parts = [w_in[order], wide(f("w_out")[0]),
             feed(tall(f("w_up")[0]), down(f("w_down")[0]), CHUNK),
             down(f("w_ple_proj")[0]), wide(f("w_ple_gate")[0]),
             feed(gated(f("ffn1_w_in_2")[0]), down(f("ffn1_w_out_2")[0]), 2 * CHUNK),
             tall(w_mix[:, :1024]), wide(w_mix[:, 1024:]), glu,
             wide(f("w_mix_out_2")[0]),
             feed(gated(f("ffn2_w_in_2")[0]), down(f("ffn2_w_out_2")[0]), 2 * CHUNK)]
    stream = np.concatenate(parts)
    colsd = {
        "g_mix": f("norm_mix_g")[0].reshape(8, P), "g_mlp": f("norm_mlp_g")[0].reshape(8, P),
        "g_ple": f("norm_ple_g")[0].reshape(8, P), "g_ffn1": f("ffn1_pre_g_2")[0].reshape(8, P),
        "g_mix2": f("mix_pre_g_2")[0].reshape(8, P), "g_ffn2": f("ffn2_pre_g_2")[0].reshape(8, P),
        "pool_b": f("pool_b")[0], "pool_scale": f("pool_scale")[0].reshape(4, P),
        "conv_w": f("conv_w")[0].reshape(16, P), "conv_b": f("conv_b")[0].reshape(4, P),
        "gate_a_b": f("gate_a_b")[0].reshape(4, P), "gate_x_b": f("gate_x_b")[0].reshape(4, P),
        "lru_L": f("lru_L")[0].reshape(4, P), "b_glu": f("b_glu_2")[0].reshape(4, P),
        "sgn": np.repeat(np.array([-1.0, 1.0], np.float32), 64)[None],
    }
    cols = np.ascontiguousarray(np.concatenate([colsd[k] for k in COLS]).T)
    gate_mats = np.zeros((P, 8, P), np.float32)
    for kind, name in enumerate(("gate_a_w", "gate_x_w")):
        w = f(name)[0]
        for j in range(4):
            for q in range(2):
                gate_mats[64 * q:64 * q + 64, 4 * kind + j, 64 * q:64 * q + 64] = w[2 * j + q]
    pool_mats = np.ascontiguousarray(f("pool_w")[0].transpose(1, 0, 2))
    rows = np.stack([np.broadcast_to(f(n).reshape(1, D), (P, D)) for n in
                     ("b_ple_gate", "norm_final_g", "ffn1_post_g_2", "mix_post_g_2", "ffn2_post_g_2")])
    twice = lambda a: np.concatenate([a, a], axis=-1)
    ssm_g = np.concatenate([twice(f("a_re_2")[0]), twice(f("a_im_2")[0]), f("log_dt_2")[0][:, None]], axis=1)
    bre, bim = (f(n)[0].transpose(1, 0, 2).reshape(STATE, -1) for n in ("b_re_2", "b_im_2"))
    cre, cim = (f(n)[0].transpose(2, 0, 1).reshape(STATE, -1) for n in ("c_re_2", "c_im_2"))
    skip = np.zeros((P, N_GROUPS), np.float32)
    skip[:GROUP] = f("d_skip_2")[0].reshape(N_GROUPS, GROUP).T
    ssm_bc = np.concatenate([np.concatenate([bre, bim]), np.concatenate([bim, bre]), np.concatenate([cre, cim]),
                             np.concatenate([cim, cre]), skip], axis=1)
    inv_count = np.zeros((P, 4, 16), np.float32)
    for j, w in enumerate(WINDOWS):
        inv_count[:, j, :w] = 1.0 / np.arange(1, w + 1)
    return dict(x=f("x")[0], p=f("p")[0, 0], stream=stream, cols=cols, rows=rows, gate_mats=gate_mats,
                pool_mats=pool_mats, inv_count=inv_count, ssm_g=ssm_g, ssm_bc=ssm_bc)


def kernel(**inputs):
    import numpy as np
    from concourse import bacc
    from concourse.bass_utils import run_bass_kernel_spmd

    packed = pack(inputs)
    nc = bacc.Bacc("TRN2", target_bir_lowering=False, num_devices=1)
    f32 = mybir.dt.float32
    aps = {n: nc.dram_tensor(n, a.shape, f32, kind="ExternalInput").ap() for n, a in packed.items()}
    x_mid = nc.dram_tensor("x_mid", (3, S, D), f32, kind="Internal").ap()
    out = nc.dram_tensor("out", (S, D), f32, kind="ExternalOutput").ap()
    program(nc, x_mid=x_mid, out=out, **aps)
    r = run_bass_kernel_spmd(nc, [packed], core_ids=[0])
    return np.asarray(r.results[0]["out"]).reshape(1, S, D)
```

```python
import concourse.bass as bass
from concourse import mybir
from contextlib import ExitStack
import math

P = 128
S = 1024
D = 1024
NT = S // P
KD = D // P
HALF = 512
UNIT = 1024
EPS = 1e-6
SBUF_BASE = 16512
D_FF1 = 4096
D_FF2 = 2816
CHUNK = 2
LRU_C = 8.0
N_HEADS = 8
HEAD_DIM = 64
N_GROUPS = 32
GROUP = 16
STATE = 64
GT = 8
WINDOWS = (2, 4, 8, 16)

COLS = {}


def _columns():
    at = 0
    for name, n in (("g_mix", 8), ("g_mlp", 8), ("g_ple", 8), ("g_ffn1", 8), ("g_mix2", 8), ("g_ffn2", 8),
                    ("pool_b", 4), ("pool_scale", 4), ("conv_w", 16), ("conv_b", 4), ("gate_a_b", 4),
                    ("gate_x_b", 4), ("lru_L", 4), ("b_glu", 4), ("sgn", 1)):
        COLS[name] = at
        at += n
    return at


NCOLS = _columns()


def program(nc, x, p, stream, cols, rows, gate_mats, pool_mats, inv_count, ssm_g, ssm_bc, x_mid, out):
    f32 = mybir.dt.float32
    f32r = mybir.dt.float32r
    i32 = mybir.dt.int32
    ALU = mybir.AluOpType
    ACT = mybir.ActivationFunctionType

    ctx = ExitStack()
    with ctx:
        def at(name, offset, shape, dt=f32):
            return nc.alloc_sbuf_tensor_at(name, [P] + shape, dt, offset=SBUF_BASE + offset)

        def sem(name):
            return ctx.enter_context(nc.semaphore(name))

        KB = 1024
        OFF_A, OFF_B, OFF_ACC, OFF_XN = 0, 64 * KB, 128 * KB, 160 * KB
        OFF_RAW, OFF_GB, OFF_ROLD, OFF_ID = 176 * KB, 184 * KB, 192 * KB, 200 * KB
        whole = ctx.enter_context(nc.sbuf_tensor("whole", [P, 206 * KB], mybir.dt.uint8))
        A = at("region_a", OFF_A, [8, 2, UNIT], f32r)
        B = at("region_b", OFF_B, [8, 2, UNIT], f32r)
        acc = at("acc", OFF_ACC, [NT, D])
        xn = at("xn", OFF_XN, [4, D])
        raw = at("raw", OFF_RAW, [2, UNIT])
        gb = at("gb", OFF_GB, [2, D])
        rold = at("rold", OFF_ROLD, [4, HALF])
        ident = at("ident", OFF_ID, [P])
        col = at("col", OFF_ID + 512, [NCOLS])
        small = at("small", OFF_ID + 1024, [128])
        ps = ctx.enter_context(nc.psum_tensor("ps", [P, 8, HALF], f32))

        def c_(name, j=0):
            k = COLS[name] + j
            return col[:, k:k + 1]

        eps = small[:, 0:1]
        ss_pre, rms_pre, rinv_pre = small[:, 8:16], small[:, 16:24], small[:, 24:32]
        ss_post, rms_post, rinv_post = small[:, 32:40], small[:, 40:48], small[:, 48:56]
        c_pos, c_neg = small[:, 56:60], small[:, 60:64]
        lr = [small[:, 64 + 4 * i:68 + 4 * i] for i in range(6)]

        params_in = sem("params_in")
        x_in = [sem(f"x_in{i}") for i in range(2)]
        ident_made = sem("ident_made")
        eps_made = sem("eps_made")
        raw_full = [sem(f"raw_full{i}") for i in range(2)]
        hi_done = sem("hi_done")
        unit_ready = sem("unit_ready")
        dve_chain = sem("dve_chain")
        act_chain = sem("act_chain")
        chained = {"dve": 0, "act": 0}

        def link_dve(dve, ins):
            chained["dve"] += 1
            ins.then_inc(dve_chain, 1)
            dve.wait_ge(dve_chain, chained["dve"])

        def link_act(act, ins):
            chained["act"] += 1
            ins.then_inc(act_chain, 1)
            act.wait_ge(act_chain, chained["act"])

        def make_hi(act, n, slot, free, odd):
            act.wait_ge(raw_full[odd], 8 * (n - odd) + 16)
            if free:
                act.wait_ge(*free)
            nc.scalar.activation(slot[:, 0, :], raw[:, odd, :], ACT.Copy).then_inc(hi_done, 1)

        def make_lo(dve, n, slot, odd):
            dve.wait_ge(hi_done, n + 1)
            nc.vector.tensor_tensor(slot[:, 1, :], raw[:, odd, :], slot[:, 0, :].bitcast(f32),
                                    ALU.subtract).then_inc(unit_ready, 1)

        def products(psum, lhs, rhs, first, last):
            nc.tensor.matmul(psum, lhs(0), rhs(0), start=first, stop=False)
            nc.tensor.matmul(psum, lhs(0), rhs(1), start=False, stop=False)
            return nc.tensor.matmul(psum, lhs(1), rhs(0), start=False, stop=last)

        shared, taken = {}, {}

        def take(user, counts):
            kind = type(user).__name__.lower()
            user.base.update({s: taken.get((kind, s), 0) for s in counts})
            for s, total in counts.items():
                if (kind, s) not in shared:
                    shared[kind, s] = sem(f"{kind}_{s}")
                user.sem[s] = shared[kind, s]
                taken[kind, s] = taken.get((kind, s), 0) + total

        class Norm:

            def __init__(self, gain, Z, acc_ready, post=None, residual=False, final=False):
                self.gain, self.Z, self.acc_ready, self.post = gain, Z, acc_ready, post
                self.residual, self.final = residual, final
                self.base, self.sem = {}, {}
                if post is not None:
                    take(self, dict(psq=NT, prms=2, prinv=2, ptmp=NT if residual else 0, res=NT))
                if not final:
                    take(self, dict(sq=NT, rms=2, rinv=2, xn=NT, tr=2 * KD, hi=2 * KD, lo=2 * KD))

            def at(self, s, count):
                return self.sem[s], self.base[s] + count

        def norm_act_post(act, N, hf):
            for t in range(4 * hf, 4 * hf + 4):
                act.wait_ge(*N.acc_ready(t))
                if hf and t == 4:
                    act.wait_ge(*N.at("res", 4))
                    if not N.final:
                        act.wait_ge(*N.at("tr", 8))
                nc.scalar.activation(xn[:, t % 4, :], acc[:, t, :], ACT.Square,
                                     accum_out=ss_post[:, t:t + 1]).then_inc(N.sem["psq"], 1)
            act.wait_ge(*N.at("psq", 4 * hf + 4))
            nc.scalar.activation(rms_post[:, 4 * hf:4 * hf + 4], ss_post[:, 4 * hf:4 * hf + 4], ACT.Sqrt,
                                 bias=eps, scale=1.0 / D).then_inc(N.sem["prms"], 1)

        def norm_dve_post(dve, N, hf):
            g = gb[:, N.post, :]
            dve.wait_ge(gb_in[N.post], 16 * N.gb_count)
            dve.wait_ge(*N.at("prms", hf + 1))
            nc.vector.reciprocal(rinv_post[:, 4 * hf:4 * hf + 4],
                                 rms_post[:, 4 * hf:4 * hf + 4]).then_inc(N.sem["prinv"], 1)
            dve.wait_ge(*N.at("prinv", hf + 1))
            for t in range(4 * hf, 4 * hf + 4):
                if not N.residual:
                    nc.vector.scalar_tensor_tensor(out=acc[:, t, :], in0=acc[:, t, :],
                                                   scalar=rinv_post[:, t:t + 1], in1=g,
                                                   op0=ALU.mult, op1=ALU.mult).then_inc(N.sem["res"], 1)
                else:
                    nc.vector.scalar_tensor_tensor(out=xn[:, t % 4, :], in0=acc[:, t, :],
                                                   scalar=rinv_post[:, t:t + 1], in1=g,
                                                   op0=ALU.mult, op1=ALU.mult).then_inc(N.sem["ptmp"], 1)
                    dve.wait_ge(*N.at("ptmp", t + 1))
                    dve.wait_ge(old_in[t % 2], 16 * (N.old_count + t // 2 + 1))
                    nc.vector.scalar_tensor_tensor(out=acc[:, t, :], in0=xn[:, t % 4, :], scalar=N.factor,
                                                   in1=old[:, t % 2, :], op0=ALU.mult,
                                                   op1=ALU.add).then_inc(N.sem["res"], 1)

        def norm_act_stats(act, N, hf):
            for t in range(4 * hf, 4 * hf + 4):
                if N.post is not None:
                    act.wait_ge(*N.at("res", t + 1))
                else:
                    act.wait_ge(*N.acc_ready(t))
                if hf and t == 4:
                    act.wait_ge(*N.at("tr", 8))
                nc.scalar.activation(xn[:, t % 4, :], acc[:, t, :], ACT.Square,
                                     accum_out=ss_pre[:, t:t + 1]).then_inc(N.sem["sq"], 1)
            act.wait_ge(*N.at("sq", 4 * hf + 4))
            nc.scalar.activation(rms_pre[:, 4 * hf:4 * hf + 4], ss_pre[:, 4 * hf:4 * hf + 4], ACT.Sqrt,
                                 bias=eps, scale=1.0 / D).then_inc(N.sem["rms"], 1)

        def norm_act_split(act, N, hf):
            for d in range(KD):
                act.wait_ge(*N.at("tr", 8 * hf + d + 1))
                nc.scalar.activation(N.Z[:, d, 0, hf * HALF:(hf + 1) * HALF], ps[:, 6 + d % 2, :], ACT.Copy,
                                     scale=c_(N.gain, d)).then_inc(N.sem["hi"], 1)

        def norm_dve_scale(dve, N, hf):
            dve.wait_ge(*N.at("rms", hf + 1))
            nc.vector.reciprocal(rinv_pre[:, 4 * hf:4 * hf + 4],
                                 rms_pre[:, 4 * hf:4 * hf + 4]).then_inc(N.sem["rinv"], 1)
            dve.wait_ge(*N.at("rinv", hf + 1))
            for t in range(4 * hf, 4 * hf + 4):
                nc.vector.tensor_scalar(xn[:, t % 4, :], acc[:, t, :], rinv_pre[:, t:t + 1], None,
                                        ALU.mult).then_inc(N.sem["xn"], 1)

        def norm_dve_split(dve, N, hf):
            for d in range(KD):
                z = N.Z[:, d, :, hf * HALF:(hf + 1) * HALF]
                dve.wait_ge(*N.at("hi", 8 * hf + d + 1))
                nc.vector.scalar_tensor_tensor(out=z[:, 1, :], in0=ps[:, 6 + d % 2, :], scalar=c_(N.gain, d),
                                               in1=z[:, 0, :].bitcast(f32), op0=ALU.mult,
                                               op1=ALU.subtract).then_inc(N.sem["lo"], 1)

        def norm_act_rows(act, N, hf):
            if N.post is not None:
                norm_act_post(act, N, hf)
            if not N.final:
                norm_act_stats(act, N, hf)

        def norm_act(act, N, hf):
            norm_act_rows(act, N, hf)
            if not N.final:
                norm_act_split(act, N, hf)

        def norm_dve_rows(dve, N, hf):
            if N.post is not None:
                norm_dve_post(dve, N, hf)
            if not N.final:
                norm_dve_scale(dve, N, hf)

        def norm_dve(dve, N, hf):
            norm_dve_rows(dve, N, hf)
            if not N.final:
                norm_dve_split(dve, N, hf)

        def norm_dve_hooks(dve, N):
            hooks = {3: lambda: norm_dve_rows(dve, N, 0)}
            if not N.final:
                hooks[6] = lambda: norm_dve_split(dve, N, 0)
            return hooks

        def norm_pe(pe, N, hf):
            pe.wait_ge(*N.at("xn", 4 * hf + 4))
            for d in range(KD):
                if 8 * hf + d >= 2:
                    pe.wait_ge(*N.at("lo", 8 * hf + d - 1))
                for t in range(4):
                    last = nc.tensor.transpose(ps[:, 6 + d % 2, t * P:(t + 1) * P],
                                               xn[:, t, d * P:(d + 1) * P], ident[:, :])
                last.then_inc(N.sem["tr"], 1)

        gb_in = [sem(f"gb_in{i}") for i in range(2)]
        old = at("old", OFF_ROLD, [2, D])
        old_in = [sem(f"old_in{i}") for i in range(2)]
        old_rows = [sem(f"old_rows{i}") for i in range(4)]
        mid_out = sem("mid_out")

        n_first = Norm("g_mix", A, lambda t: (x_in[t // 4], 16))
        TALL1 = 12
        in_done = sem("in_done")
        lru_in, gate_in, pool_in = sem("lru_in"), sem("gate_in"), sem("pool_in")
        xb_ready = sem("xb_ready")
        gates_done, poolmm_done = sem("gates_done"), sem("poolmm_done")
        sig_done, pool_evac = sem("sig_done"), sem("pool_evac")
        th_done, ex_done, q_ready, sq_done = sem("th_done"), sem("ex_done"), sem("q_ready"), sem("sq_done")
        y_ready, d_ready, cpos_ready = sem("y_ready"), sem("d_ready"), sem("cpos_ready")
        cat_hi, cat_lo = sem("cat_hi"), sem("cat_lo")
        mats_in = sem("mats_in")
        sc = at("sc", OFF_B + 32 * KB, [8, S])
        UL, XB, R, I, T, AA, Q, G = (sc[:, i, :] for i in range(8))
        scx = at("scx", OFF_XN, [4, S])
        UP, W1, W2 = (scx[:, i, :] for i in range(3))
        Y = at("ystage", OFF_ACC, [8, S])
        gate_w = at("gate_w", OFF_ROLD, [8, P])
        pool_w = at("pool_w", OFF_ROLD + 4 * KB, [4, P])
        inv_cnt = at("inv_cnt", OFF_ROLD + 6 * KB, [4, 16])

        def tall_group(pe, Z, slot, kd, half, bank):
            for k in range(kd):
                last = products(ps[:, bank, :],
                                lambda h: slot[:, h, k * P:(k + 1) * P],
                                lambda h: Z[:, k, h, half * HALF:(half + 1) * HALF],
                                k == 0, k == kd - 1)
            return last

        small_groups = [("gate", j) if q < 4 else ("pool", j) for j in range(4) for q in range(6)]

        def pe_mix1(pe):
            issued = [0]
            count = {"gate": 0, "pool": 0}

            def small_bank():
                q = issued[0]
                if q >= 2:
                    kind = small_groups[q - 2][0]
                    nth = sum(1 for g in small_groups[:q - 1] if g[0] == kind)
                    pe.wait_ge(sig_done if kind == "gate" else pool_evac, nth)
                issued[0] += 1
                return 4 + q % 2

            def gates(j):
                pe.wait_ge(xb_ready, j + 1)
                for kind in range(2):
                    for half in range(2):
                        nc.tensor.matmul(ps[:, small_bank(), :], gate_w[:, 4 * kind + j, :],
                                         XB[:, half * HALF:(half + 1) * HALF], start=True,
                                         stop=True).then_inc(gates_done, 1)

            def poolmm(j):
                pe.wait_ge(d_ready, j + 1)
                for half in range(2):
                    nc.tensor.matmul(ps[:, small_bank(), :], pool_w[:, j, :],
                                     W2[:, half * HALF:(half + 1) * HALF], start=True,
                                     stop=True).then_inc(poolmm_done, 1)

            evac = (lru_in, gate_in, pool_in)
            for m in range(TALL1):
                pe.wait_ge(unit_ready, m + 1)
                for half in range(2):
                    g = 2 * m + half
                    if m == 0:
                        pe.wait_ge(*n_first.at("lo", 8 * half + 8))
                    if g >= 4:
                        pe.wait_ge(evac[(m - 2) % 3], 2 * ((m - 2) // 3) + half + 1)
                    tall_group(pe, A, B[:, m % 4], KD, half, g % 4).then_inc(in_done, 1)
                    if g == 0:
                        norm_pe(pe, n_first, 1)
                if m == 0:
                    pe.wait_ge(mats_in, 48)
                if m % 3 == 2:
                    gates(m // 3)
                if m % 3 == 0 and m:
                    poolmm(m // 3 - 1)
            poolmm(3)

        def hi1(act, m):
            make_hi(act, m, B[:, m % 4], (in_done, 2 * (m - 4) + 2) if m >= 4 else None, m % 2)

        def act_mix1(act):
            for m in range(2):
                hi1(act, m)
            norm_act(act, n_first, 0)
            for m in range(2, 4):
                hi1(act, m)
            norm_act(act, n_first, 1)
            act.wait_ge(cpos_ready, 1)
            nc.scalar.activation(lr[1], lr[0], ACT.Exp, scale=-1.0).then_inc(cpos_ready, 1)
            for j in range(4):
                for kind in range(3):
                    m = 3 * j + kind
                    dst = (UL, G, UP)[kind]
                    if j:
                        act.wait_ge(*((xb_ready, j), (y_ready, j), (d_ready, j))[kind])
                    for half in range(2):
                        act.wait_ge(in_done, 2 * m + half + 1)
                        nc.scalar.activation(dst[:, half * HALF:(half + 1) * HALF], ps[:, (2 * m + half) % 4, :],
                                             ACT.Gelu_apprx_tanh if kind == 1 else ACT.Copy
                                             ).then_inc((lru_in, gate_in, pool_in)[kind], 1)
                    if m + 4 < TALL1:
                        hi1(act, m + 4)
                for kind in range(2):
                    for half in range(2):
                        n = 4 * j + 2 * kind + half
                        act.wait_ge(gates_done, n + 1)
                        nc.scalar.activation((R, I)[kind][:, half * HALF:(half + 1) * HALF],
                                             ps[:, 4 + (6 * j + 2 * kind + half) % 2, :], ACT.Sigmoid,
                                             bias=c_(("gate_a_b", "gate_x_b")[kind], j)).then_inc(sig_done, 1)
                if j == 0:
                    act.wait_ge(cpos_ready, 3)
                act.wait_ge(sig_done, 4 * j + 4)
                nc.scalar.activation(T, R, ACT.Tanh, scale=c_pos[:, j:j + 1]).then_inc(th_done, 1)
                nc.scalar.activation(AA, R, ACT.Exp, scale=c_neg[:, j:j + 1]).then_inc(ex_done, 1)
                act.wait_ge(q_ready, j + 1)
                nc.scalar.activation(T, Q, ACT.Sqrt, scale=2.0).then_inc(sq_done, 1)
            for k in CAT_ORDER:
                act.wait_ge(y_ready, k - 3) if k >= 4 else act.wait_ge(pool_evac, 2 * k + 2)
                act.wait_ge(in_done, 2 * TALL1)
                nc.scalar.activation(A[:, k, 0, :], Y[:, k, :], ACT.Copy).then_inc(cat_hi, 1)

        CAT_ORDER = (0, 1, 2, 4, 5, 6, 3, 7)

        def dve_mix1(dve):
            dve.wait_ge(params_in, 16)
            nc.vector.memset(eps, EPS).then_inc(eps_made, 1)
            for m in range(2):
                make_lo(dve, m, B[:, m % 4], m % 2)
            norm_dve(dve, n_first, 0)
            for m in range(2, 4):
                make_lo(dve, m, B[:, m % 4], m % 2)
            norm_dve(dve, n_first, 1)
            L = col[:, COLS["lru_L"]:COLS["lru_L"] + 4]
            nc.vector.tensor_scalar(lr[2], L, -1.0, None, ALU.mult).then_inc(dve_chain, 1)
            chained["dve"] += 1
            dve.wait_ge(dve_chain, chained["dve"])
            nc.vector.tensor_tensor(lr[0], L, lr[2], ALU.max).then_inc(cpos_ready, 1)
            dve.wait_ge(cpos_ready, 2)
            e, s_, s2, sm = lr[1], lr[3], lr[4], lr[5]
            link_dve(dve, nc.vector.tensor_scalar(s_, e, 2.0, None, ALU.add))
            link_dve(dve, nc.vector.reciprocal(s_, s_))
            link_dve(dve, nc.vector.tensor_tensor(s_, s_, e, ALU.mult))
            link_dve(dve, nc.vector.tensor_tensor(s2, s_, s_, ALU.mult))
            link_dve(dve, nc.vector.tensor_scalar(sm, s2, 1.0 / 17, 1.0 / 15, ALU.mult, ALU.add))
            for n in (13, 11, 9, 7, 5, 3, 1):
                link_dve(dve, nc.vector.tensor_tensor(sm, sm, s2, ALU.mult))
                link_dve(dve, nc.vector.tensor_scalar(sm, sm, 1.0 / n, None, ALU.add))
            link_dve(dve, nc.vector.tensor_tensor(sm, sm, s_, ALU.mult))
            link_dve(dve, nc.vector.tensor_scalar(lr[2], lr[2], 0.0, LRU_C, ALU.max, ALU.mult))
            link_dve(dve, nc.vector.scalar_tensor_tensor(out=c_pos, in0=sm, scalar=2 * LRU_C, in1=lr[2],
                                                         op0=ALU.mult, op1=ALU.add))
            nc.vector.tensor_scalar(c_neg, c_pos, -1.0, None, ALU.mult).then_inc(cpos_ready, 1)

            def pool_out(j):
                for half in range(2):
                    dve.wait_ge(poolmm_done, 2 * j + half + 1)
                    nc.vector.tensor_scalar(Y[:, j, half * HALF:(half + 1) * HALF], ps[:, 4 + (6 * j + 4 + half) % 2, :],
                                            c_("pool_b", j), c_("pool_scale", j), ALU.add,
                                            ALU.mult).then_inc(pool_evac, 1)

            def lo1(m):
                if m + 4 < TALL1:
                    make_lo(dve, m + 4, B[:, m % 4], m % 2)

            for j in range(4):
                dve.wait_ge(lru_in, 2 * j + 2)
                if j:
                    dve.wait_ge(gates_done, 4 * j)
                w = lambda k: c_("conv_w", 4 * k + j)
                link_dve(dve, nc.vector.tensor_scalar(XB, UL, w(3), c_("conv_b", j), ALU.mult, ALU.add))
                for sh in range(1, 4):
                    ins = nc.vector.scalar_tensor_tensor(out=XB[:, sh:], in0=UL[:, :S - sh], scalar=w(3 - sh),
                                                         in1=XB[:, sh:], op0=ALU.mult, op1=ALU.add)
                    if sh < 3:
                        link_dve(dve, ins)
                    else:
                        ins.then_inc(xb_ready, 1)
                lo1(3 * j)
                if j:
                    pool_out(j - 1)
                lo1(3 * j + 1)
                dve.wait_ge(pool_in, 2 * j + 2)
                if j:
                    dve.wait_ge(poolmm_done, 2 * j)
                src, width = UP, 1
                bufs = [W1, W2] if j % 2 else [W2, W1]
                for step in range(j + 1):
                    dst = bufs[step % 2]
                    link_dve(dve, nc.vector.tensor_copy(dst[:, 0:width], src[:, 0:width]))
                    link_dve(dve, nc.vector.tensor_tensor(dst[:, width:], src[:, width:], src[:, :S - width], ALU.add))
                    src, width = dst, 2 * width
                head = W1[:, 0:width] if src is W2 else W2[:, 0:width]
                link_dve(dve, nc.vector.tensor_tensor(small_f[:, 0:width], src[:, 0:width], inv_cnt[:, j, 0:width], ALU.mult))
                link_dve(dve, nc.vector.scalar_tensor_tensor(out=W2, in0=src, scalar=1.0 / width, in1=UP,
                                                             op0=ALU.mult, op1=ALU.subtract))
                nc.vector.tensor_tensor(W2[:, 0:width], small_f[:, 0:width], UP[:, 0:width],
                                        ALU.subtract).then_inc(d_ready, 1)
                lo1(3 * j + 2)
                dve.wait_ge(th_done, j + 1)
                link_dve(dve, nc.vector.tensor_scalar(Q, T, 1.0, None, ALU.add))
                link_dve(dve, nc.vector.reciprocal(Q, Q))
                link_dve(dve, nc.vector.tensor_tensor(Q, Q, T, ALU.mult))
                nc.vector.tensor_scalar(Q, Q, 1e-34, None, ALU.max).then_inc(q_ready, 1)
                dve.wait_ge(xb_ready, j + 1)
                link_dve(dve, nc.vector.tensor_tensor(I, I, XB, ALU.mult))
                dve.wait_ge(sq_done, j + 1)
                link_dve(dve, nc.vector.memset(T[:, 0:1], 1.0))
                link_dve(dve, nc.vector.tensor_tensor(I, I, T, ALU.mult))
                dve.wait_ge(ex_done, j + 1)
                link_dve(dve, nc.vector.tensor_tensor_scan(R, AA, I, 0.0, ALU.mult, ALU.add))
                dve.wait_ge(gate_in, 2 * j + 2)
                nc.vector.tensor_tensor(Y[:, 4 + j, :], R, G, ALU.mult).then_inc(y_ready, 1)
            pool_out(3)
            for i, k in enumerate(CAT_ORDER):
                dve.wait_ge(cat_hi, i + 1)
                nc.vector.tensor_tensor(A[:, k, 1, :], Y[:, k, :], A[:, k, 0, :].bitcast(f32),
                                        ALU.subtract).then_inc(cat_lo, 1)

        small_f = at("small_f", OFF_ID + 1024 + 512, [16])

        class Wide:

            def __init__(self, name, acts, slots, first_unit, before, evac_of):
                self.done, self.acts, self.slots = sem(f"{name}_done"), acts, slots
                self.n0, self.before, self.evac_of = first_unit, before, evac_of

        def wide_pe(pe, W, ready, norm=None, after_first=None, stride=None, banks=6, also=None):
            for half in range(2):
                for t in range(NT):
                    g = NT * half + t
                    if g == 0:
                        ready(0)
                    if t == 0:
                        pe.wait_ge(unit_ready, W.n0 + 4 * half + 4)
                    if g >= banks:
                        pe.wait_ge(W.evac_of, g - banks + 1)
                    for k in range(KD):
                        slot = W.slots[4 * half + k // 2]
                        last = products(ps[:, g % banks, :],
                                        lambda h: W.acts[:, k, h, t * P:(t + 1) * P],
                                        lambda h: slot[:, h, (k % 2) * HALF:(k % 2 + 1) * HALF],
                                        k == 0, k == KD - 1)
                    last.then_inc(W.done, 1)
                    if g == 0 and after_first:
                        after_first()
                    if g == NT + 6 and norm:
                        norm_pe(pe, norm, 0)

        def wide_hi(act, W, us):
            for u in us:
                make_hi(act, W.n0 + u, W.slots[u], W.before(u), (W.n0 + u) % 2)

        def wide_lo(dve, W, us):
            for u in us:
                make_lo(dve, W.n0 + u, W.slots[u], (W.n0 + u) % 2)

        U_OUT = TALL1
        res1 = sem("res1")

        def before_out(u):
            if u < 4:
                return (in_done, 2 * TALL1)
            return (y_ready, 4)

        w_out = Wide("w_out", A, [B[:, u] for u in range(8)], U_OUT, before_out, res1)
        n_mlp = Norm("g_mlp", A, lambda t: (res1, NT + t + 1))

        def dve_out1(dve, hooks):
            for g in range(2 * NT):
                half, t = divmod(g, NT)
                dve.wait_ge(w_out.done, g + 1)
                dve.wait_ge(old_rows[g % 4], 16 * (g // 4 + 1))
                nc.vector.tensor_tensor(acc[:, t, half * HALF:(half + 1) * HALF], ps[:, g % 6, :], rold[:, g % 4, :],
                                        ALU.add).then_inc(res1, 1)
                hooks.get(g - NT, lambda: None)()

        class Feed:

            def __init__(self, n, gated, Z, W, first_unit, before, add_first):
                self.n, self.gated, self.Z, self.W, self.n0 = n, gated, Z, W, first_unit
                self.nU = 2 * CHUNK if gated else CHUNK
                self.before, self.add_first = before, add_first
                self.last_n = first_unit + n * (self.nU + 2)
                halves = 2 * CHUNK * n
                self.base, self.sem = {}, {}
                take(self, dict(up=2 * self.nU * n, ge=halves if gated else 0, ue=0 if gated else halves, sq=halves,
                                hi=halves, lo=halves, dn=NT * n, de=NT * n))

            def at(self, s, count):
                return self.sem[s], self.base[s] + count

            def start(self, c):
                return self.n0 + 2 + (0 if isinstance(c, int) and c == 0 else self.nU + (c - 1) * (self.nU + 2))

            def n_up(self, c, j):
                nU = self.nU
                if j < 2 and isinstance(c, int) and c == 0:
                    return self.n0 + j
                if j >= 2:
                    cc, jj = c, j - 2
                else:
                    cc, jj = c - 1, j + nU - 2
                down = 0 if isinstance(cc, int) and cc == 0 else 2
                return self.start(cc) + jj + (down if jj >= nU - 2 else 0)

            def n_down(self, c):
                if isinstance(c, int) and c == self.n - 1:
                    return self.last_n - 2
                return self.start(c + 1) + self.nU - 2

            def down_slot(self, c, f):
                last = isinstance(c, int) and c == self.n - 1
                return self.W[:, f if last else 2 + f]

        def h_slot(F, par, f):
            return F.W[:, 4 + 2 * par + f]

        def feed_up_pe(pe, F, c, par, hooks={}):
            for j in range(F.nU):
                pe.wait_ge(unit_ready, F.n_up(c, j) + 1)
                for half in range(2):
                    g = 2 * j + half
                    f = j // 2 if F.gated else j
                    first = isinstance(c, int) and c == 0 and g < 2
                    if not first:
                        if F.gated:
                            if j % 2:
                                pe.wait_ge(*F.at("ge", 2 * CHUNK * c + 2 * f + half + 1))
                            else:
                                pe.wait_ge(*F.at("sq", 2 * CHUNK * c + 2 * f + half - 1))
                        else:
                            pe.wait_ge(*F.at("ue", 2 * F.nU * c + g - 1))
                    hooks.get(("before", g), lambda: None)()
                    tall_group(pe, F.Z, F.W[:, j % 2], KD, half, g % 2).then_inc(F.sem["up"], 1)
                    hooks.get(("after", g), lambda: None)()

        def feed_down_pe(pe, F, c, par, hooks={}):
            pe.wait_ge(unit_ready, F.n_down(c) + 2)
            pe.wait_ge(*F.at("lo", 2 * CHUNK * c + 2 * CHUNK))
            for t in range(NT):
                if not (isinstance(c, int) and c == 0 and t < 2):
                    pe.wait_ge(*F.at("de", NT * c + t - 1))
                for half in range(2):
                    for f in range(CHUNK):
                        H, slot = h_slot(F, par, f), F.down_slot(c, f)
                        last = products(ps[:, 2 + 2 * (t % 2) + half, :],
                                        lambda h: H[:, h, t * P:(t + 1) * P],
                                        lambda h: slot[:, h, half * HALF:(half + 1) * HALF],
                                        f == 0, f == CHUNK - 1)
                last.then_inc(F.sem["dn"], 1)
                hooks.get(t, lambda: None)()

        rtmp = at("rtmp", OFF_XN, [2, HALF])
        stmp = at("stmp", OFF_XN + 4 * KB, [2, HALF])

        def feed_evac_act(act, F, c, par, j):
            f = j // 2 if F.gated else j
            H = h_slot(F, par, f)
            for half in range(2):
                k = 2 * CHUNK * c + 2 * f + half
                first = isinstance(c, int) and c == 0 and f == 0
                dst = H[:, 0, half * HALF:(half + 1) * HALF]
                act.wait_ge(*F.at("up", 2 * F.nU * c + 2 * j + half + 1))
                if F.gated and j % 2 == 0:
                    if not first:
                        act.wait_ge(*F.at("sq", k - 1))
                    nc.scalar.activation(rtmp[:, half, :], ps[:, half, :], ACT.Silu).then_inc(F.sem["ge"], 1)
                elif F.gated:
                    act.wait_ge(*F.at("sq", k + 1))
                    nc.scalar.activation(dst, stmp[:, half, :], ACT.Copy).then_inc(F.sem["hi"], 1)
                else:
                    if not first:
                        act.wait_ge(*F.at("sq", k - 1))
                    nc.scalar.activation(rtmp[:, half, :], ps[:, half, :], ACT.Relu).then_inc(F.sem["ue"], 1)
                    act.wait_ge(*F.at("ue", k + 1))
                    nc.scalar.activation(dst, rtmp[:, half, :], ACT.Square).then_inc(F.sem["hi"], 1)

        def feed_evac_dve(dve, F, c, par, j):
            f = j // 2 if F.gated else j
            if F.gated and j % 2 == 0:
                return
            H = h_slot(F, par, f)
            for half in range(2):
                k = 2 * CHUNK * c + 2 * f + half
                hi, lo = (H[:, h, half * HALF:(half + 1) * HALF] for h in range(2))
                if F.gated:
                    dve.wait_ge(*F.at("ge", k + 1))
                    dve.wait_ge(*F.at("up", 2 * F.nU * c + 2 * j + half + 1))
                    if not (isinstance(c, int) and c == 0 and f == 0):
                        dve.wait_ge(*F.at("lo", k - 1))
                    nc.vector.tensor_tensor(stmp[:, half, :], rtmp[:, half, :], ps[:, half, :],
                                            ALU.mult).then_inc(F.sem["sq"], 1)
                else:
                    dve.wait_ge(*F.at("ue", k + 1))
                    if not (isinstance(c, int) and c == 0 and f == 0):
                        dve.wait_ge(*F.at("lo", k - 1))
                    nc.vector.tensor_tensor(stmp[:, half, :], rtmp[:, half, :], rtmp[:, half, :],
                                            ALU.mult).then_inc(F.sem["sq"], 1)
                dve.wait_ge(*F.at("sq", k + 1))
                dve.wait_ge(*F.at("hi", k + 1))
                nc.vector.tensor_tensor(lo, stmp[:, half, :], hi.bitcast(f32), ALU.subtract).then_inc(F.sem["lo"], 1)

        def conversions(F, c, j):
            todo = []
            first, last = (isinstance(c, int) and c == k for k in (0, F.n - 1))
            n = F.start(c) + j + (2 if j > F.nU - 2 and not first else 0)
            if j == F.nU - 2 and not first:
                for f in range(2):
                    free = None if isinstance(c, int) and c == 1 else F.at("dn", NT * (c - 1))
                    todo.append((n, F.W[:, 2 + f], free))
                    n = n + 1
            if not (last and j >= F.nU - 2):
                todo.append((n, F.W[:, j % 2], F.at("up", 2 * F.nU * c + 2 * j + 2)))
            elif last and j == F.nU - 1:
                for f in range(2):
                    todo.append((F.last_n - 2 + f, F.W[:, f], F.at("up", 2 * F.nU * F.n)))
            return todo

        def feed_act(act, F, c, par, c_par):
            for j in range(F.nU):
                feed_evac_act(act, F, c, par, j)
                for i, (n, slot, free) in enumerate(conversions(F, c, j)):
                    make_hi(act, n, slot, free, (parity_of(F, c_par, j) + i) % 2)

        def parity_of(F, c, j):
            if c == F.n - 1 and j == F.nU - 1:
                return F.last_n % 2
            return (F.start(c) + j + (2 if j > F.nU - 2 and c != 0 else 0)) % 2

        def feed_dve_up(dve, F, c, par, c_par):
            for j in range(F.nU):
                feed_evac_dve(dve, F, c, par, j)
                for i, (n, slot, free) in enumerate(conversions(F, c, j)):
                    odd = (parity_of(F, c_par, j) + i) % 2
                    make_lo(dve, n, slot, odd)

        def feed_dve_down(dve, F, c, hooks={}):
            for t in range(NT):
                dve.wait_ge(*F.at("dn", NT * c + t + 1))
                src = ps[:, 2 + 2 * (t % 2):4 + 2 * (t % 2), :].rearrange("p a b -> p (a b)")
                if isinstance(c, int) and c == 0 and not F.add_first:
                    dve.wait_ge(mid_out, F.acc_stored)
                    nc.vector.tensor_copy(acc[:, t, :], src).then_inc(F.sem["de"], 1)
                else:
                    if not (isinstance(c, int) and c == 0):
                        dve.wait_ge(*F.at("de", NT * c + t - NT + 1))
                    nc.vector.tensor_tensor(acc[:, t, :], acc[:, t, :], src, ALU.add).then_inc(F.sem["de"], 1)
                hooks.get(t, lambda: None)()

        def feed_steps(eng, F, up, down, first_hooks, last_hooks):
            n = F.n
            up(0, 0, 0, first_hooks)
            up(1, 1, 1, {})
            down(0, 0, {})
            pairs = (n - 3) // 2
            with eng.Fori(1, pairs + 1) as i:
                up(2 * i, 0, 2, {})
                down(2 * i - 1, 1, {})
                up(2 * i + 1, 1, 3, {})
                down(2 * i, 0, {})
            for c in range(2 * pairs + 2, n):
                up(c, c % 2, c, {})
                down(c - 1, (c - 1) % 2, {})
            down(n - 1, (n - 1) % 2, last_hooks)

        def feed_pe(pe, F, first_hooks, last_hooks):
            feed_steps(pe, F, lambda c, par, cp, hk: feed_up_pe(pe, F, c, par, hk),
                       lambda c, par, hk: feed_down_pe(pe, F, c, par, hk), first_hooks, last_hooks)

        def feed_on_act(act, F):
            feed_steps(act, F, lambda c, par, cp, hk: feed_act(act, F, c, par, cp),
                       lambda c, par, hk: None, {}, {})

        def feed_on_dve(dve, F, last_hooks):
            feed_steps(dve, F, lambda c, par, cp, hk: feed_dve_up(dve, F, c, par, cp),
                       lambda c, par, hk: feed_dve_down(dve, F, c, hk), {}, last_hooks)

        def first_hi(act, F):
            for u in range(2):
                make_hi(act, F.n0 + u, F.W[:, u], F.before, (F.n0 + u) % 2)

        def first_lo(dve, F):
            for u in range(2):
                make_lo(dve, F.n0 + u, F.W[:, u], (F.n0 + u) % 2)

        U_MLP = U_OUT + 8
        mlp = Feed(D_FF1 // P // CHUNK, False, A, B, U_MLP, (w_out.done, NT), True)
        U_PLE = mlp.last_n
        n_ple = Norm("g_ple", A, lambda t: mlp.at("de", NT * (mlp.n - 1) + t + 1))

        praw = at("praw", OFF_ROLD, [NT, 256])
        vtmp = at("vtmp", OFF_ROLD, [4, HALF])
        p_in = sem("p_in")
        pt_tr, pt_hi, pt_lo = sem("pt_tr"), sem("pt_hi"), sem("pt_lo")
        ple_done, ple_v, ple_s, ple_m, ple_res = (sem(f"ple_{s}") for s in ("done", "v", "s", "m", "res"))
        PLE_SLOTS = (2, 3, 0, 1)
        mlp_all = NT * mlp.n

        def ple_units():
            units = [(U_PLE + u, B[:, 4 + u], mlp.at("dn", mlp_all - NT)) for u in range(2)]
            for half in range(2):
                for u in range(4):
                    free = (mlp.at("dn", mlp_all - NT) if u < 2 else mlp.at("dn", mlp_all)) if half == 0 else (ple_done, NT)
                    units.append((U_PLE + 2 + 4 * half + u, B[:, PLE_SLOTS[u]], free))
            return units

        def ple_hi(act, a, b):
            for n, slot, free in ple_units()[a:b]:
                make_hi(act, n, slot, free, n % 2)

        def ple_lo(dve, a, b):
            for n, slot, free in ple_units()[a:b]:
                make_lo(dve, n, slot, n % 2)

        def ple_pe(pe, norm_next):
            pe.wait_ge(p_in, 16)
            for q in range(4):
                kp, half = divmod(q, 2)
                if q >= 2:
                    pe.wait_ge(pt_lo, q - 1)
                for t in range(4):
                    last = nc.tensor.transpose(ps[:, q % 2, t * P:(t + 1) * P],
                                               praw[:, 4 * half + t, kp * P:(kp + 1) * P], ident[:, :])
                last.then_inc(pt_tr, 1)
            for g in range(2 * NT):
                half, t = divmod(g, NT)
                if g == 0:
                    pe.wait_ge(pt_lo, 4)
                    pe.wait_ge(*n_ple.at("lo", 8))
                if g == 1:
                    pe.wait_ge(*mlp.at("de", mlp_all))
                if g == 4:
                    pe.wait_ge(*n_ple.at("lo", 16))
                if t == 0:
                    pe.wait_ge(unit_ready, U_PLE + 2 + 4 * (half + 1))
                if g >= 3:
                    pe.wait_ge(ple_res, g - 2)
                b0 = 2 * (g % 3)
                for k in range(KD):
                    slot = B[:, PLE_SLOTS[k // 2]]
                    products(ps[:, b0, :], lambda h: A[:, k, h, t * P:(t + 1) * P],
                             lambda h: slot[:, h, (k % 2) * HALF:(k % 2 + 1) * HALF], k == 0, k == KD - 1)
                for kp in range(2):
                    last = products(ps[:, b0 + 1, :], lambda h: B[:, 6 + kp, h, t * P:(t + 1) * P],
                                    lambda h: B[:, 4 + kp, h, half * HALF:(half + 1) * HALF], kp == 0, kp == 1)
                last.then_inc(ple_done, 1)
                if g == 0:
                    norm_pe(pe, n_ple, 1)
                if g == NT + 6:
                    norm_pe(pe, norm_next, 0)

        def ple_act_p(act):
            for q in range(4):
                kp, half = divmod(q, 2)
                if q == 0:
                    act.wait_ge(*mlp.at("dn", mlp_all))
                act.wait_ge(pt_tr, q + 1)
                nc.scalar.activation(B[:, 6 + kp, 0, half * HALF:(half + 1) * HALF], ps[:, q % 2, :],
                                     ACT.Copy).then_inc(pt_hi, 1)

        def ple_dve_p(dve):
            for q in range(4):
                kp, half = divmod(q, 2)
                dst = B[:, 6 + kp, :, half * HALF:(half + 1) * HALF]
                dve.wait_ge(pt_hi, q + 1)
                nc.vector.tensor_tensor(dst[:, 1, :], ps[:, q % 2, :], dst[:, 0, :].bitcast(f32),
                                        ALU.subtract).then_inc(pt_lo, 1)

        def ple_act(act, g0, g1):
            for g in range(g0, g1):
                act.wait_ge(ple_v, g + 1)
                nc.scalar.activation(vtmp[:, g % 2, :], vtmp[:, g % 2, :], ACT.Sigmoid).then_inc(ple_s, 1)

        def ple_dve(dve, hooks):
            def bias(g):
                half, t = divmod(g, NT)
                dve.wait_ge(ple_done, g + 1)
                if g >= 2:
                    dve.wait_ge(ple_m, g - 1)
                nc.vector.tensor_tensor(vtmp[:, g % 2, :], ps[:, 2 * (g % 3), :],
                                        gb[:, 0, half * HALF:(half + 1) * HALF], ALU.add).then_inc(ple_v, 1)

            late = (NT - 1, NT + 3, NT + 6)
            dve.wait_ge(gb_in[0], 16)
            dve.wait_ge(pt_tr, 4)
            bias(0)
            for g in range(2 * NT):
                half, t = divmod(g, NT)
                if g + 1 < 2 * NT and g not in late:
                    bias(g + 1)
                dve.wait_ge(ple_s, g + 1)
                if g >= 2:
                    dve.wait_ge(ple_res, g - 1)
                nc.vector.tensor_tensor(vtmp[:, 2 + g % 2, :], vtmp[:, g % 2, :], ps[:, 2 * (g % 3) + 1, :],
                                        ALU.mult).then_inc(ple_m, 1)
                dve.wait_ge(ple_m, g + 1)
                nc.vector.tensor_tensor(acc[:, t, half * HALF:(half + 1) * HALF],
                                        acc[:, t, half * HALF:(half + 1) * HALF], vtmp[:, 2 + g % 2, :],
                                        ALU.add).then_inc(ple_res, 1)
                hooks.get(g - NT, lambda: None)()
                if g == NT - 1:
                    ple_lo(dve, 6, 10)
                if g in late:
                    bias(g + 1)

        U_FFN1 = U_PLE + 10
        n_fin = Norm("g_ffn1", A, lambda t: (ple_res, NT + t + 1), post=1)
        n_fin.gb_count = 1
        ffn1 = Feed(D_FF2 // P // CHUNK, True, A, B, U_FFN1, (ple_done, 2 * NT), False)
        n_mix2 = Norm("g_mix2", A, lambda t: ffn1.at("de", NT * (ffn1.n - 1) + t + 1), post=0, residual=True)
        n_mix2.gb_count, n_mix2.old_count, n_mix2.factor, n_mix2.kept = 2, 0, 0.5, x_mid[1]
        U_QK = ffn1.last_n
        mid_stored = [16 * NT * (k + 1) for k in range(3)]

        U_V = U_QK + 8
        U_U = U_V + 4
        U_GLU = U_U + 4
        U_MIXO = U_GLU + 2
        U_FFN2 = U_MIXO + 8
        qk_done, qk_out, v_done, v_out, u_done, u_out = (sem(s) for s in (
            "qk_done", "qk_out", "v_done", "v_out", "u_done", "u_out"))
        QK = at("qk", OFF_ACC, [8, S])
        V = at("v", OFF_XN, [NT, HALF])
        U = at("u", OFF_GB, [GT, HALF])
        SLOTS4 = (2, 3, 0, 1)
        f1_all = NT * ffn1.n

        def qk_unit(m):
            free = (ffn1.at("dn", f1_all - NT) if m < 2 else ffn1.at("dn", f1_all)) if m < 4 \
                else (qk_done, 2 * (m - 4) + 2)
            return U_QK + m, B[:, SLOTS4[m % 4]], free

        def v_unit(u):
            return U_V + u, B[:, 4 + u], ffn1.at("dn", f1_all)

        def u_unit(u):
            return U_U + u, B[:, SLOTS4[u]], (qk_done, 2 * (4 + u) + 2)

        def hi_of(act, unit):
            n, slot, free = unit
            make_hi(act, n, slot, free, n % 2)

        def lo_of(dve, unit):
            make_lo(dve, unit[0], unit[1], unit[0] % 2)

        def proj_pe(pe):
            for m in range(8):
                pe.wait_ge(unit_ready, U_QK + m + 1)
                for half in range(2):
                    g = 2 * m + half
                    if m == 0:
                        pe.wait_ge(*n_mix2.at("lo", 8 * half + 8))
                        if half == 0:
                            pe.wait_ge(*ffn1.at("de", f1_all))
                    if g >= 4:
                        pe.wait_ge(qk_out, g - 3)
                    tall_group(pe, A, B[:, SLOTS4[m % 4]], KD, half, g % 4).then_inc(qk_done, 1)
                    if g == 0:
                        norm_pe(pe, n_mix2, 1)
            pe.wait_ge(unit_ready, U_V + 4)
            for t in range(NT):
                if t >= 2:
                    pe.wait_ge(v_out, t - 1)
                for k in range(KD):
                    slot = B[:, 4 + k // 2]
                    last = products(ps[:, 4 + t % 2, :], lambda h: A[:, k, h, t * P:(t + 1) * P],
                                    lambda h: slot[:, h, (k % 2) * HALF:(k % 2 + 1) * HALF], k == 0, k == KD - 1)
                last.then_inc(v_done, 1)
                if t == 5:
                    pe.wait_ge(g_ready, 1)
                    for q in range(7):
                        last = nc.tensor.transpose(ps[:, 6, q * 32:(q + 1) * 32], QG[:, q, :], ident[0:32, 0:32])
                    last.then_inc(g_tr, 1)
            pe.wait_ge(unit_ready, U_U + 4)
            for t in range(GT):
                pe.wait_ge(*((u_out, t - 1) if t >= 2 else (v_out, NT - 1 + t)))
                for k in range(KD):
                    slot = B[:, SLOTS4[k // 2]]
                    last = products(ps[:, 4 + t % 2, :],
                                    lambda h: A[:, k, h, :].rearrange("p (c t) -> p t c", t=GT)[:, t, :],
                                    lambda h: slot[:, h, (k % 2) * HALF:(k % 2 + 1) * HALF], k == 0, k == KD - 1)
                last.then_inc(u_done, 1)

        def proj_act(act):
            for m in range(8):
                for half in range(2):
                    if m == 0:
                        act.wait_ge(mid_out, mid_stored[1])
                        act.wait_ge(*n_mix2.at("xn", NT))
                    act.wait_ge(qk_done, 2 * m + half + 1)
                    nc.scalar.activation(QK[:, m, half * HALF:(half + 1) * HALF], ps[:, (2 * m + half) % 4, :],
                                         ACT.Copy, scale=HEAD_DIM ** -0.5 if m < 4 else 1.0).then_inc(qk_out, 1)
                hi_of(act, qk_unit(m + 4) if m < 4 else v_unit(m - 4))
            for u in range(4):
                hi_of(act, u_unit(u))

        def proj_dve(dve):
            for m in range(4):
                lo_of(dve, qk_unit(m + 4))
            for u in range(4):
                lo_of(dve, v_unit(u))
            for u in range(4):
                lo_of(dve, u_unit(u))
            ssm_params_dve(dve)
            for t in range(NT):
                dve.wait_ge(v_done, t + 1)
                nc.vector.tensor_copy(V[:, t, :], ps[:, 4 + t % 2, :]).then_inc(v_out, 1)
            ssm_powers_dve(dve)
            s5_prepare = ssm_prepare_dve(dve, 0)
            for t in range(GT):
                dve.wait_ge(u_done, t + 1)
                nc.vector.tensor_copy(U[:, t, :], ps[:, 4 + t % 2, :]).then_inc(u_out, 1)
                next(s5_prepare, None)

        params_g = at("params_g", OFF_GB, [2 * P + 1])
        g_tmp = at("g_tmp", OFF_GB + 2 * KB, [14, P])
        qg = at("qg", OFF_GB + 10 * KB, [7, P])
        G32 = slice(0, N_GROUPS)
        QG = qg[G32]
        st = at("st", OFF_ID + 2048, [26, N_GROUPS])
        (AR, SAI, UR, UI, RHO, FR, SFI, A2R, SA2I, A4R, SA4I) = (st[:, i, :] for i in range(11))
        WR = [st[:, 11 + i, :] for i in range(7)]
        NWI = [st[:, 18 + i, :] for i in range(7)]
        sgn = col[:, COLS["sgn"]:COLS["sgn"] + 1]
        nsgn = small[:, 100:101]
        g_in, g_ready, g_tr = sem("g_in"), sem("g_ready"), sem("g_tr")
        g_d, g_a = sem("g_d"), sem("g_a")
        TWO_PI = 2 * math.pi
        C1 = 6.28125
        C2 = 0.0019340515136718750
        C3 = TWO_PI - C1 - C2
        ROUND = 1.5 * 2 ** 23

        are, aim, ldt = params_g[G32, 0:P], params_g[G32, P:2 * P], params_g[G32, 2 * P:2 * P + 1]
        gt = [g_tmp[G32, i, :] for i in range(14)]
        dt_ = g_tmp[G32, 13, 0:1]
        wr, wi, th, kk_, r_, sn, s2_, cm1, e1, inv, x0, x1 = gt[:12]

        def ssm_params_act(act):
            act.wait_ge(g_in, 16)
            nc.scalar.activation(dt_, ldt, ACT.Exp).then_inc(g_a, 1)
            act.wait_ge(g_d, 1)
            nc.scalar.activation(th, wr, ACT.Tanh, scale=0.5).then_inc(g_a, 1)
            nc.scalar.activation(QG[:, 4, :], wr, ACT.Exp, scale=float(GT)).then_inc(g_a, 1)
            act.wait_ge(g_d, 2)
            nc.scalar.activation(QG[:, 3, :], r_, ACT.Sin).then_inc(g_a, 1)
            nc.scalar.activation(s2_, r_, ACT.Sin, scale=0.5).then_inc(g_a, 1)

        def ssm_params_dve(dve):
            ts, tt, stt = nc.vector.tensor_scalar, nc.vector.tensor_tensor, nc.vector.scalar_tensor_tensor
            link = lambda ins: link_dve(dve, ins)
            dve.wait_ge(g_a, 1)
            link(ts(wi, aim, dt_, None, ALU.mult))
            ts(wr, are, dt_, None, ALU.mult).then_inc(g_d, 1)
            link(ts(kk_, wi, 1.0 / TWO_PI, ROUND, ALU.mult, ALU.add))
            link(ts(kk_, kk_, -ROUND, None, ALU.add))
            link(stt(out=r_, in0=kk_, scalar=-C1, in1=wi, op0=ALU.mult, op1=ALU.add))
            link(stt(out=r_, in0=kk_, scalar=-C2, in1=r_, op0=ALU.mult, op1=ALU.add))
            link(stt(out=r_, in0=kk_, scalar=-C3, in1=r_, op0=ALU.mult, op1=ALU.add))
            ts(r_, r_, 3.1415925, -3.1415925, ALU.min, ALU.max).then_inc(g_d, 1)
            dve.wait_ge(g_a, 3)
            link(ts(x0, th, -1.0, 1.0, ALU.mult, ALU.add))
            link(nc.vector.reciprocal(x0, x0))
            link(stt(out=e1, in0=th, scalar=2.0, in1=x0, op0=ALU.mult, op1=ALU.mult))
            dve.wait_ge(g_a, 5)
            link(stt(out=cm1, in0=s2_, scalar=-2.0, in1=s2_, op0=ALU.mult, op1=ALU.mult))
            link(ts(QG[:, 2, :], cm1, 1.0, None, ALU.add))
            link(ts(x0, e1, 1.0, None, ALU.add))
            link(tt(QG[:, 0, :], x0, QG[:, 2, :], ALU.mult))
            link(tt(QG[:, 1, :], x0, QG[:, 3, :], ALU.mult))
            link(tt(x1, e1, QG[:, 2, :], ALU.mult))
            link(tt(x1, x1, cm1, ALU.add))
            link(tt(x0, are, are, ALU.mult))
            link(tt(inv, aim, aim, ALU.mult))
            link(tt(inv, inv, x0, ALU.add))
            link(nc.vector.reciprocal(inv, inv))
            link(tt(x0, QG[:, 1, :], aim, ALU.mult))
            link(tt(e1, x1, are, ALU.mult))
            link(tt(e1, e1, x0, ALU.add))
            link(tt(QG[:, 5, :], e1, inv, ALU.mult))
            link(tt(x0, QG[:, 1, :], are, ALU.mult))
            link(tt(e1, x1, aim, ALU.mult))
            link(tt(e1, x0, e1, ALU.subtract))
            tt(QG[:, 6, :], e1, inv, ALU.mult).then_inc(g_ready, 1)

        def ssm_powers_dve(dve):
            ts, tt, stt = nc.vector.tensor_scalar, nc.vector.tensor_tensor, nc.vector.scalar_tensor_tensor
            link = lambda ins: link_dve(dve, ins)
            dve.wait_ge(g_tr, 1)
            link(nc.vector.tensor_copy(st[:, 0:7, :].rearrange("p a b -> p (a b)"), ps[:, 6, 0:7 * N_GROUPS]))
            link(ts(nsgn, sgn, -1.0, None, ALU.mult))
            t0, t1 = pw_tmp[:, 0:N_GROUPS], pw_tmp[:, N_GROUPS:2 * N_GROUPS]
            ar_, ai_ = AR, SAI
            for R2, I2 in ((A2R, SA2I), (A4R, SA4I)):
                square(link, R2, I2, ar_, ai_, t0, t1)
                ar_, ai_ = R2, I2
            for x_ in (SAI, SA2I, SA4I, SFI):
                link(ts(x_, x_, sgn, None, ALU.mult))
            ur, ui = UR, UI
            for _ in range(2):
                square(link, ur, ui, ur, ui, t0, t1)
            square(link, WR[0], NWI[0], ur, ui, t0, t1)
            for m in range(1, 7):
                square(link, WR[m], NWI[m], WR[m - 1], NWI[m - 1], t0, t1)
            link(ts(st[:, 18:25, :], st[:, 18:25, :], -1.0, None, ALU.mult))
            nc.vector.tensor_copy(pw_tmp[:, 0:1], pw_tmp[:, 1:2]).then_inc(pw_ready, 1)

        def square(link, R2, I2, R1, I1, t0, t1):
            link(nc.vector.tensor_tensor(t0, R1, R1, ALU.mult))
            link(nc.vector.tensor_tensor(t1, I1, I1, ALU.mult))
            link(nc.vector.scalar_tensor_tensor(out=I2, in0=R1, scalar=2.0, in1=I1, op0=ALU.mult, op1=ALU.mult))
            link(nc.vector.tensor_tensor(R2, t0, t1, ALU.subtract))

        pw_tmp = at("pw_tmp", OFF_ID + 1024 + 256 + 64 + 128, [2 * N_GROUPS])
        pw_ready = sem("pw_ready")

        NB, GB = N_HEADS, N_GROUPS // N_HEADS
        bufs_ssm = []
        for o in (OFF_B + 40 * KB + 256, OFF_B):
            bufs_ssm.append(dict(
                VV=at("vv", o, [GB, 9 * GROUP]), VS=at("vs", o + 2304, [GB, 9 * GROUP]),
                Z=at("z", o + 4608, [GB, GT * GROUP]), ZS=at("zs", o + 6656, [GB, GT * GROUP]),
                T=at("toep", o + 8704, [GB, P]), CS=at("cs", o + 10752, [GB, P]), SN=at("sn", o + 12800, [GB, P])))
        ssm_in = at("ssm_in", OFF_B + 32 * KB, [4 * N_GROUPS * GROUP + N_GROUPS])
        BA, BB, CA, CB = (ssm_in[:, i * 512:(i + 1) * 512].rearrange("p (g c) -> p g c", g=N_GROUPS) for i in range(4))
        dT = ssm_in[0:GROUP, 2048:2048 + N_GROUPS]
        o = OFF_B + 54 * KB + 768
        tmp_v = at("tmp_v", o, [4, GB * 64])
        tmp_p = at("tmp_p", o + 4 * KB, [4, GB * 64])
        nbb = at("nbb", o + 8 * KB, [GB, GROUP])
        kd = at("kd", o + 8 * KB + 256, [GB, GROUP])
        o = OFF_B + 14 * KB + 512
        ztb = at("ztb", o, [2, 3, 512])
        ob = at("ob", o + 12 * KB, [2, GB, P + 1])
        o = OFF_A + 56 * KB
        kkb = at("kkb", o, [GB, P])
        m1b = at("m1b", o + 2 * KB, [512])
        m2b = at("m2b", o + 4 * KB, [512])
        yb = at("yb", o + 4 * KB, [GB, P])
        ub = at("ub", o + 6 * KB, [GB, GT * GROUP])
        ub_made = sem("ub_made")
        s_in = sem("s_in")
        zb_ready, tab_ready, v_ready, nb_ready = sem("zb_ready"), sem("tab_ready"), sem("v_ready"), sem("nb_ready")
        t_zero, kk_done, kk_out, kk_d, t_in = (sem(s) for s in ("t_zero", "kk_done", "kk_out", "kk_d", "t_in"))
        s5_m = sem("s5_m")
        s5_tr, s5_cp, s5_s, s5_o, s5_y, s5_g = (sem(s) for s in ("s5_tr", "s5_cp", "s5_s", "s5_o", "s5_y", "s5_g"))
        pool_chain = sem("pool_chain")
        chained["pool"] = 0

        def link_pool(pool, ins):
            chained["pool"] += 1
            ins.then_inc(pool_chain, 1)
            pool.wait_ge(pool_chain, chained["pool"])

        def cmul(eng, link, dst, dsts, src, srcs, pr, spi, tmp, last=None):
            m = src.shape[2]
            t = [tmp[:, i, 0:GB * m].rearrange("p (g m) -> p g m", g=GB) for i in range(4)]
            pr = pr.unsqueeze(2).to_broadcast([P, GB, m])
            spi = spi.unsqueeze(2).to_broadcast([P, GB, m])
            eng.tensor_tensor(t[0], src, pr, ALU.mult)
            eng.tensor_tensor(t[1], srcs, spi, ALU.mult)
            eng.tensor_tensor(t[2], srcs, pr, ALU.mult)
            link(eng.tensor_tensor(t[3], src, spi, ALU.mult))
            eng.tensor_tensor(dst, t[0], t[1], ALU.add)
            ins = eng.tensor_tensor(dsts, t[2], t[3], ALU.subtract)
            if last is None:
                link(ins)
            else:
                ins.then_inc(last, 1)

        def ssm_prepare_dve(dve, b):
            bf = bufs_ssm[b % 2]
            gs = slice(GB * b, GB * b + GB)
            link = lambda ins: link_dve(dve, ins)
            if b == 0:
                dve.wait_ge(s_in, 16)
            elif b >= 2:
                dve.wait_ge(s5_y, b - 1)
            Z, ZS, CS, SN = (bf[n] for n in ("Z", "ZS", "CS", "SN"))
            cut = lambda X, a, m: X[:, :, a * GROUP:(a + m) * GROUP]

            def doubled(k):
                m = 1 << k
                cmul(nc.vector, link, CS[:, :, m:2 * m], SN[:, :, m:2 * m], CS[:, :, 0:m], SN[:, :, 0:m],
                     WR[k][:, gs], NWI[k][:, gs], tmp_v)

            cmul(nc.vector, link, cut(Z, 7, 1), cut(ZS, 7, 1), BA[:, gs, :], BB[:, gs, :], FR[:, gs], SFI[:, gs], tmp_v)
            if b:
                dve.wait_ge(kk_done, b)
            nc.vector.tensor_scalar(nbb[:, :, :], cut(Z, 7, 1), nsgn, None, ALU.mult).then_inc(nb_ready, 1)
            yield
            cmul(nc.vector, link, cut(Z, 6, 1), cut(ZS, 6, 1), cut(Z, 7, 1), cut(ZS, 7, 1), AR[:, gs], SAI[:, gs], tmp_v)
            yield
            cmul(nc.vector, link, cut(Z, 4, 2), cut(ZS, 4, 2), cut(Z, 6, 2), cut(ZS, 6, 2), A2R[:, gs], SA2I[:, gs], tmp_v)
            cmul(nc.vector, link, cut(Z, 0, 4), cut(ZS, 0, 4), cut(Z, 4, 4), cut(ZS, 4, 4), A4R[:, gs], SA4I[:, gs],
                 tmp_v, last=zb_ready)
            yield
            nc.vector.memset(CS[:, :, 0:1], 1.0)
            link(nc.vector.memset(SN[:, :, 0:1], 0.0))
            doubled(0)
            doubled(1)
            yield
            doubled(2)
            doubled(3)
            yield
            doubled(4)
            yield
            doubled(5)
            yield
            doubled(6)
            yield

        def ssm_skip_dve(dve, b):
            gs = slice(GB * b, GB * b + GB)
            link_dve(dve, nc.vector.tensor_tensor(
                kd[0:GROUP], ident[0:GROUP, 0:GROUP].unsqueeze(1).to_broadcast([GROUP, GB, GROUP]),
                dT[:, gs].unsqueeze(2).to_broadcast([GROUP, GB, GROUP]), ALU.mult))
            dve.wait_ge(kk_out, b + 1)
            nc.vector.tensor_tensor(kkb[0:GROUP, :, 0:GROUP], kkb[0:GROUP, :, 0:GROUP], kd[0:GROUP],
                                    ALU.add).then_inc(kk_d, 1)

        def ssm_scan_dve(dve, b, part):
            link = lambda ins: link_dve(dve, ins)
            bf = bufs_ssm[b % 2]
            cs, sn_ = bf["CS"][:, :, :], bf["SN"][:, :, :]
            v = lambda X: X[:, :].rearrange("p (a b) -> p a b", a=GB)
            bank = ps[:, 7, :].rearrange("p (a b) -> p a b", a=GB)
            dve.wait_ge(s5_s, 2 * b + part + 1)
            if part == 0:
                nc.vector.tensor_tensor(v(m1b), bank, cs, ALU.mult).then_inc(s5_m, 1)
                return
            if b == 0:
                link(nc.vector.memset(ob[:, :, :, 0:1], 0.0))
            nc.vector.scalar_tensor_tensor(out=v(m2b), in0=bank, scalar=nsgn, in1=sn_, op0=ALU.mult,
                                           op1=ALU.mult).then_inc(s5_m, 1)
            dve.wait_ge(s5_m, 2 * b + 2)
            link(nc.vector.tensor_tensor(m1b[:, :], m1b[:, :], m2b[:, :], ALU.add))
            for i in range(GB):
                g = GB * b + i
                ins = nc.vector.tensor_tensor_scan(yb[:, i, :], RHO[:, g:g + 1].to_broadcast([P, P]),
                                                   m1b[:, i * P:(i + 1) * P], 0.0, ALU.mult, ALU.add)
            link(ins)
            if b:
                dve.wait_ge(s5_y, b)
            nc.vector.scalar_tensor_tensor(out=ob[:, 0, :, 1:], in0=yb[:, :, :], scalar=nsgn, in1=cs,
                                           op0=ALU.mult, op1=ALU.mult)
            nc.vector.scalar_tensor_tensor(out=ob[:, 1, :, 1:], in0=yb[:, :, :], scalar=-1.0, in1=sn_,
                                           op0=ALU.mult, op1=ALU.mult).then_inc(s5_o, 1)

        def ssm_outputs_pool(pool, b):
            bf = bufs_ssm[b % 2]
            gs = slice(GB * b, GB * b + GB)
            link = lambda ins: link_pool(pool, ins)
            if b >= 2:
                pool.wait_ge(s5_y, b - 1)
            VV, VS, T = (bf[n] for n in ("VV", "VS", "T"))
            nc.gpsimd.memset(T[:, :, :], 0.0).then_inc(t_zero, 1)
            cut = lambda X, a, m: X[:, :, a * GROUP:(a + m) * GROUP]
            nc.gpsimd.tensor_copy(cut(VV, 0, 1), CA[:, gs, :])
            link(nc.gpsimd.tensor_copy(cut(VS, 0, 1), CB[:, gs, :]))
            for a, m, src, pr, pi in ((1, 1, 0, AR, SAI), (2, 2, 0, A2R, SA2I), (4, 4, 0, A4R, SA4I), (8, 1, 7, AR, SAI)):
                cmul(nc.gpsimd, link, cut(VV, a, m), cut(VS, a, m), cut(VV, src, m), cut(VS, src, m),
                     pr[:, gs], pi[:, gs], tmp_p, last=v_ready if a == 8 else None)

        def ssm_toeplitz_pool(pool, b):
            T = bufs_ssm[b % 2]["T"]
            pool.wait_ge(kk_d, b + 1)
            pool.wait_ge(t_zero, b + 1)
            for t in range(GT):
                w = (GT - t) * GROUP
                pool.dma_start(T[t * GROUP:(t + 1) * GROUP, :, t * GROUP:P],
                               kkb[0:GROUP, :, 0:w]).then_inc(t_in, 16)

        def ssm_step_pe(pe, n):
            b, s = divmod(n, NT)
            bf, zt = bufs_ssm[b % 2], ztb[:, b % 2]
            bank = [ps[:, 7, i * P:(i + 1) * P] for i in range(GB)]
            if s == 0:
                pe.wait_ge(nb_ready, b + 1)
                pe.wait_ge(v_ready, b + 1)
                if b:
                    pe.wait_ge(s5_g, b)
                for i in range(GB):
                    last = nc.tensor.matmul(bank[i][0:GROUP], nbb[:, i, :], bf["VV"][:, i, 0:P], start=True, stop=True)
                last.then_inc(kk_done, 1)
            elif s <= 3:
                if s == 1:
                    pe.wait_ge(zb_ready, b + 1)
                    pe.wait_ge(kk_out, b + 1)
                else:
                    pe.wait_ge(s5_cp, 3 * b + s - 1)
                if s == 3:
                    pe.wait_ge(ub_made, b + 1)
                src = (bf["Z"], bf["ZS"], ub)[s - 1]
                for i in range(GB):
                    last = nc.tensor.transpose(bank[i], src[:, i, :], ident[:, :])
                last.then_inc(s5_tr, 1)
            elif s <= 5:
                pe.wait_ge(*((s5_cp, 3 * b + 3) if s == 4 else (s5_m, 2 * b + 1)))
                for i in range(GB):
                    last = nc.tensor.matmul(bank[i], zt[:, s - 4, i * P:(i + 1) * P], zt[:, 2, i * P:(i + 1) * P],
                                            start=True, stop=True)
                last.then_inc(s5_s, 1)
            elif s == 7:
                pe.wait_ge(t_in, 16 * GT * (b + 1))
                pe.wait_ge(s5_o, b + 1)
                for i in range(GB):
                    nc.tensor.matmul(bank[i], zt[:, 2, i * P:(i + 1) * P], bf["T"][:, i, :], start=True, stop=False)
                    nc.tensor.matmul(bank[i], ob[:, 0, i, 0:P], bf["VV"][:, i, GROUP:9 * GROUP], start=False, stop=False)
                    last = nc.tensor.matmul(bank[i], ob[:, 1, i, 0:P], bf["VS"][:, i, GROUP:9 * GROUP], start=False,
                                            stop=True)
                last.then_inc(s5_y, 1)

        def group_columns(b):
            return U[:, :, 64 * b:64 * b + 64].rearrange("p t (g c) -> p g t c", g=GB)

        def ssm_inputs_act(act, b):
            if b:
                act.wait_ge(s5_tr, 3 * b)
            nc.scalar.activation(ub[:, :, :].rearrange("p g (t c) -> p g t c", t=GT), group_columns(b),
                                 ACT.Copy).then_inc(ub_made, 1)

        def ssm_step_act(act, n):
            b, s = divmod(n, NT)
            if s == 0:
                act.wait_ge(kk_done, b + 1)
                if b:
                    act.wait_ge(t_in, 16 * GT * b)
                nc.scalar.activation(kkb[0:GROUP, :, :].rearrange("p a b -> p (a b)"), ps[0:GROUP, 7, :],
                                     ACT.Copy).then_inc(kk_out, 1)
            elif s <= 3:
                act.wait_ge(s5_tr, 3 * b + s)
                if b >= 2:
                    act.wait_ge(s5_y, b - 1)
                nc.scalar.activation(ztb[:, b % 2, s - 1, :], ps[:, 7, :], ACT.Copy).then_inc(s5_cp, 1)
            elif s == 4 and b + 1 < NB:
                ssm_inputs_act(act, b + 1)
            elif s == 7:
                act.wait_ge(s5_y, b + 1)
                nc.scalar.activation(group_columns(b), ps[:, 7, :].rearrange("p (g t c) -> p g t c", g=GB, t=GT),
                                     ACT.Gelu_apprx_tanh).then_inc(s5_g, 1)

        def ssm_step_dve(dve, n, prepare):
            b, s = divmod(n, NT)
            if s == 2:
                ssm_skip_dve(dve, b)
            if s == 5:
                ssm_scan_dve(dve, b, 0)
            if s == 6:
                ssm_scan_dve(dve, b, 1)
            for _ in range(S5_PIECES[s]):
                next(prepare, None)

        S5_PIECES = (0, 2, 1, 1, 1, 1, 0, 2)

        yf = at("yf", OFF_XN, [4, S])
        YH = A[:, 4:8]
        glu_w = at("glu_w", OFF_ACC, [2, 2, UNIT], f32r)
        sg = at("sg", OFF_ACC + 16 * KB, [2, HALF])
        pr_ = at("pr", OFF_ACC + 20 * KB, [2, HALF])
        yt_tr, yt_f, yt_hi, yt_lo = (sem(s) for s in ("yt_tr", "yt_f", "yt_hi", "yt_lo"))
        gl_done, gl_s, gl_p, gl_hi, gl_lo = (sem(s) for s in ("gl_done", "gl_s", "gl_p", "gl_hi", "gl_lo"))

        def glu_unit(u):
            return U_GLU + u, glu_w[:, u], (at_s, NA)

        def eighths(X, half):
            return X.rearrange("p (c t) -> p t c", t=GT)[:, 4 * half:4 * half + 4, :]

        def glu_pe(pe):
            pe.wait_ge(s5_g, 8)
            for q in range(8):
                j, half = divmod(q, 2)
                if q >= 2:
                    pe.wait_ge(yt_f, q - 1)
                for t in range(4):
                    tt_ = 4 * half + t
                    last = nc.tensor.transpose(ps[:, 2 + q % 2, t * P:(t + 1) * P],
                                               U[:, tt_, j * P:(j + 1) * P], ident[:, :])
                last.then_inc(yt_tr, 1)
            pe.wait_ge(ot_lo, 8)
            pe.wait_ge(yt_lo, 8)
            pe.wait_ge(unit_ready, U_GLU + 2)
            for g in range(8):
                j, half = divmod(g, 2)
                if g >= 4:
                    pe.wait_ge(gl_s, g - 3)
                slot = glu_w[:, j // 2]
                for k in range(4):
                    c0 = (j % 2) * HALF + k * P
                    last = products(ps[:, (0, 1, 4, 5)[g % 4], :], lambda h: slot[:, h, c0:c0 + P],
                                    lambda h: YH[:, k, h, half * HALF:(half + 1) * HALF], k == 0, k == 3)
                last.then_inc(gl_done, 1)

        def glu_act(act):
            for q in range(8):
                j, half = divmod(q, 2)
                act.wait_ge(yt_tr, q + 1)
                nc.scalar.activation(eighths(yf[:, j, :], half), ps[:, 2 + q % 2, :].rearrange("p (t c) -> p t c", t=4),
                                     ACT.Copy).then_inc(yt_f, 1)
                if half:
                    act.wait_ge(yt_f, q + 1)
                    nc.scalar.activation(YH[:, j, 0, :], yf[:, j, :], ACT.Copy).then_inc(yt_hi, 1)
            for g in range(8):
                j, half = divmod(g, 2)
                act.wait_ge(gl_done, g + 1)
                if g >= 2:
                    act.wait_ge(gl_p, g - 1)
                nc.scalar.activation(sg[:, g % 2, :], ps[:, (0, 1, 4, 5)[g % 4], :], ACT.Sigmoid,
                                     bias=c_("b_glu", j)).then_inc(gl_s, 1)
                act.wait_ge(gl_p, g + 1)
                nc.scalar.activation(B[:, 4 + j, 0, half * HALF:(half + 1) * HALF], pr_[:, g % 2, :],
                                     ACT.Copy).then_inc(gl_hi, 1)

        def glu_dve(dve):
            for j in range(4):
                dve.wait_ge(yt_hi, j + 1)
                nc.vector.tensor_tensor(YH[:, j, 1, :], yf[:, j, :], YH[:, j, 0, :].bitcast(f32),
                                        ALU.subtract).then_inc(yt_lo, 2)
            for g in range(8):
                j, half = divmod(g, 2)
                cut = slice(half * HALF, (half + 1) * HALF)
                dve.wait_ge(gl_s, g + 1)
                if g >= 2:
                    dve.wait_ge(gl_lo, g - 1)
                nc.vector.tensor_tensor(pr_[:, g % 2, :], yf[:, j, cut], sg[:, g % 2, :], ALU.mult).then_inc(gl_p, 1)
                dve.wait_ge(gl_hi, g + 1)
                nc.vector.tensor_tensor(B[:, 4 + j, 1, cut], pr_[:, g % 2, :], B[:, 4 + j, 0, cut].bitcast(f32),
                                        ALU.subtract).then_inc(gl_lo, 1)

        dist = at("dist", OFF_A, [S])
        lmul = at("lmul", OFF_A + 4 * KB, [S])
        ib = at("ib", OFF_A + 48 * KB, [S], i32)
        ibf = at("ibf", OFF_A + 48 * KB, [S])
        xb_i = at("xb_i", OFF_A + 52 * KB, [S], i32)
        xb_f = at("xb_f", OFF_A + 52 * KB, [S])
        bias_h = at("bias_h", OFF_A + 8 * KB, [2, S])
        sco = at("sco", OFF_A + 16 * KB, [2, S])
        prob = at("prob", OFF_A + 24 * KB, [2, S])
        probT = at("probT", OFF_A + 32 * KB, [2, NT, P])
        O = at("att_o", OFF_A + 40 * KB, [NT, HALF])
        stats = at("stats", OFF_B + 31 * KB, [4, N_HEADS * NT])
        mx_, nm_, den_, rd_ = (stats[:, i, :] for i in range(4))
        io_done = sem("io_done")
        at_s, at_m, at_n, at_e, at_tr, at_pt, at_pv, at_r, at_o = (sem(f"at_{s}") for s in (
            "s", "m", "n", "e", "tr", "pt", "pv", "r", "o"))
        ot_tr, ot_hi, ot_lo = sem("ot_tr"), sem("ot_hi"), sem("ot_lo")
        NA = N_HEADS * NT

        def bias_dve(dve, cut):
            ts, tt, stt = nc.vector.tensor_scalar, nc.vector.tensor_tensor, nc.vector.scalar_tensor_tensor
            link = lambda ins: link_dve(dve, ins)
            dve.wait_ge(io_done, 1)
            d, L, xi, x_, y_ = dist[:, cut], lmul[:, cut], xb_i[:, cut], xb_f[:, cut], ibf[:, cut]
            link(nc.vector.tensor_copy(d, ib[:, cut]))
            link(ts(xi, ib[:, cut], 3, None, ALU.bitwise_and))
            link(ts(L, xi, 0.0, None, ALU.is_equal))
            link(stt(out=L, in0=d, scalar=512.0, in1=L, op0=ALU.is_le, op1=ALU.mult))
            link(stt(out=L, in0=d, scalar=128.0, in1=L, op0=ALU.is_le, op1=ALU.add))
            link(ts(xi, ib[:, cut], 15, None, ALU.bitwise_and))
            link(stt(out=L, in0=xi, scalar=0.0, in1=L, op0=ALU.is_equal, op1=ALU.add))
            link(stt(out=L, in0=d, scalar=0.0, in1=L, op0=ALU.is_ge, op1=ALU.mult))
            link(ts(x_, L, 2.0, math.log(2.0), ALU.is_ge, ALU.mult))
            link(ts(y_, L, 3.0, math.log(1.5), ALU.is_ge, ALU.mult))
            link(tt(x_, x_, y_, ALU.add))
            link(ts(y_, L, 1.0, -1e30, ALU.is_lt, ALU.mult))
            link(tt(L, x_, y_, ALU.add))

        def att_pe(pe):
            def scores(n):
                h, i = divmod(n, NT)
                rows_ = slice(64 * (h % 2), 64 * (h % 2) + 64)
                W = (i + 1) * P
                if n >= 2:
                    pe.wait_ge(at_m, n - 1)
                for c0 in range(0, W, HALF):
                    w = min(HALF, W - c0)
                    last = nc.tensor.matmul(ps[:, 2 * (n % 2) + c0 // HALF, 0:w], QK[rows_, h // 2, i * P:(i + 1) * P],
                                            QK[rows_, 4 + h // 2, c0:c0 + w], start=True, stop=True)
                last.then_inc(at_s, 1)

            def transposes(n):
                i = n % NT
                pe.wait_ge(at_e, n + 1)
                if n:
                    pe.wait_ge(at_pt, n)
                for k in range(i + 1):
                    last = nc.tensor.transpose(ps[:, 4 + k // 4, (k % 4) * P:(k % 4 + 1) * P],
                                               prob[:, n % 2, k * P:(k + 1) * P], ident[:, :])
                last.then_inc(at_tr, 1)

            def values(n):
                h, i = divmod(n, NT)
                pe.wait_ge(at_pt, n + 1)
                if n:
                    pe.wait_ge(at_o, n)
                for k in range(i + 1):
                    last = nc.tensor.matmul(ps[:, 6, 0:HEAD_DIM], probT[:, n % 2, k, :],
                                            V[:, k, h * HEAD_DIM:(h + 1) * HEAD_DIM], start=k == 0, stop=k == i)
                last.then_inc(at_pv, 1)

            pe.wait_ge(qk_out, 16)
            pe.wait_ge(u_out, GT)
            scores(0)
            scores(1)
            for n in range(NA):
                if n + 2 < NA:
                    scores(n + 2)
                transposes(n)
                ssm_step_pe(pe, n)
                if n:
                    values(n - 1)
            values(NA - 1)
            pe.wait_ge(at_o, NA)
            for q in range(8):
                j, half = divmod(q, 2)
                if q >= 2:
                    pe.wait_ge(ot_lo, q - 1)
                for t in range(4):
                    last = nc.tensor.transpose(ps[:, q % 2, t * P:(t + 1) * P],
                                               O[:, 4 * half + t, j * P:(j + 1) * P], ident[:, :])
                last.then_inc(ot_tr, 1)

        def att_act(act):
            def rest(n):
                i = n % NT
                act.wait_ge(at_tr, n + 1)
                if n >= 2:
                    act.wait_ge(at_pv, n - 1)
                w = (i + 1) * P
                nc.scalar.activation(probT[:, n % 2, 0:i + 1, :].rearrange("p a b -> p (a b)"),
                                     ps[:, 4:6, :].rearrange("p a b -> p (a b)")[:, 0:w], ACT.Copy).then_inc(at_pt, 1)

            act.wait_ge(u_out, GT)
            ssm_inputs_act(act, 0)
            for n in range(NA):
                w = (n % NT + 1) * P
                act.wait_ge(at_n, n + 1)
                if n >= 2:
                    act.wait_ge(at_tr, n - 1)
                nc.scalar.activation(prob[:, n % 2, 0:w], sco[:, n % 2, 0:w], ACT.Exp, bias=nm_[:, n:n + 1],
                                     accum_out=den_[:, n:n + 1]).then_inc(at_e, 1)
                if n:
                    rest(n - 1)
                    ssm_step_act(act, n - 1)
            rest(NA - 1)
            ssm_step_act(act, NA - 1)
            for u in range(2):
                hi_of(act, glu_unit(u))
            for q in range(8):
                j, half = divmod(q, 2)
                act.wait_ge(ot_tr, q + 1)
                nc.scalar.activation(B[:, j, 0, half * HALF:(half + 1) * HALF], ps[:, q % 2, :],
                                     ACT.Copy).then_inc(ot_hi, 1)

        def att_dve(dve):
            link = lambda ins: link_dve(dve, ins)

            def head_bias(h, cut=slice(0, S)):
                nc.vector.scalar_tensor_tensor(out=bias_h[:, h % 2, cut], in0=dist[:, cut], scalar=-2.0 ** (-(h + 1.0)),
                                               in1=lmul[:, cut], op0=ALU.mult, op1=ALU.add).then_inc(dve_chain, 1)
                chained["dve"] += 1
                return chained["dve"]

            def maximum(n, made):
                h, i = divmod(n, NT)
                w = (i + 1) * P
                if i == 0:
                    dve.wait_ge(dve_chain, made)
                dve.wait_ge(at_s, n + 1)
                if n >= 2:
                    dve.wait_ge(at_e, n - 1)
                b = 2 * (n % 2)
                nc.vector.tensor_tensor_reduce(out=sco[:, n % 2, 0:w],
                                               in0=ps[:, b:b + 2, :].rearrange("p a b -> p (a b)")[:, 0:w],
                                               in1=bias_h[:, h % 2, S - w:S], scale=1.0, scalar=-3e38, op0=ALU.add,
                                               op1=ALU.max, accum_out=mx_[:, n:n + 1]).then_inc(at_m, 1)
                dve.wait_ge(at_m, n + 1)
                nc.vector.tensor_scalar(nm_[:, n:n + 1], mx_[:, n:n + 1], -1.0, None, ALU.mult).then_inc(at_n, 1)

            def finish(n):
                h, i = divmod(n, NT)
                dve.wait_ge(at_e, n + 1)
                nc.vector.reciprocal(rd_[:, n:n + 1], den_[:, n:n + 1]).then_inc(at_r, 1)
                dve.wait_ge(at_r, n + 1)
                dve.wait_ge(at_pv, n + 1)
                nc.vector.tensor_scalar(O[:, i, h * HEAD_DIM:(h + 1) * HEAD_DIM], ps[:, 6, 0:HEAD_DIM],
                                        rd_[:, n:n + 1], None, ALU.mult).then_inc(at_o, 1)

            near, far = slice(HALF, S), slice(0, HALF)
            bias_dve(dve, near)
            made = [head_bias(0, near)]
            maximum(0, made[0])
            for n in range(NA):
                if n % NT == 0:
                    prepare = ssm_prepare_dve(dve, n // NT + 1) if n // NT + 1 < NB else iter(())
                if n == 3:
                    dve.wait_ge(dve_chain, made[0])
                if n >= 2:
                    finish(n - 2)
                if n + 1 < NA:
                    maximum(n + 1, made[(n + 1) // NT])
                if n == 1:
                    bias_dve(dve, far)
                    made[0] = head_bias(0, far)
                if n == 4:
                    made.append(head_bias(1))
                if n % NT == NT - 1 and n // NT + 2 < N_HEADS:
                    made.append(head_bias(n // NT + 2))
                ssm_step_dve(dve, n, prepare)
            finish(NA - 2)
            finish(NA - 1)
            for u in range(2):
                lo_of(dve, glu_unit(u))
            for q in range(8):
                j, half = divmod(q, 2)
                dst = B[:, j, :, half * HALF:(half + 1) * HALF]
                dve.wait_ge(ot_hi, q + 1)
                nc.vector.tensor_tensor(dst[:, 1, :], ps[:, q % 2, :], dst[:, 0, :].bitcast(f32),
                                        ALU.subtract).then_inc(ot_lo, 1)

        mix_out = sem("mix_out")
        mixo = Wide("mixo", B, [A[:, u] for u in range(8)], U_MIXO,
                    lambda u: (at_pv, NA) if u < 4 else (gl_done, 8), mix_out)
        n_ffn2 = Norm("g_ffn2", B, lambda t: (mix_out, NT + t + 1), post=1, residual=True)
        n_ffn2.gb_count, n_ffn2.old_count, n_ffn2.factor, n_ffn2.kept = 2, 4, 1.0, x_mid[2]
        ffn2 = Feed(D_FF2 // P // CHUNK, True, B, A, U_FFN2, (mixo.done, NT), False)
        ffn2.acc_stored = mid_stored[2]
        n_last = Norm(None, None, lambda t: ffn2.at("de", NT * (ffn2.n - 1) + t + 1), post=0, residual=True, final=True)
        n_last.gb_count, n_last.old_count, n_last.factor, n_last.kept = 3, 8, 0.5, out
        N_UNITS = ffn2.last_n

        def dve_mixo(dve, hooks):
            for g in range(2 * NT):
                half, t = divmod(g, NT)
                dve.wait_ge(mixo.done, g + 1)
                nc.vector.tensor_copy(acc[:, t, half * HALF:(half + 1) * HALF], ps[:, g % 6, :]).then_inc(mix_out, 1)
                hooks.get(g - NT, lambda: None)()

        block = ctx.enter_context(nc.Block())
        ffn1.acc_stored = mid_stored[0]
        assert N_UNITS % 2 == 0

        @block.sync
        def _(sp):
            for r in range(2):
                sp.dma_start(raw[:, r, :], stream[r, :, :]).then_inc(raw_full[r], 16)
            with sp.Fori(1, N_UNITS // 2) as i:
                for r in range(2):
                    sp.wait_ge(unit_ready, 2 * i + r - 1)
                    sp.dma_start(raw[:, r, :], stream[bass.ds(2 * i + r, 1), :, :].rearrange("a p n -> (a p) n")
                                 ).then_inc(raw_full[r], 16)

        def keep_rows(pool, N, k):
            for t in range(NT):
                pool.wait_ge(*N.at("res", t + 1))
                pool.dma_start(x_mid[k, t * P:(t + 1) * P, :], acc[:, t, :]).then_inc(mid_out, 16)

        def old_rows_again(pool, N, k):
            pool.wait_ge(mid_out, mid_stored[k])
            for t in range(NT):
                if t >= 2:
                    pool.wait_ge(*N.at("res", t - 1))
                pool.dma_start(old[:, t % 2, :], x_mid[k, t * P:(t + 1) * P, :]).then_inc(old_in[t % 2], 16)
                if t >= 1:
                    pool.wait_ge(*N.at("res", t))
                    pool.dma_start(N.kept[(t - 1) * P:t * P, :], acc[:, t - 1, :]).then_inc(mid_out, 16)
            pool.wait_ge(*N.at("res", NT))
            pool.dma_start(N.kept[(NT - 1) * P:NT * P, :], acc[:, NT - 1, :]).then_inc(mid_out, 16)

        @block.gpsimd
        def _(pool):
            pool.dma_start(col[:, :], cols).then_inc(params_in, 16)
            for i in range(2):
                pool.dma_start(acc[:, 4 * i:4 * i + 4, :],
                               x[i * HALF:(i + 1) * HALF, :].rearrange("(t p) d -> p t d", p=P)).then_inc(x_in[i], 16)
            pool.dma_start(gate_w[:, :, :], gate_mats).then_inc(mats_in, 16)
            pool.dma_start(pool_w[:, :, :], pool_mats).then_inc(mats_in, 16)
            pool.dma_start(inv_cnt[:, :, :], inv_count).then_inc(mats_in, 16)
            nc.gpsimd.memset(ident[:, :], 0.0).then_inc(ident_made, 1)
            pool.wait_ge(ident_made, 1)
            nc.gpsimd.affine_select(out=ident[:, :], in_=ident[:, :], compare_op=ALU.not_equal, fill=1.0, base=0,
                                    pattern=[[-1, P]], channel_multiplier=1).then_inc(ident_made, 1)
            pool.wait_ge(gates_done, 16)
            pool.wait_ge(poolmm_done, 8)
            pool.wait_ge(d_ready, 4)
            for g in range(2 * NT):
                half, t = divmod(g, NT)
                if g >= 4:
                    pool.wait_ge(res1, g - 3)
                pool.dma_start(rold[:, g % 4, :], x[t * P:(t + 1) * P, half * HALF:(half + 1) * HALF]
                               ).then_inc(old_rows[g % 4], 16)
            pool.wait_ge(res1, 2 * NT)
            pool.dma_start(praw[:, :, :], p.rearrange("(t p) d -> p t d", p=P)).then_inc(p_in, 16)
            pool.dma_start(gb[:, 0, :], rows[0, :, :]).then_inc(gb_in[0], 16)
            pool.dma_start(gb[:, 1, :], rows[1, :, :]).then_inc(gb_in[1], 16)
            keep_rows(pool, n_fin, 0)
            pool.wait_ge(ple_res, 2 * NT)
            pool.dma_start(gb[:, 0, :], rows[2, :, :]).then_inc(gb_in[0], 16)
            old_rows_again(pool, n_mix2, 0)
            pool.wait_ge(*n_mix2.at("res", NT))
            pool.dma_start(params_g[0:N_GROUPS, :], ssm_g).then_inc(g_in, 16)
            pool.wait_ge(v_done, NT)
            pool.dma_start(ssm_in[:, :], ssm_bc).then_inc(s_in, 16)
            pool.wait_ge(s_in, 16)
            pool.wait_ge(pw_ready, 1)
            ssm_outputs_pool(pool, 0)
            pool.wait_ge(u_done, GT)
            nc.gpsimd.iota(ib[:, :], [[-1, S]], base=S - P, channel_multiplier=1).then_inc(io_done, 1)
            for b in range(NB):
                if b + 1 < NB:
                    ssm_outputs_pool(pool, b + 1)
                ssm_toeplitz_pool(pool, b)
            pool.wait_ge(yt_tr, 8)
            pool.dma_start(gb[:, 1, :], rows[3, :, :]).then_inc(gb_in[1], 16)
            pool.dma_start(gb[:, 0, :], rows[4, :, :]).then_inc(gb_in[0], 16)
            old_rows_again(pool, n_ffn2, 1)
            old_rows_again(pool, n_last, 2)
            pool.wait_ge(mid_out, 16 * NT * 4)

        @block.scalar
        def _(act):
            act.wait_ge(params_in, 16)
            act.wait_ge(eps_made, 1)
            act_mix1(act)
            wide_hi(act, w_out, range(8))
            norm_act(act, n_mlp, 0)
            first_hi(act, mlp)
            norm_act(act, n_mlp, 1)
            feed_on_act(act, mlp)
            ple_hi(act, 0, 4)
            norm_act(act, n_ple, 0)
            ple_hi(act, 4, 6)
            ple_act_p(act)
            norm_act(act, n_ple, 1)
            ple_act(act, 0, NT)
            ple_hi(act, 6, 10)
            ple_act(act, NT, NT + 4)
            norm_act_rows(act, n_fin, 0)
            ple_act(act, NT + 4, NT + 7)
            norm_act_split(act, n_fin, 0)
            ple_act(act, NT + 7, 2 * NT)
            first_hi(act, ffn1)
            norm_act(act, n_fin, 1)
            feed_on_act(act, ffn1)
            hi_of(act, qk_unit(0))
            hi_of(act, qk_unit(1))
            norm_act(act, n_mix2, 0)
            hi_of(act, qk_unit(2))
            hi_of(act, qk_unit(3))
            norm_act(act, n_mix2, 1)
            proj_act(act)
            ssm_params_act(act)
            att_act(act)
            glu_act(act)
            wide_hi(act, mixo, range(8))
            norm_act(act, n_ffn2, 0)
            first_hi(act, ffn2)
            norm_act(act, n_ffn2, 1)
            feed_on_act(act, ffn2)
            norm_act(act, n_last, 0)
            norm_act(act, n_last, 1)

        @block.vector
        def _(dve):
            dve.wait_ge(params_in, 16)
            dve.wait_ge(mats_in, 48)
            dve_mix1(dve)
            wide_lo(dve, w_out, range(8))
            dve_out1(dve, {**norm_dve_hooks(dve, n_mlp)})
            first_lo(dve, mlp)
            norm_dve(dve, n_mlp, 1)
            hooks = norm_dve_hooks(dve, n_ple)
            hooks[2] = lambda: ple_lo(dve, 0, 4)
            feed_on_dve(dve, mlp, hooks)
            ple_lo(dve, 4, 6)
            ple_dve_p(dve)
            norm_dve(dve, n_ple, 1)
            ple_dve(dve, norm_dve_hooks(dve, n_fin))
            first_lo(dve, ffn1)
            norm_dve(dve, n_fin, 1)
            hooks = norm_dve_hooks(dve, n_mix2)
            hooks[2] = lambda: [lo_of(dve, qk_unit(m)) for m in range(2)]
            feed_on_dve(dve, ffn1, hooks)
            for m in range(2, 4):
                lo_of(dve, qk_unit(m))
            norm_dve(dve, n_mix2, 1)
            proj_dve(dve)
            att_dve(dve)
            glu_dve(dve)
            wide_lo(dve, mixo, range(8))
            dve_mixo(dve, norm_dve_hooks(dve, n_ffn2))
            first_lo(dve, ffn2)
            norm_dve(dve, n_ffn2, 1)
            feed_on_dve(dve, ffn2, norm_dve_hooks(dve, n_last))
            norm_dve(dve, n_last, 1)

        @block.tensor
        def _(pe):
            pe.wait_ge(ident_made, 2)
            norm_pe(pe, n_first, 0)
            pe_mix1(pe)
            wide_pe(pe, w_out, lambda h: pe.wait_ge(cat_lo, 8), norm=n_mlp)
            feed_pe(pe, mlp, {("before", 0): lambda: pe.wait_ge(*n_mlp.at("lo", 8)),
                              ("after", 0): lambda: norm_pe(pe, n_mlp, 1),
                              ("before", 1): lambda: pe.wait_ge(*n_mlp.at("lo", 16))},
                    {6: lambda: norm_pe(pe, n_ple, 0)})
            ple_pe(pe, n_fin)
            feed_pe(pe, ffn1, {("before", 0): lambda: pe.wait_ge(*n_fin.at("lo", 8)),
                               ("after", 0): lambda: norm_pe(pe, n_fin, 1),
                               ("before", 1): lambda: pe.wait_ge(*n_fin.at("lo", 16))},
                    {6: lambda: norm_pe(pe, n_mix2, 0)})
            proj_pe(pe)
            att_pe(pe)
            glu_pe(pe)
            wide_pe(pe, mixo, lambda h: pe.wait_ge(gl_lo, 8), norm=n_ffn2)
            feed_pe(pe, ffn2, {("before", 0): lambda: pe.wait_ge(*n_ffn2.at("lo", 8)),
                               ("after", 0): lambda: norm_pe(pe, n_ffn2, 1),
                               ("before", 1): lambda: pe.wait_ge(*n_ffn2.at("lo", 16))}, {})


def pack(i):
    import numpy as np
    f = lambda n: np.asarray(i[n])

    def tall(w):
        K, N = w.shape
        u = w.reshape(K // P, P, N // P, P).transpose(2, 1, 0, 3)
        return u.reshape(-1, P, UNIT)

    def wide(w):
        u = w.reshape(4, 2, P, w.shape[1] // HALF, HALF).transpose(3, 0, 2, 1, 4)
        return u.reshape(-1, P, UNIT)

    def down(w):
        return w.reshape(-1, P, UNIT)

    def feed(up, dn, nU):
        n = dn.shape[0] // CHUNK
        out = [up[0], up[1]]
        nxt = 2
        for c in range(n):
            for j in range(nU):
                if j == nU - 2 and c:
                    out += [dn[CHUNK * (c - 1)], dn[CHUNK * (c - 1) + 1]]
                if nxt < len(up):
                    out.append(up[nxt])
                    nxt += 1
        out += [dn[-2], dn[-1]]
        return np.stack(out)

    def gated(w):
        u = tall(w)
        n = len(u) // 2
        return np.stack([u[:n], u[n:]], axis=1).reshape(-1, P, UNIT)

    w_mix = f("w_mix_in_2")[0]
    glu = f("w_glu_2")[0].reshape(4, P, 2, 2, P).transpose(2, 1, 3, 0, 4).reshape(2, P, UNIT)
    w_in = tall(f("w_in")[0])
    order = [k for j in range(4) for k in (4 + j, 8 + j, j)]
    parts = [w_in[order], wide(f("w_out")[0]),
             feed(tall(f("w_up")[0]), down(f("w_down")[0]), CHUNK),
             down(f("w_ple_proj")[0]), wide(f("w_ple_gate")[0]),
             feed(gated(f("ffn1_w_in_2")[0]), down(f("ffn1_w_out_2")[0]), 2 * CHUNK),
             tall(w_mix[:, :1024]), wide(w_mix[:, 1024:]), glu,
             wide(f("w_mix_out_2")[0]),
             feed(gated(f("ffn2_w_in_2")[0]), down(f("ffn2_w_out_2")[0]), 2 * CHUNK)]
    stream = np.concatenate(parts)
    colsd = {
        "g_mix": f("norm_mix_g")[0].reshape(8, P), "g_mlp": f("norm_mlp_g")[0].reshape(8, P),
        "g_ple": f("norm_ple_g")[0].reshape(8, P), "g_ffn1": f("ffn1_pre_g_2")[0].reshape(8, P),
        "g_mix2": f("mix_pre_g_2")[0].reshape(8, P), "g_ffn2": f("ffn2_pre_g_2")[0].reshape(8, P),
        "pool_b": f("pool_b")[0], "pool_scale": f("pool_scale")[0].reshape(4, P),
        "conv_w": f("conv_w")[0].reshape(16, P), "conv_b": f("conv_b")[0].reshape(4, P),
        "gate_a_b": f("gate_a_b")[0].reshape(4, P), "gate_x_b": f("gate_x_b")[0].reshape(4, P),
        "lru_L": f("lru_L")[0].reshape(4, P), "b_glu": f("b_glu_2")[0].reshape(4, P),
        "sgn": np.repeat(np.array([-1.0, 1.0], np.float32), 64)[None],
    }
    cols = np.ascontiguousarray(np.concatenate([colsd[k] for k in COLS]).T)
    gate_mats = np.zeros((P, 8, P), np.float32)
    for kind, name in enumerate(("gate_a_w", "gate_x_w")):
        w = f(name)[0]
        for j in range(4):
            for q in range(2):
                gate_mats[64 * q:64 * q + 64, 4 * kind + j, 64 * q:64 * q + 64] = w[2 * j + q]
    pool_mats = np.ascontiguousarray(f("pool_w")[0].transpose(1, 0, 2))
    rows = np.stack([np.broadcast_to(f(n).reshape(1, D), (P, D)) for n in
                     ("b_ple_gate", "norm_final_g", "ffn1_post_g_2", "mix_post_g_2", "ffn2_post_g_2")])
    twice = lambda a: np.concatenate([a, a], axis=-1)
    ssm_g = np.concatenate([twice(f("a_re_2")[0]), twice(f("a_im_2")[0]), f("log_dt_2")[0][:, None]], axis=1)
    bre, bim = (f(n)[0].transpose(1, 0, 2).reshape(STATE, -1) for n in ("b_re_2", "b_im_2"))
    cre, cim = (f(n)[0].transpose(2, 0, 1).reshape(STATE, -1) for n in ("c_re_2", "c_im_2"))
    skip = np.zeros((P, N_GROUPS), np.float32)
    skip[:GROUP] = f("d_skip_2")[0].reshape(N_GROUPS, GROUP).T
    ssm_bc = np.concatenate([np.concatenate([bre, bim]), np.concatenate([bim, bre]), np.concatenate([cre, cim]),
                             np.concatenate([cim, cre]), skip], axis=1)
    inv_count = np.zeros((P, 4, 16), np.float32)
    for j, w in enumerate(WINDOWS):
        inv_count[:, j, :w] = 1.0 / np.arange(1, w + 1)
    return dict(x=f("x")[0], p=f("p")[0, 0], stream=stream, cols=cols, rows=rows, gate_mats=gate_mats,
                pool_mats=pool_mats, inv_count=inv_count, ssm_g=ssm_g, ssm_bc=ssm_bc)


def kernel(**inputs):
    import numpy as np
    from concourse import bacc
    from concourse.bass_utils import run_bass_kernel_spmd

    packed = pack(inputs)
    nc = bacc.Bacc("TRN2", target_bir_lowering=False, num_devices=1)
    f32 = mybir.dt.float32
    aps = {n: nc.dram_tensor(n, a.shape, f32, kind="ExternalInput").ap() for n, a in packed.items()}
    x_mid = nc.dram_tensor("x_mid", (3, S, D), f32, kind="Internal").ap()
    out = nc.dram_tensor("out", (S, D), f32, kind="ExternalOutput").ap()
    program(nc, x_mid=x_mid, out=out, **aps)
    r = run_bass_kernel_spmd(nc, [packed], core_ids=[0])
    return np.asarray(r.results[0]["out"]).reshape(1, S, D)
```

```python
import concourse.bass as bass
from concourse import mybir
from contextlib import ExitStack
import math

P = 128
S = 1024
D = 1024
NT = S // P
KD = D // P
HALF = 512
UNIT = 1024
EPS = 1e-6
SBUF_BASE = 16512
D_FF1 = 4096
D_FF2 = 2816
CHUNK = 2
LRU_C = 8.0
N_HEADS = 8
HEAD_DIM = 64
N_GROUPS = 32
GROUP = 16
STATE = 64
GT = 8
WINDOWS = (2, 4, 8, 16)

COLS = {}


def _columns():
    at = 0
    for name, n in (("g_mix", 8), ("g_mlp", 8), ("g_ple", 8), ("g_ffn1", 8), ("g_mix2", 8), ("g_ffn2", 8),
                    ("pool_b", 4), ("pool_scale", 4), ("conv_w", 16), ("conv_b", 4), ("gate_a_b", 4),
                    ("gate_x_b", 4), ("lru_L", 4), ("b_glu", 4), ("sgn", 1)):
        COLS[name] = at
        at += n
    return at


NCOLS = _columns()


def program(nc, x, p, stream, cols, rows, gate_mats, pool_mats, inv_count, ssm_g, ssm_bc, x_mid, out):
    f32 = mybir.dt.float32
    f32r = mybir.dt.float32r
    i32 = mybir.dt.int32
    ALU = mybir.AluOpType
    ACT = mybir.ActivationFunctionType

    ctx = ExitStack()
    with ctx:
        def at(name, offset, shape, dt=f32):
            return nc.alloc_sbuf_tensor_at(name, [P] + shape, dt, offset=SBUF_BASE + offset)

        def sem(name):
            return ctx.enter_context(nc.semaphore(name))

        KB = 1024
        OFF_A, OFF_B, OFF_ACC, OFF_XN = 0, 64 * KB, 128 * KB, 160 * KB
        OFF_RAW, OFF_GB, OFF_ROLD, OFF_ID = 176 * KB, 184 * KB, 192 * KB, 200 * KB
        whole = ctx.enter_context(nc.sbuf_tensor("whole", [P, 206 * KB], mybir.dt.uint8))
        A = at("region_a", OFF_A, [8, 2, UNIT], f32r)
        B = at("region_b", OFF_B, [8, 2, UNIT], f32r)
        acc = at("acc", OFF_ACC, [NT, D])
        xn = at("xn", OFF_XN, [4, D])
        raw = at("raw", OFF_RAW, [2, UNIT])
        gb = at("gb", OFF_GB, [2, D])
        rold = at("rold", OFF_ROLD, [4, HALF])
        ident = at("ident", OFF_ID, [P])
        col = at("col", OFF_ID + 512, [NCOLS])
        small = at("small", OFF_ID + 1024, [128])
        ps = ctx.enter_context(nc.psum_tensor("ps", [P, 8, HALF], f32))

        def c_(name, j=0):
            k = COLS[name] + j
            return col[:, k:k + 1]

        eps = small[:, 0:1]
        ss_pre, rms_pre, rinv_pre = small[:, 8:16], small[:, 16:24], small[:, 24:32]
        ss_post, rms_post, rinv_post = small[:, 32:40], small[:, 40:48], small[:, 48:56]
        c_pos, c_neg = small[:, 56:60], small[:, 60:64]
        lr = [small[:, 64 + 4 * i:68 + 4 * i] for i in range(6)]

        params_in = sem("params_in")
        x_in = [sem(f"x_in{t}") for t in range(NT)]
        ident_made = sem("ident_made")
        eps_made = sem("eps_made")
        raw_full = [sem(f"raw_full{i}") for i in range(2)]
        hi_done = sem("hi_done")
        unit_ready = sem("unit_ready")
        dve_chain = sem("dve_chain")
        act_chain = sem("act_chain")
        chained = {"dve": 0, "act": 0}

        def link_dve(dve, ins):
            chained["dve"] += 1
            ins.then_inc(dve_chain, 1)
            dve.wait_ge(dve_chain, chained["dve"])

        def link_act(act, ins):
            chained["act"] += 1
            ins.then_inc(act_chain, 1)
            act.wait_ge(act_chain, chained["act"])

        def make_hi(act, n, slot, free, odd):
            act.wait_ge(raw_full[odd], 8 * (n - odd) + 16)
            if free:
                act.wait_ge(*free)
            nc.scalar.activation(slot[:, 0, :], raw[:, odd, :], ACT.Copy).then_inc(hi_done, 1)

        def make_lo(dve, n, slot, odd):
            dve.wait_ge(hi_done, n + 1)
            nc.vector.tensor_tensor(slot[:, 1, :], raw[:, odd, :], slot[:, 0, :].bitcast(f32),
                                    ALU.subtract).then_inc(unit_ready, 1)

        def products(psum, lhs, rhs, first, last):
            nc.tensor.matmul(psum, lhs(0), rhs(0), start=first, stop=False)
            nc.tensor.matmul(psum, lhs(0), rhs(1), start=False, stop=False)
            return nc.tensor.matmul(psum, lhs(1), rhs(0), start=False, stop=last)

        shared, taken = {}, {}

        def take(user, counts):
            kind = type(user).__name__.lower()
            user.base.update({s: taken.get((kind, s), 0) for s in counts})
            for s, total in counts.items():
                if (kind, s) not in shared:
                    shared[kind, s] = sem(f"{kind}_{s}")
                user.sem[s] = shared[kind, s]
                taken[kind, s] = taken.get((kind, s), 0) + total

        class Norm:

            def __init__(self, gain, Z, acc_ready, post=None, residual=False, final=False):
                self.gain, self.Z, self.acc_ready, self.post = gain, Z, acc_ready, post
                self.residual, self.final = residual, final
                self.base, self.sem = {}, {}
                if post is not None:
                    take(self, dict(psq=NT, prms=2, prinv=2, ptmp=NT if residual else 0, res=NT))
                if not final:
                    take(self, dict(sq=NT, rms=2, rinv=2, xn=NT, tr=2 * KD, hi=2 * KD, lo=2 * KD))

            def at(self, s, count):
                return self.sem[s], self.base[s] + count

        def norm_act_post(act, N, hf):
            for t in range(4 * hf, 4 * hf + 4):
                act.wait_ge(*N.acc_ready(t))
                if not N.residual and hf and t == 4:
                    act.wait_ge(*N.at("res", 4))
                    if not N.final:
                        act.wait_ge(*N.at("tr", 8))
                nc.scalar.activation(N.squares(t) if N.residual else xn[:, t % 4, :], acc[:, t, :], ACT.Square,
                                     accum_out=ss_post[:, t:t + 1]).then_inc(N.sem["psq"], 1)
            act.wait_ge(*N.at("psq", 4 * hf + 4))
            nc.scalar.activation(rms_post[:, 4 * hf:4 * hf + 4], ss_post[:, 4 * hf:4 * hf + 4], ACT.Sqrt,
                                 bias=eps, scale=1.0 / D).then_inc(N.sem["prms"], 1)

        def norm_dve_post(dve, N, hf, rows=range(4)):
            g = gb[:, N.post, :]
            if 0 in rows:
                dve.wait_ge(gb_in[N.post], 16 * N.gb_count)
                dve.wait_ge(*N.at("prms", hf + 1))
                nc.vector.reciprocal(rinv_post[:, 4 * hf:4 * hf + 4],
                                     rms_post[:, 4 * hf:4 * hf + 4]).then_inc(N.sem["prinv"], 1)
                dve.wait_ge(*N.at("prinv", hf + 1))
            for t in [4 * hf + k for k in rows]:
                if not N.residual:
                    nc.vector.scalar_tensor_tensor(out=acc[:, t, :], in0=acc[:, t, :],
                                                   scalar=rinv_post[:, t:t + 1], in1=g,
                                                   op0=ALU.mult, op1=ALU.mult).then_inc(N.sem["res"], 1)
                else:
                    nc.vector.scalar_tensor_tensor(out=xn[:, t % 4, :], in0=acc[:, t, :],
                                                   scalar=rinv_post[:, t:t + 1], in1=g,
                                                   op0=ALU.mult, op1=ALU.mult).then_inc(N.sem["ptmp"], 1)
                    dve.wait_ge(*N.at("ptmp", t + 1))
                    dve.wait_ge(old_in[t % 2], 16 * (N.old_count + t // 2 + 1))
                    nc.vector.scalar_tensor_tensor(out=acc[:, t, :], in0=xn[:, t % 4, :], scalar=N.factor,
                                                   in1=old[:, t % 2, :], op0=ALU.mult,
                                                   op1=ALU.add).then_inc(N.sem["res"], 1)

        def norm_act_stats(act, N, hf):
            for t in range(4 * hf, 4 * hf + 4):
                if N.post is not None:
                    act.wait_ge(*N.at("res", t + 1))
                else:
                    act.wait_ge(*N.acc_ready(t))
                if hf and t == 4 and not N.residual:
                    act.wait_ge(*N.at("tr", 8))
                nc.scalar.activation(N.squares(t) if N.residual else xn[:, t % 4, :], acc[:, t, :], ACT.Square,
                                     accum_out=ss_pre[:, t:t + 1]).then_inc(N.sem["sq"], 1)
            act.wait_ge(*N.at("sq", 4 * hf + 4))
            nc.scalar.activation(rms_pre[:, 4 * hf:4 * hf + 4], ss_pre[:, 4 * hf:4 * hf + 4], ACT.Sqrt,
                                 bias=eps, scale=1.0 / D).then_inc(N.sem["rms"], 1)

        def norm_act_split(act, N, hf):
            for d in range(KD):
                act.wait_ge(*N.at("tr", 8 * hf + d + 1))
                nc.scalar.activation(N.Z[:, d, 0, hf * HALF:(hf + 1) * HALF], ps[:, 6 + d % 2, :], ACT.Copy,
                                     scale=c_(N.gain, d)).then_inc(N.sem["hi"], 1)

        def norm_dve_scale(dve, N, hf):
            dve.wait_ge(*N.at("rms", hf + 1))
            nc.vector.reciprocal(rinv_pre[:, 4 * hf:4 * hf + 4],
                                 rms_pre[:, 4 * hf:4 * hf + 4]).then_inc(N.sem["rinv"], 1)
            dve.wait_ge(*N.at("rinv", hf + 1))
            for t in range(4 * hf, 4 * hf + 4):
                nc.vector.tensor_scalar(xn[:, t % 4, :], acc[:, t, :], rinv_pre[:, t:t + 1], None,
                                        ALU.mult).then_inc(N.sem["xn"], 1)

        def norm_dve_split(dve, N, hf):
            for d in range(KD):
                z = N.Z[:, d, :, hf * HALF:(hf + 1) * HALF]
                dve.wait_ge(*N.at("hi", 8 * hf + d + 1))
                nc.vector.scalar_tensor_tensor(out=z[:, 1, :], in0=ps[:, 6 + d % 2, :], scalar=c_(N.gain, d),
                                               in1=z[:, 0, :].bitcast(f32), op0=ALU.mult,
                                               op1=ALU.subtract).then_inc(N.sem["lo"], 1)

        def sqrt_ready(act):
            link_act(act, nc.scalar.activation(small[:, 1:2], eps, ACT.Sqrt))

        def norm_act_rows(act, N, hf):
            if hf == 0:
                sqrt_ready(act)
            if N.post is not None:
                norm_act_post(act, N, hf)
            if not N.final:
                norm_act_stats(act, N, hf)

        def norm_act(act, N, hf):
            if N.residual and not N.final:
                if hf == 0:
                    sqrt_ready(act)
                    norm_act_post(act, N, 0)
                norm_act_stats(act, N, hf)
                if hf == 0:
                    norm_act_post(act, N, 1)
                norm_act_split(act, N, hf)
                return
            norm_act_rows(act, N, hf)
            if not N.final:
                norm_act_split(act, N, hf)

        def norm_dve_rows(dve, N, hf):
            if N.post is not None:
                norm_dve_post(dve, N, hf)
            if not N.final:
                norm_dve_scale(dve, N, hf)

        def norm_dve(dve, N, hf):
            norm_dve_rows(dve, N, hf)
            if not N.final:
                norm_dve_split(dve, N, hf)

        def norm_dve_hooks(dve, N):
            if N.residual:
                hooks = {4 + k: (lambda k=k: norm_dve_post(dve, N, 0, [k])) for k in range(4)}
                if not N.final:
                    hooks[7] = lambda: [norm_dve_post(dve, N, 0, [3]), norm_dve_scale(dve, N, 0), norm_dve_split(dve, N, 0)]
                return hooks
            hooks = {3: lambda: norm_dve_rows(dve, N, 0)}
            if not N.final:
                hooks[6] = lambda: norm_dve_split(dve, N, 0)
            return hooks

        def norm_pe_step(pe, N, hf, d):
            if d == 0:
                pe.wait_ge(*N.at("xn", 4 * hf + 4))
            if 8 * hf + d >= 2:
                pe.wait_ge(*N.at("lo", 8 * hf + d - 1))
            for t in range(4):
                last = nc.tensor.transpose(ps[:, 6 + d % 2, t * P:(t + 1) * P],
                                           xn[:, t, d * P:(d + 1) * P], ident[:, :])
            last.then_inc(N.sem["tr"], 1)

        def norm_pe(pe, N, hf, first=0, last=KD):
            for d in range(first, last):
                norm_pe_step(pe, N, hf, d)

        gb_in = [sem(f"gb_in{i}") for i in range(2)]
        old = at("old", OFF_ROLD, [2, D])
        old_in = [sem(f"old_in{i}") for i in range(2)]
        old_rows = [sem(f"old_rows{i}") for i in range(4)]
        mid_out = sem("mid_out")

        n_first = Norm("g_mix", A, lambda t: (x_in[t], 16))
        UNITS1 = [(kind, j) for j in range(4) for kind in ("lru", "gate")] + [("pool", j) for j in (3, 2, 1, 0)]
        TALL1 = len(UNITS1)
        GROUPS1 = [(0, 0), (1, 0), (0, 1), (1, 1)] + [(m, half) for m in range(2, TALL1) for half in range(2)]
        in_done = sem("in_done")
        lru_in, gate_in, pool_in = sem("lru_in"), sem("gate_in"), sem("pool_in")
        xb_ready = sem("xb_ready")
        gates_done, poolmm_done = sem("gates_done"), sem("poolmm_done")
        sig_done, pool_evac = sem("sig_done"), sem("pool_evac")
        th_done, ex_done, q_ready, sq_done = sem("th_done"), sem("ex_done"), sem("q_ready"), sem("sq_done")
        y_ready, d_ready, cpos_ready = sem("y_ready"), sem("d_ready"), sem("cpos_ready")
        cat_hi, cat_lo = sem("cat_hi"), sem("cat_lo")
        mats_in = sem("mats_in")
        sc = at("sc", OFF_B + 32 * KB, [8, S])
        UL, XB, R, I, T, AA, Q = (sc[:, i, :] for i in range(7))
        scx = at("scx", OFF_XN, [4, S])
        UP, W1, W2 = (scx[:, i, :] for i in range(3))
        G = [sc[:, 7, :], scx[:, 3, :]]
        Y = at("ystage", OFF_ACC, [8, S])
        gate_w = at("gate_w", OFF_ROLD, [8, P])
        pool_w = at("pool_w", OFF_ROLD + 4 * KB, [4, P])
        inv_cnt = at("inv_cnt", OFF_ROLD + 6 * KB, [4, 16])

        def tall_group(pe, Z, slot, kd, half, bank, each=None):
            for k in range(kd):
                last = products(ps[:, bank, :],
                                lambda h: slot[:, h, k * P:(k + 1) * P],
                                lambda h: Z[:, k, h, half * HALF:(half + 1) * HALF],
                                k == 0, k == kd - 1)
                if each and k < kd - 1:
                    each(k)
            return last

        def pe_mix1(pe):
            def small_bank(q):
                if q >= 2:
                    pe.wait_ge(*((sig_done, q - 1) if q - 2 < 16 else (pool_evac, q - 17)))
                return 4 + q % 2

            def gates(j):
                pe.wait_ge(xb_ready, j + 1)
                for kind in range(2):
                    for half in range(2):
                        nc.tensor.matmul(ps[:, small_bank(4 * j + 2 * kind + half), :], gate_w[:, 4 * kind + j, :],
                                         XB[:, half * HALF:(half + 1) * HALF], start=True,
                                         stop=True).then_inc(gates_done, 1)

            def poolmm(i):
                pe.wait_ge(d_ready, i + 1)
                for half in range(2):
                    nc.tensor.matmul(ps[:, small_bank(16 + 2 * i + half), :], pool_w[:, 3 - i, :],
                                     W2[:, half * HALF:(half + 1) * HALF], start=True,
                                     stop=True).then_inc(poolmm_done, 1)

            for m in range(TALL1):
                if m:
                    pe.wait_ge(unit_ready, m + 1)
                for g in (2 * m, 2 * m + 1):
                    mm, half = GROUPS1[g]
                    if g < 2:
                        pe.wait_ge(unit_ready, mm + 1)
                        pe.wait_ge(*n_first.at("lo", 8))
                    if g == 2:
                        norm_pe_step(pe, n_first, 1, 7)
                        pe.wait_ge(*n_first.at("lo", 16))
                    if g >= 4:
                        pe.wait_ge(*out_of(*GROUPS1[g - 4]))
                    each = (lambda k: norm_pe_step(pe, n_first, 1, k)) if g == 1 else None
                    tall_group(pe, A, B[:, mm % 4], KD, half, g % 4, each).then_inc(in_done, 1)
                if m == 2:
                    pe.wait_ge(mats_in, 48)
                if m % 2 == 0 and 2 <= m <= 8:
                    gates(m // 2 - 1)
                if m >= 9:
                    poolmm(m - 9)
            poolmm(3)

        def out_of(m, half):
            kind = UNITS1[m][0]
            nth = sum(1 for k, _ in UNITS1[:m] if k == kind)
            return {"lru": lru_in, "gate": gate_in, "pool": pool_in}[kind], 2 * nth + half + 1

        def hi1(act, m):
            make_hi(act, m, B[:, m % 4], (in_done, GROUPS1.index((m - 4, 1)) + 1) if m >= 4 else None, m % 2)

        def lru_act(act, j):
            for kind in range(2):
                for half in range(2):
                    n = 4 * j + 2 * kind + half
                    act.wait_ge(gates_done, n + 1)
                    nc.scalar.activation((R, I)[kind][:, half * HALF:(half + 1) * HALF], ps[:, 4 + n % 2, :],
                                         ACT.Sigmoid, bias=c_(("gate_a_b", "gate_x_b")[kind], j)).then_inc(sig_done, 1)
            if j == 0:
                act.wait_ge(cpos_ready, 3)
            act.wait_ge(sig_done, 4 * j + 4)
            nc.scalar.activation(AA, R, ACT.Exp, scale=c_neg[:, j:j + 1]).then_inc(ex_done, 1)
            nc.scalar.activation(T, R, ACT.Tanh, scale=c_pos[:, j:j + 1]).then_inc(th_done, 1)
            act.wait_ge(q_ready, j + 1)
            nc.scalar.activation(T, Q, ACT.Sqrt).then_inc(sq_done, 1)

        def act_mix1(act):
            norm_act_rows(act, n_first, 0)
            act.wait_ge(params_in, 16)
            for m in range(2):
                hi1(act, m)
            norm_act_split(act, n_first, 0)
            for m in range(2, 4):
                hi1(act, m)
            norm_act(act, n_first, 1)
            act.wait_ge(cpos_ready, 1)
            nc.scalar.activation(lr[1], lr[0], ACT.Exp, scale=-1.0).then_inc(cpos_ready, 1)
            for m, (kind, j) in enumerate(UNITS1):
                if kind == "lru" and j:
                    act.wait_ge(xb_ready, j)
                if kind == "gate" and j >= 2:
                    act.wait_ge(y_ready, j - 1)
                if kind == "pool" and j < 3:
                    act.wait_ge(d_ready, 3 - j)
                dst = {"lru": UL, "gate": G[j % 2], "pool": UP}[kind]
                for half in range(2):
                    g = GROUPS1.index((m, half))
                    act.wait_ge(in_done, g + 1)
                    nc.scalar.activation(dst[:, half * HALF:(half + 1) * HALF], ps[:, g % 4, :],
                                         ACT.Gelu_apprx_tanh if kind == "gate" else ACT.Copy
                                         ).then_inc(out_of(m, half)[0], 1)
                hi1(act, m + 4)
                if m % 2 == 0 and 2 <= m <= 8:
                    lru_act(act, m // 2 - 1)
            for k in CAT_ORDER:
                act.wait_ge(*((y_ready, k - 3) if k >= 4 else (pool_evac, 8 - 2 * k)))
                act.wait_ge(in_done, 2 * TALL1)
                nc.scalar.activation(A[:, k, 0, :], Y[:, k, :], ACT.Copy).then_inc(cat_hi, 1)

        CAT_ORDER = (4, 5, 6, 7, 3, 2, 1, 0)

        def dve_mix1(dve):
            nc.vector.memset(eps, EPS).then_inc(eps_made, 1)
            norm_dve_rows(dve, n_first, 0)
            dve.wait_ge(params_in, 16)
            for m in range(2):
                make_lo(dve, m, B[:, m % 4], m % 2)
            norm_dve_split(dve, n_first, 0)
            for m in range(2, 4):
                make_lo(dve, m, B[:, m % 4], m % 2)
            norm_dve(dve, n_first, 1)
            L = col[:, COLS["lru_L"]:COLS["lru_L"] + 4]
            nc.vector.tensor_scalar(lr[2], L, -1.0, None, ALU.mult).then_inc(dve_chain, 1)
            chained["dve"] += 1
            dve.wait_ge(dve_chain, chained["dve"])
            nc.vector.tensor_tensor(lr[0], L, lr[2], ALU.max).then_inc(cpos_ready, 1)
            dve.wait_ge(cpos_ready, 2)
            e, s_, s2, sm = lr[1], lr[3], lr[4], lr[5]
            link_dve(dve, nc.vector.tensor_scalar(s_, e, 2.0, None, ALU.add))
            link_dve(dve, nc.vector.reciprocal(s_, s_))
            link_dve(dve, nc.vector.tensor_tensor(s_, s_, e, ALU.mult))
            link_dve(dve, nc.vector.tensor_tensor(s2, s_, s_, ALU.mult))
            link_dve(dve, nc.vector.tensor_scalar(sm, s2, 1.0 / 17, 1.0 / 15, ALU.mult, ALU.add))
            for n in (13, 11, 9, 7, 5, 3, 1):
                link_dve(dve, nc.vector.tensor_tensor(sm, sm, s2, ALU.mult))
                link_dve(dve, nc.vector.tensor_scalar(sm, sm, 1.0 / n, None, ALU.add))
            link_dve(dve, nc.vector.tensor_tensor(sm, sm, s_, ALU.mult))
            link_dve(dve, nc.vector.tensor_scalar(lr[2], lr[2], 0.0, LRU_C, ALU.max, ALU.mult))
            link_dve(dve, nc.vector.scalar_tensor_tensor(out=c_pos, in0=sm, scalar=2 * LRU_C, in1=lr[2],
                                                         op0=ALU.mult, op1=ALU.add))
            nc.vector.tensor_scalar(c_neg, c_pos, -1.0, None, ALU.mult).then_inc(cpos_ready, 1)

            def pool_out(i):
                for half in range(2):
                    dve.wait_ge(poolmm_done, 2 * i + half + 1)
                    nc.vector.tensor_scalar(Y[:, 3 - i, half * HALF:(half + 1) * HALF], ps[:, 4 + half, :],
                                            c_("pool_b", 3 - i), c_("pool_scale", 3 - i), ALU.add,
                                            ALU.mult).then_inc(pool_evac, 1)

            def convolve(j):
                dve.wait_ge(lru_in, 2 * j + 2)
                if j:
                    dve.wait_ge(gates_done, 4 * j)
                w = lambda k: c_("conv_w", 4 * k + j)
                link_dve(dve, nc.vector.tensor_scalar(XB, UL, w(3), c_("conv_b", j), ALU.mult, ALU.add))
                for sh in range(1, 4):
                    ins = nc.vector.scalar_tensor_tensor(out=XB[:, sh:], in0=UL[:, :S - sh], scalar=w(3 - sh),
                                                         in1=XB[:, sh:], op0=ALU.mult, op1=ALU.add)
                    if sh < 3:
                        link_dve(dve, ins)
                    else:
                        ins.then_inc(xb_ready, 1)

            def window_means(i):
                j = 3 - i
                dve.wait_ge(pool_in, 2 * i + 2)
                if i:
                    dve.wait_ge(poolmm_done, 2 * i)
                src, width = UP, 1
                bufs = [W1, W2] if j % 2 else [W2, W1]
                for step in range(j + 1):
                    dst = bufs[step % 2]
                    link_dve(dve, nc.vector.tensor_copy(dst[:, 0:width], src[:, 0:width]))
                    link_dve(dve, nc.vector.tensor_tensor(dst[:, width:], src[:, width:], src[:, :S - width], ALU.add))
                    src, width = dst, 2 * width
                link_dve(dve, nc.vector.tensor_tensor(small_f[:, 0:width], src[:, 0:width], inv_cnt[:, j, 0:width], ALU.mult))
                link_dve(dve, nc.vector.scalar_tensor_tensor(out=W2, in0=src, scalar=1.0 / width, in1=UP,
                                                             op0=ALU.mult, op1=ALU.subtract))
                nc.vector.tensor_tensor(W2[:, 0:width], small_f[:, 0:width], UP[:, 0:width],
                                        ALU.subtract).then_inc(d_ready, 1)

            def recur(j):
                dve.wait_ge(sig_done, 4 * j + 4)
                dve.wait_ge(xb_ready, j + 1)
                link_dve(dve, nc.vector.tensor_tensor(I, I, XB, ALU.mult))
                dve.wait_ge(ex_done, j + 1)
                link_dve(dve, nc.vector.tensor_tensor(Q, AA, AA, ALU.mult))
                dve.wait_ge(th_done, j + 1)
                nc.vector.scalar_tensor_tensor(out=Q, in0=Q, scalar=1.0, in1=T, op0=ALU.add,
                                               op1=ALU.mult).then_inc(q_ready, 1)
                dve.wait_ge(sq_done, j + 1)
                link_dve(dve, nc.vector.memset(T[:, 0:1], 1.0))
                link_dve(dve, nc.vector.tensor_tensor(I, I, T, ALU.mult))
                link_dve(dve, nc.vector.tensor_tensor_scan(R, AA, I, 0.0, ALU.mult, ALU.add))
                dve.wait_ge(gate_in, 2 * j + 2)
                nc.vector.tensor_tensor(Y[:, 4 + j, :], R, G[j % 2], ALU.mult).then_inc(y_ready, 1)

            def lo1(m):
                make_lo(dve, m, B[:, m % 4], m % 2)

            for m, (kind, j) in enumerate(UNITS1):
                if m == 0:
                    convolve(0)
                lo1(m + 4)
                if kind == "lru" and j:
                    recur(j - 1)
                    convolve(j)
                if kind == "pool":
                    if m == 8:
                        dve.wait_ge(mats_in, 48)
                    window_means(m - 8)
                    if m == 8:
                        recur(3)
                    else:
                        pool_out(m - 9)
            pool_out(3)
            for i, k in enumerate(CAT_ORDER):
                dve.wait_ge(cat_hi, i + 1)
                nc.vector.tensor_tensor(A[:, k, 1, :], Y[:, k, :], A[:, k, 0, :].bitcast(f32),
                                        ALU.subtract).then_inc(cat_lo, 1)

        small_f = at("small_f", OFF_ID + 1024 + 512, [16])

        class Wide:

            def __init__(self, name, acts, slots, first_unit, before, evac_of):
                self.done, self.acts, self.slots = sem(f"{name}_done"), acts, slots
                self.n0, self.before, self.evac_of = first_unit, before, evac_of

        def wide_pe(pe, W, ready, norm, order=tuple(range(KD)), banks=6):
            def part(half, t, i, first, last):
                k = order[i]
                slot = W.slots[4 * half + k // 2]
                return products(ps[:, (NT * half + t) % banks, :],
                                lambda h: W.acts[:, k, h, t * P:(t + 1) * P],
                                lambda h: slot[:, h, (k % 2) * HALF:(k % 2 + 1) * HALF], first, last)

            for i in range(KD):
                ready(i)
                pe.wait_ge(unit_ready, W.n0 + order[i] // 2 + 1)
                for t in range(banks):
                    ins = part(0, t, i, i == 0, i == KD - 1)
                    if i == KD - 1:
                        ins.then_inc(W.done, 1)
            for g in range(banks, 2 * NT):
                half, t = divmod(g, NT)
                if t == 0:
                    pe.wait_ge(unit_ready, W.n0 + 4 * half + 4)
                pe.wait_ge(W.evac_of, g - banks + 1)
                for i in range(KD):
                    last = part(half, t, i, i == 0, i == KD - 1)
                    if g == NT + 7 and not norm.residual and i < 6:
                        norm_pe_step(pe, norm, 0, 2 + i)
                last.then_inc(W.done, 1)
                if g == NT + 6 and not norm.residual:
                    norm_pe(pe, norm, 0, 0, 2)
            if norm.residual:
                norm_pe(pe, norm, 0)

        def wide_hi(act, W, us):
            for u in us:
                make_hi(act, W.n0 + u, W.slots[u], W.before(u), (W.n0 + u) % 2)

        def wide_lo(dve, W, us):
            for u in us:
                make_lo(dve, W.n0 + u, W.slots[u], (W.n0 + u) % 2)

        U_OUT = TALL1
        res1 = sem("res1")

        w_out = Wide("w_out", A, [B[:, u] for u in range(8)], U_OUT, lambda u: (y_ready, 4), res1)
        n_mlp = Norm("g_mlp", A, lambda t: (res1, NT + t + 1))

        def dve_out1(dve, hooks):
            for g in range(2 * NT):
                half, t = divmod(g, NT)
                dve.wait_ge(w_out.done, g + 1)
                dve.wait_ge(old_rows[g % 4], 16 * (g // 4 + 1))
                nc.vector.tensor_tensor(acc[:, t, half * HALF:(half + 1) * HALF], ps[:, g % 6, :], rold[:, g % 4, :],
                                        ALU.add).then_inc(res1, 1)
                hooks.get(g - NT, lambda: None)()

        class Feed:

            def __init__(self, n, gated, Z, W, first_unit, before, add_first):
                self.n, self.gated, self.Z, self.W, self.n0 = n, gated, Z, W, first_unit
                self.nU = 2 * CHUNK if gated else CHUNK
                self.before, self.add_first = before, add_first
                self.last_n = first_unit + n * (self.nU + 2)
                halves = 2 * CHUNK * n
                self.base, self.sem = {}, {}
                take(self, dict(up=2 * self.nU * n, ge=halves if gated else 0, ue=0 if gated else halves, sq=halves,
                                hi=halves, lo=halves, dn=NT * n, de=NT * n))

            def at(self, s, count):
                return self.sem[s], self.base[s] + count

            def start(self, c):
                return self.n0 + 2 + (0 if isinstance(c, int) and c == 0 else self.nU + (c - 1) * (self.nU + 2))

            def n_up(self, c, j):
                nU = self.nU
                if j < 2 and isinstance(c, int) and c == 0:
                    return self.n0 + j
                if j >= 2:
                    cc, jj = c, j - 2
                else:
                    cc, jj = c - 1, j + nU - 2
                down = 0 if isinstance(cc, int) and cc == 0 else 2
                return self.start(cc) + jj + (down if jj >= nU - 2 else 0)

            def n_down(self, c):
                if isinstance(c, int) and c == self.n - 1:
                    return self.last_n - 2
                return self.start(c + 1) + self.nU - 2

            def down_slot(self, c, f):
                last = isinstance(c, int) and c == self.n - 1
                return self.W[:, f if last else 2 + f]

        def h_slot(F, par, f):
            return F.W[:, 4 + 2 * par + f]

        def at_start(c):
            return isinstance(c, int) and c == 0

        def up_place(F, c, j, half):
            return 2 * half + j if at_start(c) and j < 2 else 2 * j + half

        def up_bank(c, j, half):
            return 2 * j + half if at_start(c) and j < 2 else half

        def feed_up_pe(pe, F, c, par, norm=None):
            for g in range(2 * F.nU):
                by_halves = at_start(c) and g < 4
                j, half = (g % 2, g // 2) if by_halves else (g // 2, g % 2)
                f = j // 2 if F.gated else j
                pe.wait_ge(unit_ready, F.n_up(c, j) + 1)
                if not by_halves:
                    if F.gated:
                        if j % 2:
                            pe.wait_ge(*F.at("ge", 2 * CHUNK * c + 2 * f + half + 1))
                        else:
                            pe.wait_ge(*F.at("sq", 2 * CHUNK * c + 2 * f + half - 1))
                    else:
                        pe.wait_ge(*F.at("ue", 2 * F.nU * c + g - 1))
                if norm and g == 0:
                    pe.wait_ge(*norm.at("lo", 8))
                each = None
                if norm and g == 1 and not norm.residual:
                    each = lambda k: norm_pe_step(pe, norm, 1, k)
                if norm and g == 2:
                    norm_pe(pe, norm, 1, 0 if norm.residual else 7)
                    pe.wait_ge(*norm.at("lo", 16))
                tall_group(pe, F.Z, F.W[:, j % 2], KD, half, up_bank(c, j, half), each).then_inc(F.sem["up"], 1)

        def feed_down_pe(pe, F, c, par, hooks={}):
            pe.wait_ge(unit_ready, F.n_down(c) + 2)
            pe.wait_ge(*F.at("lo", 2 * CHUNK * c + 2 * CHUNK))
            for t in range(NT):
                if not (isinstance(c, int) and c == 0 and t < 2):
                    pe.wait_ge(*F.at("de", NT * c + t - 1))
                for half in range(2):
                    for f in range(CHUNK):
                        H, slot = h_slot(F, par, f), F.down_slot(c, f)
                        last = products(ps[:, 2 + 2 * (t % 2) + half, :],
                                        lambda h: H[:, h, t * P:(t + 1) * P],
                                        lambda h: slot[:, h, half * HALF:(half + 1) * HALF],
                                        f == 0, f == CHUNK - 1)
                        if 2 * half + f < 3:
                            hooks.get((t, 2 * half + f), lambda: None)()
                last.then_inc(F.sem["dn"], 1)
                hooks.get(t, lambda: None)()

        rtmp = at("rtmp", OFF_XN, [2, HALF])
        stmp = at("stmp", OFF_XN + 4 * KB, [2, HALF])

        def feed_evac_act(act, F, c, par, j):
            f = j // 2 if F.gated else j
            H = h_slot(F, par, f)
            for half in range(2):
                k = 2 * CHUNK * c + 2 * f + half
                first = isinstance(c, int) and c == 0 and f == 0
                dst = H[:, 0, half * HALF:(half + 1) * HALF]
                act.wait_ge(*F.at("up", 2 * F.nU * c + up_place(F, c, j, half) + 1))
                if F.gated and j % 2 == 0:
                    if not first:
                        act.wait_ge(*F.at("sq", k - 1))
                    nc.scalar.activation(rtmp[:, half, :], ps[:, up_bank(c, j, half), :], ACT.Silu).then_inc(F.sem["ge"], 1)
                elif F.gated:
                    act.wait_ge(*F.at("sq", k + 1))
                    nc.scalar.activation(dst, stmp[:, half, :], ACT.Copy).then_inc(F.sem["hi"], 1)
                else:
                    if not first:
                        act.wait_ge(*F.at("sq", k - 1))
                    nc.scalar.activation(rtmp[:, half, :], ps[:, up_bank(c, j, half), :], ACT.Relu).then_inc(F.sem["ue"], 1)
                    act.wait_ge(*F.at("ue", k + 1))
                    nc.scalar.activation(dst, rtmp[:, half, :], ACT.Square).then_inc(F.sem["hi"], 1)

        def feed_evac_dve(dve, F, c, par, j):
            f = j // 2 if F.gated else j
            if F.gated and j % 2 == 0:
                return
            H = h_slot(F, par, f)
            for half in range(2):
                k = 2 * CHUNK * c + 2 * f + half
                hi, lo = (H[:, h, half * HALF:(half + 1) * HALF] for h in range(2))
                if F.gated:
                    dve.wait_ge(*F.at("ge", k + 1))
                    dve.wait_ge(*F.at("up", 2 * F.nU * c + up_place(F, c, j, half) + 1))
                    if not (isinstance(c, int) and c == 0 and f == 0):
                        dve.wait_ge(*F.at("lo", k - 1))
                    nc.vector.tensor_tensor(stmp[:, half, :], rtmp[:, half, :], ps[:, up_bank(c, j, half), :],
                                            ALU.mult).then_inc(F.sem["sq"], 1)
                else:
                    dve.wait_ge(*F.at("ue", k + 1))
                    if not (isinstance(c, int) and c == 0 and f == 0):
                        dve.wait_ge(*F.at("lo", k - 1))
                    nc.vector.tensor_tensor(stmp[:, half, :], rtmp[:, half, :], rtmp[:, half, :],
                                            ALU.mult).then_inc(F.sem["sq"], 1)
                dve.wait_ge(*F.at("sq", k + 1))
                dve.wait_ge(*F.at("hi", k + 1))
                nc.vector.tensor_tensor(lo, stmp[:, half, :], hi.bitcast(f32), ALU.subtract).then_inc(F.sem["lo"], 1)

        def conversions(F, c, j):
            todo = []
            first, last = (isinstance(c, int) and c == k for k in (0, F.n - 1))
            n = F.start(c) + j + (2 if j > F.nU - 2 and not first else 0)
            if j == F.nU - 2 and not first:
                for f in range(2):
                    free = None if isinstance(c, int) and c == 1 else F.at("dn", NT * (c - 1))
                    todo.append((n, F.W[:, 2 + f], free))
                    n = n + 1
            if not (last and j >= F.nU - 2):
                todo.append((n, F.W[:, j % 2], F.at("up", 2 * F.nU * c + up_place(F, c, j, 1) + 1)))
            elif last and j == F.nU - 1:
                for f in range(2):
                    todo.append((F.last_n - 2 + f, F.W[:, f], F.at("up", 2 * F.nU * F.n)))
            return todo

        def feed_act(act, F, c, par, c_par):
            for j in range(F.nU):
                feed_evac_act(act, F, c, par, j)
                for i, (n, slot, free) in enumerate(conversions(F, c, j)):
                    make_hi(act, n, slot, free, (parity_of(F, c_par, j) + i) % 2)

        def parity_of(F, c, j):
            if c == F.n - 1 and j == F.nU - 1:
                return F.last_n % 2
            return (F.start(c) + j + (2 if j > F.nU - 2 and c != 0 else 0)) % 2

        def feed_dve_up(dve, F, c, par, c_par):
            for j in range(F.nU):
                feed_evac_dve(dve, F, c, par, j)
                for i, (n, slot, free) in enumerate(conversions(F, c, j)):
                    odd = (parity_of(F, c_par, j) + i) % 2
                    make_lo(dve, n, slot, odd)

        def feed_dve_down(dve, F, c, hooks={}):
            for t in range(NT):
                dve.wait_ge(*F.at("dn", NT * c + t + 1))
                src = ps[:, 2 + 2 * (t % 2):4 + 2 * (t % 2), :].rearrange("p a b -> p (a b)")
                if isinstance(c, int) and c == 0 and not F.add_first:
                    dve.wait_ge(mid_out, F.acc_stored)
                    nc.vector.tensor_copy(acc[:, t, :], src).then_inc(F.sem["de"], 1)
                else:
                    if not (isinstance(c, int) and c == 0):
                        dve.wait_ge(*F.at("de", NT * c + t - NT + 1))
                    nc.vector.tensor_tensor(acc[:, t, :], acc[:, t, :], src, ALU.add).then_inc(F.sem["de"], 1)
                hooks.get(t, lambda: None)()

        def feed_steps(eng, F, up, down, first_hooks, last_hooks):
            n = F.n
            up(0, 0, 0, first_hooks)
            up(1, 1, 1, {})
            down(0, 0, {})
            pairs = (n - 3) // 2
            with eng.Fori(1, pairs + 1) as i:
                up(2 * i, 0, 2, {})
                down(2 * i - 1, 1, {})
                up(2 * i + 1, 1, 3, {})
                down(2 * i, 0, {})
            for c in range(2 * pairs + 2, n):
                up(c, c % 2, c, {})
                down(c - 1, (c - 1) % 2, {})
            down(n - 1, (n - 1) % 2, last_hooks)

        def feed_pe(pe, F, norm, last_hooks):
            feed_steps(pe, F, lambda c, par, cp, hk: feed_up_pe(pe, F, c, par, hk.get("norm")),
                       lambda c, par, hk: feed_down_pe(pe, F, c, par, hk), {"norm": norm}, last_hooks)

        def feed_on_act(act, F):
            feed_steps(act, F, lambda c, par, cp, hk: feed_act(act, F, c, par, cp),
                       lambda c, par, hk: None, {}, {})

        def feed_on_dve(dve, F, last_hooks):
            feed_steps(dve, F, lambda c, par, cp, hk: feed_dve_up(dve, F, c, par, cp),
                       lambda c, par, hk: feed_dve_down(dve, F, c, hk), {}, last_hooks)

        def first_hi(act, F):
            for u in range(2):
                make_hi(act, F.n0 + u, F.W[:, u], F.before, (F.n0 + u) % 2)

        def first_lo(dve, F):
            for u in range(2):
                make_lo(dve, F.n0 + u, F.W[:, u], (F.n0 + u) % 2)

        U_MLP = U_OUT + 8
        mlp = Feed(D_FF1 // P // CHUNK, False, A, B, U_MLP, (w_out.done, NT), True)
        U_PLE = mlp.last_n
        n_ple = Norm("g_ple", A, lambda t: mlp.at("de", NT * (mlp.n - 1) + t + 1))

        praw = at("praw", OFF_ROLD, [NT, 256])
        vtmp = at("vtmp", OFF_ROLD, [4, HALF])
        p_in = sem("p_in")
        pt_tr, pt_hi, pt_lo = sem("pt_tr"), sem("pt_hi"), sem("pt_lo")
        ple_done, ple_v, ple_s, ple_m, ple_res = (sem(f"ple_{s}") for s in ("done", "v", "s", "m", "res"))
        PLE_SLOTS = (2, 3, 0, 1)
        mlp_all = NT * mlp.n

        def ple_units():
            units = [(U_PLE + u, B[:, 4 + u], mlp.at("dn", mlp_all - NT)) for u in range(2)]
            for half in range(2):
                for u in range(4):
                    free = (mlp.at("dn", mlp_all - NT) if u < 2 else mlp.at("dn", mlp_all)) if half == 0 else (ple_done, NT)
                    units.append((U_PLE + 2 + 4 * half + u, B[:, PLE_SLOTS[u]], free))
            return units

        def ple_hi(act, a, b):
            for n, slot, free in ple_units()[a:b]:
                make_hi(act, n, slot, free, n % 2)

        def ple_lo(dve, a, b):
            for n, slot, free in ple_units()[a:b]:
                make_lo(dve, n, slot, n % 2)

        def ple_part(half, t, k):
            slot = B[:, PLE_SLOTS[k // 2]]
            products(ps[:, 2 * ((NT * half + t) % 3), :], lambda h: A[:, k, h, t * P:(t + 1) * P],
                     lambda h: slot[:, h, (k % 2) * HALF:(k % 2 + 1) * HALF], k == 0, k == KD - 1)

        def ple_pe(pe, norm_next):
            pe.wait_ge(p_in, 16)
            for q in range(4):
                kp, half = divmod(q, 2)
                if q >= 2:
                    pe.wait_ge(pt_lo, q - 1)
                for t in range(4):
                    last = nc.tensor.transpose(ps[:, q % 2, t * P:(t + 1) * P],
                                               praw[:, 4 * half + t, kp * P:(kp + 1) * P], ident[:, :])
                last.then_inc(pt_tr, 1)
            for g in range(2 * NT):
                half, t = divmod(g, NT)
                if g == 0:
                    pe.wait_ge(pt_lo, 4)
                    pe.wait_ge(*n_ple.at("lo", 8))
                if g == 1:
                    pe.wait_ge(*mlp.at("de", mlp_all))
                if g == 4:
                    pe.wait_ge(*n_ple.at("lo", 16))
                if g == 0:
                    pe.wait_ge(unit_ready, U_PLE + 2 + 4)
                if g == NT:
                    pe.wait_ge(ple_res, NT)
                    for k in range(KD):
                        pe.wait_ge(unit_ready, U_PLE + 2 + 4 + k // 2 + 1)
                        for tt_ in range(3):
                            ple_part(1, tt_, k)
                if g >= 3:
                    pe.wait_ge(ple_res, g - 2)
                b0 = 2 * (g % 3)
                for k in range(KD):
                    if not NT <= g < NT + 3:
                        ple_part(half, t, k)
                    if g == 1:
                        norm_pe_step(pe, n_ple, 1, k)
                    if g == NT + 7 and k < 6:
                        norm_pe_step(pe, norm_next, 0, 2 + k)
                for kp in range(2):
                    last = products(ps[:, b0 + 1, :], lambda h: B[:, 6 + kp, h, t * P:(t + 1) * P],
                                    lambda h: B[:, 4 + kp, h, half * HALF:(half + 1) * HALF], kp == 0, kp == 1)
                last.then_inc(ple_done, 1)
                if g == NT + 6:
                    norm_pe(pe, norm_next, 0, 0, 2)

        def ple_act_p(act):
            for q in range(4):
                kp, half = divmod(q, 2)
                if q == 0:
                    act.wait_ge(*mlp.at("dn", mlp_all))
                act.wait_ge(pt_tr, q + 1)
                nc.scalar.activation(B[:, 6 + kp, 0, half * HALF:(half + 1) * HALF], ps[:, q % 2, :],
                                     ACT.Copy).then_inc(pt_hi, 1)

        def ple_dve_p(dve):
            for q in range(4):
                kp, half = divmod(q, 2)
                dst = B[:, 6 + kp, :, half * HALF:(half + 1) * HALF]
                dve.wait_ge(pt_hi, q + 1)
                nc.vector.tensor_tensor(dst[:, 1, :], ps[:, q % 2, :], dst[:, 0, :].bitcast(f32),
                                        ALU.subtract).then_inc(pt_lo, 1)

        def ple_act(act, g0, g1):
            for g in range(g0, g1):
                act.wait_ge(ple_v, g + 1)
                nc.scalar.activation(vtmp[:, g % 2, :], vtmp[:, g % 2, :], ACT.Sigmoid).then_inc(ple_s, 1)

        def ple_dve(dve, hooks):
            def bias(g):
                half, t = divmod(g, NT)
                dve.wait_ge(ple_done, g + 1)
                if g >= 2:
                    dve.wait_ge(ple_m, g - 1)
                nc.vector.tensor_tensor(vtmp[:, g % 2, :], ps[:, 2 * (g % 3), :],
                                        gb[:, 0, half * HALF:(half + 1) * HALF], ALU.add).then_inc(ple_v, 1)

            late = (NT - 1, NT + 3, NT + 6)
            dve.wait_ge(gb_in[0], 16)
            dve.wait_ge(pt_tr, 4)
            bias(0)
            for g in range(2 * NT):
                half, t = divmod(g, NT)
                if g + 1 < 2 * NT and g not in late:
                    bias(g + 1)
                dve.wait_ge(ple_s, g + 1)
                if g >= 2:
                    dve.wait_ge(ple_res, g - 1)
                nc.vector.tensor_tensor(vtmp[:, 2 + g % 2, :], vtmp[:, g % 2, :], ps[:, 2 * (g % 3) + 1, :],
                                        ALU.mult).then_inc(ple_m, 1)
                dve.wait_ge(ple_m, g + 1)
                nc.vector.tensor_tensor(acc[:, t, half * HALF:(half + 1) * HALF],
                                        acc[:, t, half * HALF:(half + 1) * HALF], vtmp[:, 2 + g % 2, :],
                                        ALU.add).then_inc(ple_res, 1)
                hooks.get(g - NT, lambda: None)()
                if g == NT - 1:
                    ple_lo(dve, 6, 10)
                if g in late:
                    bias(g + 1)

        U_FFN1 = U_PLE + 10
        n_fin = Norm("g_ffn1", A, lambda t: (ple_res, NT + t + 1), post=1)
        n_fin.gb_count = 1
        ffn1 = Feed(D_FF2 // P // CHUNK, True, A, B, U_FFN1, (ple_done, 2 * NT), False)
        n_mix2 = Norm("g_mix2", A, lambda t: ffn1.at("de", NT * (ffn1.n - 1) + t + 1), post=0, residual=True)
        n_mix2.gb_count, n_mix2.old_count, n_mix2.factor, n_mix2.kept = 2, 0, 0.5, x_mid[1]
        n_mix2.squares = lambda t: B[:, 6 + t % 4 // 2, t % 2, :]
        U_QK = ffn1.last_n
        mid_stored = [16 * NT * (k + 1) for k in range(3)]

        U_V = U_QK + 8
        U_U = U_V + 4
        U_GLU = U_U + 4
        U_MIXO = U_GLU + 2
        U_FFN2 = U_MIXO + 8
        qk_done, qk_out, v_done, v_out, u_done, u_out = (sem(s) for s in (
            "qk_done", "qk_out", "v_done", "v_out", "u_done", "u_out"))
        QK = at("qk", OFF_ACC, [8, S])
        V = at("v", OFF_XN, [NT, HALF])
        U = at("u", OFF_GB, [GT, HALF])
        SLOTS4 = (2, 3, 0, 1)
        f1_all = NT * ffn1.n
        QK_ORDER = [(m, half) for half in range(2) for m in range(4)] + [(m, half) for m in range(4, 8) for half in range(2)]
        V_BANKS = (4, 5, 2, 3)

        def qk_unit(m):
            free = (ffn1.at("dn", f1_all - NT) if m < 2 else ffn1.at("dn", f1_all)) if m < 4 \
                else (qk_done, m + 1)
            return U_QK + m, B[:, SLOTS4[m % 4]], free

        def v_unit(u):
            return U_V + u, B[:, 4 + u], ffn1.at("dn", f1_all)

        def u_unit(u):
            return U_U + u, B[:, SLOTS4[u]], (qk_done, 2 * (4 + u) + 2)

        def hi_of(act, unit):
            n, slot, free = unit
            make_hi(act, n, slot, free, n % 2)

        def lo_of(dve, unit):
            make_lo(dve, unit[0], unit[1], unit[0] % 2)

        def proj_pe(pe):
            for n, (m, half) in enumerate(QK_ORDER):
                pe.wait_ge(unit_ready, U_QK + m + 1)
                if n == 0:
                    pe.wait_ge(*n_mix2.at("lo", 8))
                    pe.wait_ge(*ffn1.at("de", f1_all))
                if n == 4:
                    norm_pe_step(pe, n_mix2, 1, 7)
                    pe.wait_ge(*n_mix2.at("lo", 16))
                if n >= 4:
                    pe.wait_ge(qk_out, n - 3)
                each = (lambda k: norm_pe_step(pe, n_mix2, 1, k)) if n == 3 else None
                tall_group(pe, A, B[:, SLOTS4[m % 4]], KD, half, n % 4, each).then_inc(qk_done, 1)
                if n == 13:
                    pe.wait_ge(g_ready, 1)
                    for q in range(7):
                        last = nc.tensor.transpose(ps[:, 6, q * 32:(q + 1) * 32], QG[:, q, :], ident[0:32, 0:32])
                    last.then_inc(g_tr, 1)
            for t0 in range(0, NT, 2):
                if t0 >= 4:
                    pe.wait_ge(v_out, t0 - 2)
                elif t0 == 2:
                    pe.wait_ge(qk_out, 16)
                for k in range(KD):
                    pe.wait_ge(unit_ready, U_V + k // 2 + 1)
                    slot = B[:, 4 + k // 2]
                    for t in (t0, t0 + 1):
                        last = products(ps[:, V_BANKS[t % 4], :], lambda h: A[:, k, h, t * P:(t + 1) * P],
                                        lambda h: slot[:, h, (k % 2) * HALF:(k % 2 + 1) * HALF], k == 0, k == KD - 1)
                        if k == KD - 1:
                            last.then_inc(v_done, 1)
            pe.wait_ge(unit_ready, U_U + 4)
            for t in range(GT):
                pe.wait_ge(*((u_out, t - 1) if t >= 2 else (v_out, NT - 3 + t)))
                for k in range(KD):
                    slot = B[:, SLOTS4[k // 2]]
                    last = products(ps[:, 4 + t % 2, :],
                                    lambda h: A[:, k, h, :].rearrange("p (c t) -> p t c", t=GT)[:, t, :],
                                    lambda h: slot[:, h, (k % 2) * HALF:(k % 2 + 1) * HALF], k == 0, k == KD - 1)
                last.then_inc(u_done, 1)

        def proj_act(act):
            for n, (m, half) in enumerate(QK_ORDER):
                if n == 0:
                    act.wait_ge(mid_out, mid_stored[1])
                    act.wait_ge(*n_mix2.at("xn", NT))
                act.wait_ge(qk_done, n + 1)
                nc.scalar.activation(QK[:, m, half * HALF:(half + 1) * HALF], ps[:, n % 4, :],
                                     ACT.Copy, scale=HEAD_DIM ** -0.5 if m < 4 else 1.0).then_inc(qk_out, 1)
                if 4 <= n < 8:
                    hi_of(act, qk_unit(n))
                elif n >= 8 and n % 2:
                    hi_of(act, v_unit((n - 9) // 2))
                if n == 4:
                    ssm_params_act(act)
            for u in range(4):
                hi_of(act, u_unit(u))

        def proj_dve(dve):
            lo_of(dve, qk_unit(4))
            ssm_params_dve(dve)
            for m in range(5, 8):
                lo_of(dve, qk_unit(m))
            for u in range(4):
                lo_of(dve, v_unit(u))
                if u == 2:
                    ssm_powers_dve(dve)
            for t in range(NT):
                dve.wait_ge(v_done, t + 1)
                nc.vector.tensor_copy(V[:, t, :], ps[:, V_BANKS[t % 4], :]).then_inc(v_out, 1)
                if t % 2:
                    lo_of(dve, u_unit(t // 2))
            s5_prepare = ssm_prepare_dve(dve, 0)
            for t in range(GT):
                dve.wait_ge(u_done, t + 1)
                nc.vector.tensor_copy(U[:, t, :], ps[:, 4 + t % 2, :]).then_inc(u_out, 1)
                next(s5_prepare, None)
            next(s5_prepare, None)

        params_g = at("params_g", OFF_GB, [2 * P + 1])
        g_tmp = at("g_tmp", OFF_GB + 2 * KB, [14, P])
        qg = at("qg", OFF_GB + 10 * KB, [7, P])
        G32 = slice(0, N_GROUPS)
        QG = qg[G32]
        st = at("st", OFF_ID + 2048, [26, N_GROUPS])
        (AR, SAI, UR, UI, RHO, FR, SFI, A2R, SA2I, A4R, SA4I) = (st[:, i, :] for i in range(11))
        WR = [st[:, 11 + i, :] for i in range(7)]
        NWI = [st[:, 18 + i, :] for i in range(7)]
        sgn = col[:, COLS["sgn"]:COLS["sgn"] + 1]
        nsgn = small[:, 100:101]
        g_in, g_ready, g_tr = sem("g_in"), sem("g_ready"), sem("g_tr")
        g_d, g_a = sem("g_d"), sem("g_a")
        TWO_PI = 2 * math.pi
        C1 = 6.28125
        C2 = 0.0019340515136718750
        C3 = TWO_PI - C1 - C2
        ROUND = 1.5 * 2 ** 23

        are, aim, ldt = params_g[G32, 0:P], params_g[G32, P:2 * P], params_g[G32, 2 * P:2 * P + 1]
        gt = [g_tmp[G32, i, :] for i in range(14)]
        dt_ = g_tmp[G32, 13, 0:1]
        wr, wi, th, kk_, r_, _, s2_, cm1, e1, inv, x0, x1 = gt[:12]

        def ssm_params_act(act):
            act.wait_ge(g_in, 16)
            nc.scalar.activation(dt_, ldt, ACT.Exp).then_inc(g_a, 1)
            act.wait_ge(g_d, 1)
            nc.scalar.activation(th, wr, ACT.Tanh, scale=0.5).then_inc(g_a, 1)
            nc.scalar.activation(QG[:, 4, :], wr, ACT.Exp, scale=float(GT)).then_inc(g_a, 1)
            act.wait_ge(g_d, 2)
            nc.scalar.activation(QG[:, 3, :], r_, ACT.Sin).then_inc(g_a, 1)
            nc.scalar.activation(s2_, r_, ACT.Sin, scale=0.5).then_inc(g_a, 1)

        def ssm_params_dve(dve):
            ts, tt, stt = nc.vector.tensor_scalar, nc.vector.tensor_tensor, nc.vector.scalar_tensor_tensor
            link = lambda ins: link_dve(dve, ins)
            dve.wait_ge(g_a, 1)
            link(ts(wi, aim, dt_, None, ALU.mult))
            ts(wr, are, dt_, None, ALU.mult).then_inc(g_d, 1)
            link(ts(kk_, wi, 1.0 / TWO_PI, ROUND, ALU.mult, ALU.add))
            link(ts(kk_, kk_, -ROUND, None, ALU.add))
            link(stt(out=r_, in0=kk_, scalar=-C1, in1=wi, op0=ALU.mult, op1=ALU.add))
            link(stt(out=r_, in0=kk_, scalar=-C2, in1=r_, op0=ALU.mult, op1=ALU.add))
            link(stt(out=r_, in0=kk_, scalar=-C3, in1=r_, op0=ALU.mult, op1=ALU.add))
            ts(r_, r_, 3.1415925, -3.1415925, ALU.min, ALU.max).then_inc(g_d, 1)
            dve.wait_ge(g_a, 3)
            link(ts(x0, th, -1.0, 1.0, ALU.mult, ALU.add))
            link(nc.vector.reciprocal(x0, x0))
            link(stt(out=e1, in0=th, scalar=2.0, in1=x0, op0=ALU.mult, op1=ALU.mult))
            dve.wait_ge(g_a, 5)
            link(stt(out=cm1, in0=s2_, scalar=-2.0, in1=s2_, op0=ALU.mult, op1=ALU.mult))
            link(ts(QG[:, 2, :], cm1, 1.0, None, ALU.add))
            link(ts(x0, e1, 1.0, None, ALU.add))
            link(tt(QG[:, 0, :], x0, QG[:, 2, :], ALU.mult))
            link(tt(QG[:, 1, :], x0, QG[:, 3, :], ALU.mult))
            link(tt(x1, e1, QG[:, 2, :], ALU.mult))
            link(tt(x1, x1, cm1, ALU.add))
            link(tt(x0, are, are, ALU.mult))
            link(tt(inv, aim, aim, ALU.mult))
            link(tt(inv, inv, x0, ALU.add))
            link(nc.vector.reciprocal(inv, inv))
            link(tt(x0, QG[:, 1, :], aim, ALU.mult))
            link(tt(e1, x1, are, ALU.mult))
            link(tt(e1, e1, x0, ALU.add))
            link(tt(QG[:, 5, :], e1, inv, ALU.mult))
            link(tt(x0, QG[:, 1, :], are, ALU.mult))
            link(tt(e1, x1, aim, ALU.mult))
            link(tt(e1, x0, e1, ALU.subtract))
            tt(QG[:, 6, :], e1, inv, ALU.mult).then_inc(g_ready, 1)

        def ssm_powers_dve(dve):
            ts, tt, stt = nc.vector.tensor_scalar, nc.vector.tensor_tensor, nc.vector.scalar_tensor_tensor
            link = lambda ins: link_dve(dve, ins)
            dve.wait_ge(g_tr, 1)
            link(nc.vector.tensor_copy(st[:, 0:7, :].rearrange("p a b -> p (a b)"), ps[:, 6, 0:7 * N_GROUPS]))
            link(ts(nsgn, sgn, -1.0, None, ALU.mult))
            t0, t1 = pw_tmp[:, 0:N_GROUPS], pw_tmp[:, N_GROUPS:2 * N_GROUPS]
            ar_, ai_ = AR, SAI
            for R2, I2 in ((A2R, SA2I), (A4R, SA4I)):
                square(link, R2, I2, ar_, ai_, t0, t1)
                ar_, ai_ = R2, I2
            for x_ in (SAI, SA2I, SA4I, SFI):
                link(ts(x_, x_, sgn, None, ALU.mult))
            ur, ui = UR, UI
            for _ in range(2):
                square(link, ur, ui, ur, ui, t0, t1)
            square(link, WR[0], NWI[0], ur, ui, t0, t1)
            for m in range(1, 7):
                square(link, WR[m], NWI[m], WR[m - 1], NWI[m - 1], t0, t1)
            link(ts(st[:, 18:25, :], st[:, 18:25, :], -1.0, None, ALU.mult))
            nc.vector.tensor_copy(pw_tmp[:, 0:1], pw_tmp[:, 1:2]).then_inc(pw_ready, 1)

        def square(link, R2, I2, R1, I1, t0, t1):
            link(nc.vector.tensor_tensor(t0, R1, R1, ALU.mult))
            link(nc.vector.tensor_tensor(t1, I1, I1, ALU.mult))
            link(nc.vector.scalar_tensor_tensor(out=I2, in0=R1, scalar=2.0, in1=I1, op0=ALU.mult, op1=ALU.mult))
            link(nc.vector.tensor_tensor(R2, t0, t1, ALU.subtract))

        pw_tmp = at("pw_tmp", OFF_ID + 1024 + 256 + 64 + 128, [2 * N_GROUPS])
        pw_ready = sem("pw_ready")

        NB, GB = N_HEADS, N_GROUPS // N_HEADS
        bufs_ssm = []
        for o in (OFF_B + 40 * KB + 256, OFF_B):
            bufs_ssm.append(dict(
                VV=at("vv", o, [GB, 9 * GROUP]), VS=at("vs", o + 2304, [GB, 9 * GROUP]),
                Z=at("z", o + 4608, [GB, GT * GROUP]), ZS=at("zs", o + 6656, [GB, GT * GROUP]),
                T=at("toep", o + 8704, [GB, P]), CS=at("cs", o + 10752, [GB, P]), SN=at("sn", o + 12800, [GB, P])))
        ssm_in = at("ssm_in", OFF_B + 32 * KB, [4 * N_GROUPS * GROUP + N_GROUPS])
        BA, BB, CA, CB = (ssm_in[:, i * 512:(i + 1) * 512].rearrange("p (g c) -> p g c", g=N_GROUPS) for i in range(4))
        dT = ssm_in[0:GROUP, 2048:2048 + N_GROUPS]
        o = OFF_B + 54 * KB + 768
        tmp_v = at("tmp_v", o, [4, GB * 64])
        tmp_p = at("tmp_p", o + 4 * KB, [4, GB * 64])
        nbb = at("nbb", o + 8 * KB, [GB, GROUP])
        kd = at("kd", o + 8 * KB + 256, [GB, GROUP])
        o = OFF_B + 14 * KB + 512
        ztb = at("ztb", o, [2, 3, 512])
        ob = at("ob", o + 12 * KB, [2, GB, P + 1])
        o = OFF_A + 56 * KB
        kkb = at("kkb", o, [GB, P])
        m1b = at("m1b", o + 2 * KB, [512])
        m2b = at("m2b", o + 4 * KB, [512])
        yb = at("yb", o + 4 * KB, [GB, P])
        ub = at("ub", o + 6 * KB, [GB, GT * GROUP])
        ub_made = sem("ub_made")
        s_in = sem("s_in")
        zb_ready, v_ready, nb_ready = sem("zb_ready"), sem("v_ready"), sem("nb_ready")
        t_zero, kk_done, kk_out, kk_d, t_in = (sem(s) for s in ("t_zero", "kk_done", "kk_out", "kk_d", "t_in"))
        s5_m = sem("s5_m")
        s5_tr, s5_cp, s5_s, s5_o, s5_y, s5_g = (sem(s) for s in ("s5_tr", "s5_cp", "s5_s", "s5_o", "s5_y", "s5_g"))
        pool_chain = sem("pool_chain")
        chained["pool"] = 0

        def link_pool(pool, ins):
            chained["pool"] += 1
            ins.then_inc(pool_chain, 1)
            pool.wait_ge(pool_chain, chained["pool"])

        def cmul(eng, link, dst, dsts, src, srcs, pr, spi, tmp, last=None):
            m = src.shape[2]
            t = [tmp[:, i, 0:GB * m].rearrange("p (g m) -> p g m", g=GB) for i in range(4)]
            pr = pr.unsqueeze(2).to_broadcast([P, GB, m])
            spi = spi.unsqueeze(2).to_broadcast([P, GB, m])
            eng.tensor_tensor(t[0], src, pr, ALU.mult)
            eng.tensor_tensor(t[1], srcs, spi, ALU.mult)
            eng.tensor_tensor(t[2], srcs, pr, ALU.mult)
            link(eng.tensor_tensor(t[3], src, spi, ALU.mult))
            eng.tensor_tensor(dst, t[0], t[1], ALU.add)
            ins = eng.tensor_tensor(dsts, t[2], t[3], ALU.subtract)
            if last is None:
                link(ins)
            else:
                ins.then_inc(last, 1)

        def ssm_prepare_dve(dve, b):
            bf = bufs_ssm[b % 2]
            gs = slice(GB * b, GB * b + GB)
            link = lambda ins: link_dve(dve, ins)
            if b == 0:
                dve.wait_ge(s_in, 16)
            elif b >= 2:
                dve.wait_ge(s5_y, b - 1)
            Z, ZS, CS, SN = (bf[n] for n in ("Z", "ZS", "CS", "SN"))
            cut = lambda X, a, m: X[:, :, a * GROUP:(a + m) * GROUP]

            def doubled(k):
                m = 1 << k
                cmul(nc.vector, link, CS[:, :, m:2 * m], SN[:, :, m:2 * m], CS[:, :, 0:m], SN[:, :, 0:m],
                     WR[k][:, gs], NWI[k][:, gs], tmp_v)

            cmul(nc.vector, link, cut(Z, 7, 1), cut(ZS, 7, 1), BA[:, gs, :], BB[:, gs, :], FR[:, gs], SFI[:, gs], tmp_v)
            if b:
                dve.wait_ge(kk_done, b)
            nc.vector.tensor_scalar(nbb[:, :, :], cut(Z, 7, 1), nsgn, None, ALU.mult).then_inc(nb_ready, 1)
            yield
            cmul(nc.vector, link, cut(Z, 6, 1), cut(ZS, 6, 1), cut(Z, 7, 1), cut(ZS, 7, 1), AR[:, gs], SAI[:, gs], tmp_v)
            yield
            cmul(nc.vector, link, cut(Z, 4, 2), cut(ZS, 4, 2), cut(Z, 6, 2), cut(ZS, 6, 2), A2R[:, gs], SA2I[:, gs], tmp_v)
            yield
            cmul(nc.vector, link, cut(Z, 0, 4), cut(ZS, 0, 4), cut(Z, 4, 4), cut(ZS, 4, 4), A4R[:, gs], SA4I[:, gs],
                 tmp_v, last=zb_ready)
            yield
            nc.vector.memset(CS[:, :, 0:1], 1.0)
            link(nc.vector.memset(SN[:, :, 0:1], 0.0))
            doubled(0)
            doubled(1)
            yield
            doubled(2)
            doubled(3)
            yield
            doubled(4)
            yield
            doubled(5)
            yield
            doubled(6)
            yield

        def ssm_skip_dve(dve, b):
            gs = slice(GB * b, GB * b + GB)
            link_dve(dve, nc.vector.tensor_tensor(
                kd[0:GROUP], ident[0:GROUP, 0:GROUP].unsqueeze(1).to_broadcast([GROUP, GB, GROUP]),
                dT[:, gs].unsqueeze(2).to_broadcast([GROUP, GB, GROUP]), ALU.mult))
            dve.wait_ge(kk_out, b + 1)
            nc.vector.tensor_tensor(kkb[0:GROUP, :, 0:GROUP], kkb[0:GROUP, :, 0:GROUP], kd[0:GROUP],
                                    ALU.add).then_inc(kk_d, 1)

        def ssm_scan_dve(dve, b, part):
            link = lambda ins: link_dve(dve, ins)
            bf = bufs_ssm[b % 2]
            cs, sn_ = bf["CS"][:, :, :], bf["SN"][:, :, :]
            v = lambda X: X[:, :].rearrange("p (a b) -> p a b", a=GB)
            bank = ps[:, 7, :].rearrange("p (a b) -> p a b", a=GB)
            dve.wait_ge(s5_s, 2 * b + part + 1)
            if part == 0:
                nc.vector.tensor_tensor(v(m1b), bank, cs, ALU.mult).then_inc(s5_m, 1)
                return
            if b == 0:
                link(nc.vector.memset(ob[:, :, :, 0:1], 0.0))
            nc.vector.scalar_tensor_tensor(out=v(m2b), in0=bank, scalar=nsgn, in1=sn_, op0=ALU.mult,
                                           op1=ALU.mult).then_inc(s5_m, 1)
            dve.wait_ge(s5_m, 2 * b + 2)
            link(nc.vector.tensor_tensor(m1b[:, :], m1b[:, :], m2b[:, :], ALU.add))
            for i in range(GB):
                g = GB * b + i
                ins = nc.vector.tensor_tensor_scan(yb[:, i, :], RHO[:, g:g + 1].to_broadcast([P, P]),
                                                   m1b[:, i * P:(i + 1) * P], 0.0, ALU.mult, ALU.add)
            link(ins)
            if b:
                dve.wait_ge(s5_y, b)
            nc.vector.scalar_tensor_tensor(out=ob[:, 0, :, 1:], in0=yb[:, :, :], scalar=nsgn, in1=cs,
                                           op0=ALU.mult, op1=ALU.mult)
            nc.vector.scalar_tensor_tensor(out=ob[:, 1, :, 1:], in0=yb[:, :, :], scalar=-1.0, in1=sn_,
                                           op0=ALU.mult, op1=ALU.mult).then_inc(s5_o, 1)

        def ssm_outputs_pool(pool, b):
            bf = bufs_ssm[b % 2]
            gs = slice(GB * b, GB * b + GB)
            link = lambda ins: link_pool(pool, ins)
            if b >= 2:
                pool.wait_ge(s5_y, b - 1)
            VV, VS, T = (bf[n] for n in ("VV", "VS", "T"))
            nc.gpsimd.memset(T[:, :, :], 0.0).then_inc(t_zero, 1)
            cut = lambda X, a, m: X[:, :, a * GROUP:(a + m) * GROUP]
            nc.gpsimd.tensor_copy(cut(VV, 0, 1), CA[:, gs, :])
            link(nc.gpsimd.tensor_copy(cut(VS, 0, 1), CB[:, gs, :]))
            for a, m, src, pr, pi in ((1, 1, 0, AR, SAI), (2, 2, 0, A2R, SA2I), (4, 4, 0, A4R, SA4I), (8, 1, 7, AR, SAI)):
                cmul(nc.gpsimd, link, cut(VV, a, m), cut(VS, a, m), cut(VV, src, m), cut(VS, src, m),
                     pr[:, gs], pi[:, gs], tmp_p, last=v_ready if a == 8 else None)

        def ssm_toeplitz_pool(pool, b):
            T = bufs_ssm[b % 2]["T"]
            pool.wait_ge(kk_d, b + 1)
            pool.wait_ge(t_zero, b + 1)
            for t in range(GT):
                w = (GT - t) * GROUP
                pool.dma_start(T[t * GROUP:(t + 1) * GROUP, :, t * GROUP:P],
                               kkb[0:GROUP, :, 0:w]).then_inc(t_in, 16)

        def ssm_step_pe(pe, n):
            b, s = divmod(n, NT)
            bf, zt = bufs_ssm[b % 2], ztb[:, b % 2]
            bank = [ps[:, 7, i * P:(i + 1) * P] for i in range(GB)]
            if s == 0:
                pe.wait_ge(nb_ready, b + 1)
                pe.wait_ge(v_ready, b + 1)
                if b:
                    pe.wait_ge(s5_g, b)
                for i in range(GB):
                    last = nc.tensor.matmul(bank[i][0:GROUP], nbb[:, i, :], bf["VV"][:, i, 0:P], start=True, stop=True)
                last.then_inc(kk_done, 1)
            elif s <= 3:
                if s == 1:
                    pe.wait_ge(zb_ready, b + 1)
                    pe.wait_ge(kk_out, b + 1)
                else:
                    pe.wait_ge(s5_cp, 3 * b + s - 1)
                if s == 3:
                    pe.wait_ge(ub_made, b + 1)
                src = (bf["Z"], bf["ZS"], ub)[s - 1]
                for i in range(GB):
                    last = nc.tensor.transpose(bank[i], src[:, i, :], ident[:, :])
                last.then_inc(s5_tr, 1)
            elif s <= 5:
                pe.wait_ge(*((s5_cp, 3 * b + 3) if s == 4 else (s5_m, 2 * b + 1)))
                for i in range(GB):
                    last = nc.tensor.matmul(bank[i], zt[:, s - 4, i * P:(i + 1) * P], zt[:, 2, i * P:(i + 1) * P],
                                            start=True, stop=True)
                last.then_inc(s5_s, 1)
            elif s == 7:
                pe.wait_ge(t_in, 16 * GT * (b + 1))
                pe.wait_ge(s5_o, b + 1)
                for i in range(GB):
                    nc.tensor.matmul(bank[i], zt[:, 2, i * P:(i + 1) * P], bf["T"][:, i, :], start=True, stop=False)
                    nc.tensor.matmul(bank[i], ob[:, 0, i, 0:P], bf["VV"][:, i, GROUP:9 * GROUP], start=False, stop=False)
                    last = nc.tensor.matmul(bank[i], ob[:, 1, i, 0:P], bf["VS"][:, i, GROUP:9 * GROUP], start=False,
                                            stop=True)
                last.then_inc(s5_y, 1)

        def group_columns(b):
            return U[:, :, 64 * b:64 * b + 64].rearrange("p t (g c) -> p g t c", g=GB)

        def ssm_inputs_act(act, b):
            if b:
                act.wait_ge(s5_tr, 3 * b)
            nc.scalar.activation(ub[:, :, :].rearrange("p g (t c) -> p g t c", t=GT), group_columns(b),
                                 ACT.Copy).then_inc(ub_made, 1)

        def ssm_step_act(act, n):
            b, s = divmod(n, NT)
            if s == 0:
                act.wait_ge(kk_done, b + 1)
                if b:
                    act.wait_ge(t_in, 16 * GT * b)
                nc.scalar.activation(kkb[0:GROUP, :, :].rearrange("p a b -> p (a b)"), ps[0:GROUP, 7, :],
                                     ACT.Copy).then_inc(kk_out, 1)
            elif s <= 3:
                act.wait_ge(s5_tr, 3 * b + s)
                if b >= 2:
                    act.wait_ge(s5_y, b - 1)
                nc.scalar.activation(ztb[:, b % 2, s - 1, :], ps[:, 7, :], ACT.Copy).then_inc(s5_cp, 1)
            elif s == 4 and b + 1 < NB:
                ssm_inputs_act(act, b + 1)
            elif s == 7:
                act.wait_ge(s5_y, b + 1)
                nc.scalar.activation(group_columns(b), ps[:, 7, :].rearrange("p (g t c) -> p g t c", g=GB, t=GT),
                                     ACT.Gelu_apprx_tanh).then_inc(s5_g, 1)

        def ssm_step_dve(dve, n, prepare):
            b, s = divmod(n, NT)
            if s == 2:
                ssm_skip_dve(dve, b)
            if s == 5:
                ssm_scan_dve(dve, b, 0)
            if s == 6:
                ssm_scan_dve(dve, b, 1)
            for _ in range(S5_PIECES[s]):
                next(prepare, None)

        S5_PIECES = (1, 0, 0, 1, 2, 2, 1, 2)

        yf = at("yf", OFF_XN, [4, S])
        YH = A[:, 4:8]
        glu_w = at("glu_w", OFF_ACC, [2, 2, UNIT], f32r)
        sg = at("sg", OFF_ACC + 16 * KB, [2, HALF])
        pr_ = at("pr", OFF_ACC + 20 * KB, [2, HALF])
        yt_tr, yt_f, yt_hi, yt_lo = (sem(s) for s in ("yt_tr", "yt_f", "yt_hi", "yt_lo"))
        gl_done, gl_s, gl_p, gl_hi, gl_lo = (sem(s) for s in ("gl_done", "gl_s", "gl_p", "gl_hi", "gl_lo"))

        def glu_unit(u):
            return U_GLU + u, glu_w[:, u], (at_s, NA)

        def eighths(X, half):
            return X.rearrange("p (c t) -> p t c", t=GT)[:, 4 * half:4 * half + 4, :]

        def glu_pe(pe):
            pe.wait_ge(s5_g, 8)
            for q in range(8):
                j, half = divmod(q, 2)
                if q >= 2:
                    pe.wait_ge(yt_f, q - 1)
                for t in range(4):
                    tt_ = 4 * half + t
                    last = nc.tensor.transpose(ps[:, 2 + q % 2, t * P:(t + 1) * P],
                                               U[:, tt_, j * P:(j + 1) * P], ident[:, :])
                last.then_inc(yt_tr, 1)
            pe.wait_ge(ot_lo, 8)
            pe.wait_ge(yt_lo, 8)
            pe.wait_ge(unit_ready, U_GLU + 2)
            for g in range(8):
                j, half = divmod(g, 2)
                if g >= 4:
                    pe.wait_ge(gl_s, g - 3)
                slot = glu_w[:, j // 2]
                for k in range(4):
                    c0 = (j % 2) * HALF + k * P
                    last = products(ps[:, (0, 1, 4, 5)[g % 4], :], lambda h: slot[:, h, c0:c0 + P],
                                    lambda h: YH[:, k, h, half * HALF:(half + 1) * HALF], k == 0, k == 3)
                last.then_inc(gl_done, 1)

        def glu_act(act):
            for q in range(8):
                j, half = divmod(q, 2)
                act.wait_ge(yt_tr, q + 1)
                nc.scalar.activation(eighths(yf[:, j, :], half), ps[:, 2 + q % 2, :].rearrange("p (t c) -> p t c", t=4),
                                     ACT.Copy).then_inc(yt_f, 1)
                if half:
                    act.wait_ge(yt_f, q + 1)
                    nc.scalar.activation(YH[:, j, 0, :], yf[:, j, :], ACT.Copy).then_inc(yt_hi, 1)
            for g in range(8):
                j, half = divmod(g, 2)
                act.wait_ge(gl_done, g + 1)
                if g >= 2:
                    act.wait_ge(gl_p, g - 1)
                nc.scalar.activation(sg[:, g % 2, :], ps[:, (0, 1, 4, 5)[g % 4], :], ACT.Sigmoid,
                                     bias=c_("b_glu", j)).then_inc(gl_s, 1)
                act.wait_ge(gl_p, g + 1)
                nc.scalar.activation(B[:, 4 + j, 0, half * HALF:(half + 1) * HALF], pr_[:, g % 2, :],
                                     ACT.Copy).then_inc(gl_hi, 1)

        def glu_dve(dve):
            for j in range(4):
                dve.wait_ge(yt_hi, j + 1)
                nc.vector.tensor_tensor(YH[:, j, 1, :], yf[:, j, :], YH[:, j, 0, :].bitcast(f32),
                                        ALU.subtract).then_inc(yt_lo, 2)
            for g in range(8):
                j, half = divmod(g, 2)
                cut = slice(half * HALF, (half + 1) * HALF)
                dve.wait_ge(gl_s, g + 1)
                if g >= 2:
                    dve.wait_ge(gl_lo, g - 1)
                nc.vector.tensor_tensor(pr_[:, g % 2, :], yf[:, j, cut], sg[:, g % 2, :], ALU.mult).then_inc(gl_p, 1)
                dve.wait_ge(gl_hi, g + 1)
                nc.vector.tensor_tensor(B[:, 4 + j, 1, cut], pr_[:, g % 2, :], B[:, 4 + j, 0, cut].bitcast(f32),
                                        ALU.subtract).then_inc(gl_lo, 1)

        dist = at("dist", OFF_A, [S])
        lmul = at("lmul", OFF_A + 4 * KB, [S])
        ib = at("ib", OFF_A + 48 * KB, [S], i32)
        ibf = at("ibf", OFF_A + 48 * KB, [S])
        xb_i = at("xb_i", OFF_A + 52 * KB, [S], i32)
        xb_f = at("xb_f", OFF_A + 52 * KB, [S])
        bias_h = at("bias_h", OFF_A + 8 * KB, [2, S])
        sco = at("sco", OFF_A + 16 * KB, [2, S])
        prob = at("prob", OFF_A + 24 * KB, [2, S])
        probT = at("probT", OFF_A + 32 * KB, [2, NT, P])
        O = at("att_o", OFF_A + 40 * KB, [NT, HALF])
        stats = at("stats", OFF_B + 31 * KB, [4, N_HEADS * NT])
        mx_, nm_, den_, rd_ = (stats[:, i, :] for i in range(4))
        io_done = sem("io_done")
        at_s, at_m, at_n, at_e, at_tr, at_pt, at_pv, at_r, at_o = (sem(f"at_{s}") for s in (
            "s", "m", "n", "e", "tr", "pt", "pv", "r", "o"))
        ot_tr, ot_hi, ot_lo = sem("ot_tr"), sem("ot_hi"), sem("ot_lo")
        NA = N_HEADS * NT

        def bias_dve(dve, cut):
            ts, tt, stt = nc.vector.tensor_scalar, nc.vector.tensor_tensor, nc.vector.scalar_tensor_tensor
            link = lambda ins: link_dve(dve, ins)
            d, L, xi, x_, y_ = dist[:, cut], lmul[:, cut], xb_i[:, cut], xb_f[:, cut], ibf[:, cut]
            link(nc.vector.tensor_copy(d, ib[:, cut]))
            link(ts(xi, ib[:, cut], 3, None, ALU.bitwise_and))
            link(ts(L, xi, 0.0, None, ALU.is_equal))
            link(stt(out=L, in0=d, scalar=512.0, in1=L, op0=ALU.is_le, op1=ALU.mult))
            link(stt(out=L, in0=d, scalar=128.0, in1=L, op0=ALU.is_le, op1=ALU.add))
            link(ts(xi, ib[:, cut], 15, None, ALU.bitwise_and))
            link(stt(out=L, in0=xi, scalar=0.0, in1=L, op0=ALU.is_equal, op1=ALU.add))
            link(stt(out=L, in0=d, scalar=0.0, in1=L, op0=ALU.is_ge, op1=ALU.mult))
            link(ts(x_, L, 2.0, math.log(2.0), ALU.is_ge, ALU.mult))
            link(ts(y_, L, 3.0, math.log(1.5), ALU.is_ge, ALU.mult))
            link(tt(x_, x_, y_, ALU.add))
            link(ts(y_, L, 1.0, -1e30, ALU.is_lt, ALU.mult))
            link(tt(L, x_, y_, ALU.add))

        def att_pe(pe):
            def scores(n):
                h, i = divmod(n, NT)
                rows_ = slice(64 * (h % 2), 64 * (h % 2) + 64)
                W = (i + 1) * P
                if n >= 2:
                    pe.wait_ge(at_m, n - 1)
                for c0 in range(0, W, HALF):
                    w = min(HALF, W - c0)
                    last = nc.tensor.matmul(ps[:, 2 * (n % 2) + c0 // HALF, 0:w], QK[rows_, h // 2, i * P:(i + 1) * P],
                                            QK[rows_, 4 + h // 2, c0:c0 + w], start=True, stop=True)
                last.then_inc(at_s, 1)

            def transposes(n):
                i = n % NT
                pe.wait_ge(at_e, n + 1)
                if n:
                    pe.wait_ge(at_pt, n)
                for k in range(i + 1):
                    last = nc.tensor.transpose(ps[:, 4 + k // 4, (k % 4) * P:(k % 4 + 1) * P],
                                               prob[:, n % 2, k * P:(k + 1) * P], ident[:, :])
                last.then_inc(at_tr, 1)

            def values(n):
                h, i = divmod(n, NT)
                pe.wait_ge(at_pt, n + 1)
                if n:
                    pe.wait_ge(at_o, n)
                for k in range(i + 1):
                    last = nc.tensor.matmul(ps[:, 6, 0:HEAD_DIM], probT[:, n % 2, k, :],
                                            V[:, k, h * HEAD_DIM:(h + 1) * HEAD_DIM], start=k == 0, stop=k == i)
                last.then_inc(at_pv, 1)

            pe.wait_ge(qk_out, 16)
            pe.wait_ge(u_out, GT)
            scores(0)
            scores(1)
            for n in range(NA):
                if n + 2 < NA:
                    scores(n + 2)
                transposes(n)
                ssm_step_pe(pe, n)
                if n:
                    values(n - 1)
            values(NA - 1)
            pe.wait_ge(at_o, NA)
            for q in range(8):
                j, half = divmod(q, 2)
                if q >= 2:
                    pe.wait_ge(ot_lo, q - 1)
                for t in range(4):
                    last = nc.tensor.transpose(ps[:, q % 2, t * P:(t + 1) * P],
                                               O[:, 4 * half + t, j * P:(j + 1) * P], ident[:, :])
                last.then_inc(ot_tr, 1)

        def att_act(act):
            def rest(n):
                i = n % NT
                act.wait_ge(at_tr, n + 1)
                if n >= 2:
                    act.wait_ge(at_pv, n - 1)
                w = (i + 1) * P
                nc.scalar.activation(probT[:, n % 2, 0:i + 1, :].rearrange("p a b -> p (a b)"),
                                     ps[:, 4:6, :].rearrange("p a b -> p (a b)")[:, 0:w], ACT.Copy).then_inc(at_pt, 1)

            act.wait_ge(u_out, GT)
            ssm_inputs_act(act, 0)
            for n in range(NA):
                w = (n % NT + 1) * P
                act.wait_ge(at_n, n + 1)
                if n >= 2:
                    act.wait_ge(at_tr, n - 1)
                nc.scalar.activation(prob[:, n % 2, 0:w], sco[:, n % 2, 0:w], ACT.Exp, bias=nm_[:, n:n + 1],
                                     accum_out=den_[:, n:n + 1]).then_inc(at_e, 1)
                if n:
                    rest(n - 1)
                    ssm_step_act(act, n - 1)
            rest(NA - 1)
            ssm_step_act(act, NA - 1)
            for u in range(2):
                hi_of(act, glu_unit(u))
            for q in range(8):
                j, half = divmod(q, 2)
                act.wait_ge(ot_tr, q + 1)
                nc.scalar.activation(B[:, j, 0, half * HALF:(half + 1) * HALF], ps[:, q % 2, :],
                                     ACT.Copy).then_inc(ot_hi, 1)

        def att_dve(dve):
            link = lambda ins: link_dve(dve, ins)

            def head_bias(h, cut=slice(0, S)):
                nc.vector.scalar_tensor_tensor(out=bias_h[:, h % 2, cut], in0=dist[:, cut], scalar=-2.0 ** (-(h + 1.0)),
                                               in1=lmul[:, cut], op0=ALU.mult, op1=ALU.add).then_inc(dve_chain, 1)
                chained["dve"] += 1
                return chained["dve"]

            def maximum(n, made):
                h, i = divmod(n, NT)
                w = (i + 1) * P
                if i == 0:
                    dve.wait_ge(dve_chain, made)
                dve.wait_ge(at_s, n + 1)
                if n >= 2:
                    dve.wait_ge(at_e, n - 1)
                b = 2 * (n % 2)
                nc.vector.tensor_tensor_reduce(out=sco[:, n % 2, 0:w],
                                               in0=ps[:, b:b + 2, :].rearrange("p a b -> p (a b)")[:, 0:w],
                                               in1=bias_h[:, h % 2, S - w:S], scale=1.0, scalar=-3e38, op0=ALU.add,
                                               op1=ALU.max, accum_out=mx_[:, n:n + 1]).then_inc(at_m, 1)
                dve.wait_ge(at_m, n + 1)
                nc.vector.tensor_scalar(nm_[:, n:n + 1], mx_[:, n:n + 1], -1.0, None, ALU.mult).then_inc(at_n, 1)

            def finish(n):
                h, i = divmod(n, NT)
                dve.wait_ge(at_e, n + 1)
                nc.vector.reciprocal(rd_[:, n:n + 1], den_[:, n:n + 1]).then_inc(at_r, 1)
                dve.wait_ge(at_r, n + 1)
                dve.wait_ge(at_pv, n + 1)
                nc.vector.tensor_scalar(O[:, i, h * HEAD_DIM:(h + 1) * HEAD_DIM], ps[:, 6, 0:HEAD_DIM],
                                        rd_[:, n:n + 1], None, ALU.mult).then_inc(at_o, 1)

            near, middle, far = slice(S - 256, S), slice(HALF, S - 256), slice(0, HALF)
            dve.wait_ge(io_done, 1)
            bias_dve(dve, near)
            made = [head_bias(0, near)]
            maximum(0, made[0])
            for n in range(NA):
                if n % NT == 0:
                    prepare = ssm_prepare_dve(dve, n // NT + 1) if n // NT + 1 < NB else iter(())
                if n == 1 or n == 3:
                    dve.wait_ge(dve_chain, made[0])
                if n >= 2:
                    finish(n - 2)
                if n + 1 < NA:
                    maximum(n + 1, made[(n + 1) // NT])
                if n == 0:
                    dve.wait_ge(io_done, 2)
                    bias_dve(dve, middle)
                    made[0] = head_bias(0, middle)
                if n == 2:
                    bias_dve(dve, far)
                    made[0] = head_bias(0, far)
                if n == 4:
                    made.append(head_bias(1))
                if n % NT == NT - 1 and n // NT + 2 < N_HEADS:
                    made.append(head_bias(n // NT + 2))
                ssm_step_dve(dve, n, prepare)
            finish(NA - 2)
            finish(NA - 1)
            for u in range(2):
                lo_of(dve, glu_unit(u))
            for q in range(8):
                j, half = divmod(q, 2)
                dst = B[:, j, :, half * HALF:(half + 1) * HALF]
                dve.wait_ge(ot_hi, q + 1)
                nc.vector.tensor_tensor(dst[:, 1, :], ps[:, q % 2, :], dst[:, 0, :].bitcast(f32),
                                        ALU.subtract).then_inc(ot_lo, 1)

        mix_out = sem("mix_out")
        mixo = Wide("mixo", B, [A[:, u] for u in range(8)], U_MIXO,
                    lambda u: (at_pv, NA) if u < 4 else (gl_done, 8), mix_out)
        n_ffn2 = Norm("g_ffn2", B, lambda t: (mix_out, NT + t + 1), post=1, residual=True)
        n_ffn2.gb_count, n_ffn2.old_count, n_ffn2.factor, n_ffn2.kept = 2, 4, 1.0, x_mid[2]
        ffn2 = Feed(D_FF2 // P // CHUNK, True, B, A, U_FFN2, (mixo.done, NT), False)
        ffn2.acc_stored = mid_stored[2]
        n_last = Norm(None, None, lambda t: ffn2.at("de", NT * (ffn2.n - 1) + t + 1), post=0, residual=True, final=True)
        n_last.gb_count, n_last.old_count, n_last.factor, n_last.kept = 3, 8, 0.5, out
        n_ffn2.squares = lambda t: A[:, 2 + t % 4 // 2, t % 2, :]
        n_last.squares = lambda t: B[:, t % 4, 1, :]
        N_UNITS = ffn2.last_n

        def dve_mixo(dve, hooks):
            for g in range(2 * NT):
                half, t = divmod(g, NT)
                dve.wait_ge(mixo.done, g + 1)
                nc.vector.tensor_copy(acc[:, t, half * HALF:(half + 1) * HALF], ps[:, g % 6, :]).then_inc(mix_out, 1)
                hooks.get(g - NT, lambda: None)()

        block = ctx.enter_context(nc.Block())
        ffn1.acc_stored = mid_stored[0]
        assert N_UNITS % 2 == 0

        @block.sync
        def _(sp):
            for t in range(NT):
                if t == 4:
                    for r in range(2):
                        sp.dma_start(raw[:, r, :], stream[r, :, :]).then_inc(raw_full[r], 16)
                sp.dma_start(acc[:, t, :], x[t * P:(t + 1) * P, :]).then_inc(x_in[t], 16)
            with sp.Fori(1, N_UNITS // 2) as i:
                for r in range(2):
                    sp.wait_ge(unit_ready, 2 * i + r - 1)
                    sp.dma_start(raw[:, r, :], stream[bass.ds(2 * i + r, 1), :, :].rearrange("a p n -> (a p) n")
                                 ).then_inc(raw_full[r], 16)

        def keep_rows(pool, N, k):
            for t in range(NT):
                pool.wait_ge(*N.at("res", t + 1))
                pool.dma_start(x_mid[k, t * P:(t + 1) * P, :], acc[:, t, :]).then_inc(mid_out, 16)

        def old_rows_again(pool, N, k):
            pool.wait_ge(mid_out, mid_stored[k])
            for t in range(NT):
                if t >= 2:
                    pool.wait_ge(*N.at("res", t - 1))
                pool.dma_start(old[:, t % 2, :], x_mid[k, t * P:(t + 1) * P, :]).then_inc(old_in[t % 2], 16)
                if t >= 1:
                    pool.wait_ge(*N.at("res", t))
                    pool.dma_start(N.kept[(t - 1) * P:t * P, :], acc[:, t - 1, :]).then_inc(mid_out, 16)
            pool.wait_ge(*N.at("res", NT))
            pool.dma_start(N.kept[(NT - 1) * P:NT * P, :], acc[:, NT - 1, :]).then_inc(mid_out, 16)

        @block.gpsimd
        def _(pool):
            pool.dma_start(col[:, :], cols).then_inc(params_in, 16)
            nc.gpsimd.memset(ident[:, :], 0.0).then_inc(ident_made, 1)
            pool.wait_ge(ident_made, 1)
            nc.gpsimd.affine_select(out=ident[:, :], in_=ident[:, :], compare_op=ALU.not_equal, fill=1.0, base=0,
                                    pattern=[[-1, P]], channel_multiplier=1).then_inc(ident_made, 1)
            pool.wait_ge(x_in[NT - 1], 16)
            pool.dma_start(gate_w[:, :, :], gate_mats).then_inc(mats_in, 16)
            pool.dma_start(pool_w[:, :, :], pool_mats).then_inc(mats_in, 16)
            pool.dma_start(inv_cnt[:, :, :], inv_count).then_inc(mats_in, 16)
            pool.wait_ge(gates_done, 16)
            pool.wait_ge(poolmm_done, 8)
            pool.wait_ge(d_ready, 4)
            for g in range(2 * NT):
                half, t = divmod(g, NT)
                if g >= 4:
                    pool.wait_ge(res1, g - 3)
                pool.dma_start(rold[:, g % 4, :], x[t * P:(t + 1) * P, half * HALF:(half + 1) * HALF]
                               ).then_inc(old_rows[g % 4], 16)
            pool.wait_ge(res1, 2 * NT)
            pool.dma_start(praw[:, :, :], p.rearrange("(t p) d -> p t d", p=P)).then_inc(p_in, 16)
            pool.dma_start(gb[:, 0, :], rows[0, :, :]).then_inc(gb_in[0], 16)
            pool.dma_start(gb[:, 1, :], rows[1, :, :]).then_inc(gb_in[1], 16)
            keep_rows(pool, n_fin, 0)
            pool.wait_ge(ple_res, 2 * NT)
            pool.dma_start(gb[:, 0, :], rows[2, :, :]).then_inc(gb_in[0], 16)
            old_rows_again(pool, n_mix2, 0)
            pool.wait_ge(*n_mix2.at("res", NT))
            pool.dma_start(params_g[0:N_GROUPS, :], ssm_g).then_inc(g_in, 16)
            pool.wait_ge(v_done, NT)
            pool.dma_start(ssm_in[:, :], ssm_bc).then_inc(s_in, 16)
            pool.wait_ge(s_in, 16)
            pool.wait_ge(pw_ready, 1)
            ssm_outputs_pool(pool, 0)
            pool.wait_ge(u_done, GT)
            nc.gpsimd.iota(ib[:, S - 256:], [[-1, 256]], base=256 - P, channel_multiplier=1).then_inc(io_done, 1)
            nc.gpsimd.iota(ib[:, :S - 256], [[-1, S - 256]], base=S - P, channel_multiplier=1).then_inc(io_done, 1)
            for b in range(NB):
                if b + 1 < NB:
                    ssm_outputs_pool(pool, b + 1)
                ssm_toeplitz_pool(pool, b)
            pool.wait_ge(yt_tr, 8)
            pool.dma_start(gb[:, 1, :], rows[3, :, :]).then_inc(gb_in[1], 16)
            pool.dma_start(gb[:, 0, :], rows[4, :, :]).then_inc(gb_in[0], 16)
            old_rows_again(pool, n_ffn2, 1)
            old_rows_again(pool, n_last, 2)
            pool.wait_ge(mid_out, 16 * NT * 4)

        @block.scalar
        def _(act):
            act.wait_ge(eps_made, 1)
            act_mix1(act)
            wide_hi(act, w_out, range(4, 8))
            first_hi(act, mlp)
            norm_act(act, n_mlp, 0)
            norm_act(act, n_mlp, 1)
            feed_on_act(act, mlp)
            ple_hi(act, 0, 2)
            norm_act_rows(act, n_ple, 0)
            ple_hi(act, 2, 4)
            norm_act_split(act, n_ple, 0)
            ple_hi(act, 4, 6)
            ple_act_p(act)
            norm_act(act, n_ple, 1)
            ple_act(act, 0, NT)
            ple_hi(act, 6, 10)
            ple_act(act, NT, NT + 4)
            norm_act_rows(act, n_fin, 0)
            ple_act(act, NT + 4, NT + 7)
            norm_act_split(act, n_fin, 0)
            ple_act(act, NT + 7, 2 * NT)
            first_hi(act, ffn1)
            norm_act(act, n_fin, 1)
            feed_on_act(act, ffn1)
            hi_of(act, qk_unit(0))
            hi_of(act, qk_unit(1))
            norm_act(act, n_mix2, 0)
            hi_of(act, qk_unit(2))
            hi_of(act, qk_unit(3))
            norm_act(act, n_mix2, 1)
            proj_act(act)
            att_act(act)
            glu_act(act)
            wide_hi(act, mixo, range(8))
            first_hi(act, ffn2)
            norm_act(act, n_ffn2, 0)
            norm_act(act, n_ffn2, 1)
            feed_on_act(act, ffn2)
            norm_act(act, n_last, 0)
            norm_act(act, n_last, 1)

        @block.vector
        def _(dve):
            dve_mix1(dve)
            wide_lo(dve, w_out, range(4, 8))
            dve_out1(dve, {**norm_dve_hooks(dve, n_mlp), 0: lambda: first_lo(dve, mlp)})
            norm_dve(dve, n_mlp, 1)
            hooks = norm_dve_hooks(dve, n_ple)
            for u, t in enumerate((0, 1, 4, 5)):
                hooks[t] = lambda u=u: ple_lo(dve, u, u + 1)
            feed_on_dve(dve, mlp, hooks)
            ple_lo(dve, 4, 6)
            ple_dve_p(dve)
            norm_dve(dve, n_ple, 1)
            ple_dve(dve, norm_dve_hooks(dve, n_fin))
            first_lo(dve, ffn1)
            norm_dve(dve, n_fin, 1)
            hooks = norm_dve_hooks(dve, n_mix2)
            hooks[0] = lambda: lo_of(dve, qk_unit(0))
            hooks[1] = lambda: lo_of(dve, qk_unit(1))
            feed_on_dve(dve, ffn1, hooks)
            for m in range(2, 4):
                lo_of(dve, qk_unit(m))
            norm_dve(dve, n_mix2, 1)
            proj_dve(dve)
            att_dve(dve)
            glu_dve(dve)
            wide_lo(dve, mixo, range(8))
            dve_mixo(dve, {**norm_dve_hooks(dve, n_ffn2), 0: lambda: first_lo(dve, ffn2)})
            norm_dve(dve, n_ffn2, 1)
            feed_on_dve(dve, ffn2, norm_dve_hooks(dve, n_last))
            norm_dve(dve, n_last, 1)

        @block.tensor
        def _(pe):
            pe.wait_ge(ident_made, 2)
            norm_pe(pe, n_first, 0)
            pe_mix1(pe)
            wide_pe(pe, w_out, lambda i: pe.wait_ge(cat_lo, i + 1), n_mlp, CAT_ORDER)
            feed_pe(pe, mlp, n_mlp, {6: lambda: norm_pe(pe, n_ple, 0, 0, 2),
                     (7, 0): lambda: norm_pe(pe, n_ple, 0, 2, 4), (7, 1): lambda: norm_pe(pe, n_ple, 0, 4, 5),
                     (7, 2): lambda: norm_pe(pe, n_ple, 0, 5, 7), 7: lambda: norm_pe(pe, n_ple, 0, 7, 8)})
            ple_pe(pe, n_fin)
            feed_pe(pe, ffn1, n_fin, {7: lambda: norm_pe(pe, n_mix2, 0)})
            proj_pe(pe)
            att_pe(pe)
            glu_pe(pe)
            wide_pe(pe, mixo, lambda i: pe.wait_ge(gl_lo, max(2, 2 * i - 6)), n_ffn2)
            feed_pe(pe, ffn2, n_ffn2, {})


def pack(i):
    import numpy as np
    f = lambda n: np.asarray(i[n])

    def tall(w):
        K, N = w.shape
        u = w.reshape(K // P, P, N // P, P).transpose(2, 1, 0, 3)
        return u.reshape(-1, P, UNIT)

    def wide(w):
        u = w.reshape(4, 2, P, w.shape[1] // HALF, HALF).transpose(3, 0, 2, 1, 4)
        return u.reshape(-1, P, UNIT)

    def down(w):
        return w.reshape(-1, P, UNIT)

    def feed(up, dn, nU):
        n = dn.shape[0] // CHUNK
        out = [up[0], up[1]]
        nxt = 2
        for c in range(n):
            for j in range(nU):
                if j == nU - 2 and c:
                    out += [dn[CHUNK * (c - 1)], dn[CHUNK * (c - 1) + 1]]
                if nxt < len(up):
                    out.append(up[nxt])
                    nxt += 1
        out += [dn[-2], dn[-1]]
        return np.stack(out)

    def gated(w):
        u = tall(w)
        n = len(u) // 2
        return np.stack([u[:n], u[n:]], axis=1).reshape(-1, P, UNIT)

    w_mix = f("w_mix_in_2")[0]
    glu = f("w_glu_2")[0].reshape(4, P, 2, 2, P).transpose(2, 1, 3, 0, 4).reshape(2, P, UNIT)
    w_in = tall(f("w_in")[0])
    order = [k for j in range(4) for k in (4 + j, 8 + j)] + [3, 2, 1, 0]
    parts = [w_in[order], wide(f("w_out")[0]),
             feed(tall(f("w_up")[0]), down(f("w_down")[0]), CHUNK),
             down(f("w_ple_proj")[0]), wide(f("w_ple_gate")[0]),
             feed(gated(f("ffn1_w_in_2")[0]), down(f("ffn1_w_out_2")[0]), 2 * CHUNK),
             tall(w_mix[:, :1024]), wide(w_mix[:, 1024:]), glu,
             wide(f("w_mix_out_2")[0]),
             feed(gated(f("ffn2_w_in_2")[0]), down(f("ffn2_w_out_2")[0]), 2 * CHUNK)]
    stream = np.concatenate(parts)
    colsd = {
        "g_mix": f("norm_mix_g")[0].reshape(8, P), "g_mlp": f("norm_mlp_g")[0].reshape(8, P),
        "g_ple": f("norm_ple_g")[0].reshape(8, P), "g_ffn1": f("ffn1_pre_g_2")[0].reshape(8, P),
        "g_mix2": f("mix_pre_g_2")[0].reshape(8, P), "g_ffn2": f("ffn2_pre_g_2")[0].reshape(8, P),
        "pool_b": f("pool_b")[0], "pool_scale": f("pool_scale")[0].reshape(4, P),
        "conv_w": f("conv_w")[0].reshape(16, P), "conv_b": f("conv_b")[0].reshape(4, P),
        "gate_a_b": f("gate_a_b")[0].reshape(4, P), "gate_x_b": f("gate_x_b")[0].reshape(4, P),
        "lru_L": f("lru_L")[0].reshape(4, P), "b_glu": f("b_glu_2")[0].reshape(4, P),
        "sgn": np.repeat(np.array([-1.0, 1.0], np.float32), 64)[None],
    }
    cols = np.ascontiguousarray(np.concatenate([colsd[k] for k in COLS]).T)
    gate_mats = np.zeros((P, 8, P), np.float32)
    for kind, name in enumerate(("gate_a_w", "gate_x_w")):
        w = f(name)[0]
        for j in range(4):
            for q in range(2):
                gate_mats[64 * q:64 * q + 64, 4 * kind + j, 64 * q:64 * q + 64] = w[2 * j + q]
    pool_mats = np.ascontiguousarray(f("pool_w")[0].transpose(1, 0, 2))
    rows = np.stack([np.broadcast_to(f(n).reshape(1, D), (P, D)) for n in
                     ("b_ple_gate", "norm_final_g", "ffn1_post_g_2", "mix_post_g_2", "ffn2_post_g_2")])
    twice = lambda a: np.concatenate([a, a], axis=-1)
    ssm_g = np.concatenate([twice(f("a_re_2")[0]), twice(f("a_im_2")[0]), f("log_dt_2")[0][:, None]], axis=1)
    bre, bim = (f(n)[0].transpose(1, 0, 2).reshape(STATE, -1) for n in ("b_re_2", "b_im_2"))
    cre, cim = (f(n)[0].transpose(2, 0, 1).reshape(STATE, -1) for n in ("c_re_2", "c_im_2"))
    skip = np.zeros((P, N_GROUPS), np.float32)
    skip[:GROUP] = f("d_skip_2")[0].reshape(N_GROUPS, GROUP).T
    ssm_bc = np.concatenate([np.concatenate([bre, bim]), np.concatenate([bim, bre]), np.concatenate([cre, cim]),
                             np.concatenate([cim, cre]), skip], axis=1)
    inv_count = np.zeros((P, 4, 16), np.float32)
    for j, w in enumerate(WINDOWS):
        inv_count[:, j, :w] = 1.0 / np.arange(1, w + 1)
    return dict(x=f("x")[0], p=f("p")[0, 0], stream=stream, cols=cols, rows=rows, gate_mats=gate_mats,
                pool_mats=pool_mats, inv_count=inv_count, ssm_g=ssm_g, ssm_bc=ssm_bc)


def kernel(**inputs):
    import numpy as np
    from concourse import bacc
    from concourse.bass_utils import run_bass_kernel_spmd

    packed = pack(inputs)
    nc = bacc.Bacc("TRN2", target_bir_lowering=False, num_devices=1)
    f32 = mybir.dt.float32
    aps = {n: nc.dram_tensor(n, a.shape, f32, kind="ExternalInput").ap() for n, a in packed.items()}
    x_mid = nc.dram_tensor("x_mid", (3, S, D), f32, kind="Internal").ap()
    out = nc.dram_tensor("out", (S, D), f32, kind="ExternalOutput").ap()
    program(nc, x_mid=x_mid, out=out, **aps)
    r = run_bass_kernel_spmd(nc, [packed], core_ids=[0])
    return np.asarray(r.results[0]["out"]).reshape(1, S, D)
```
